# Optimizing a Trainium2 kernel written in Bass

```python
import jax, jax.numpy as jnp
from jax import lax
import numpy as np
import math

D_MODEL = 1024
BATCH = 1
SEQ = 1024
DEPTH = 1

CONV_CH = D_MODEL // 2
CONV_WIDTH = 31
N_HEADS = 8
HEAD_DIM = 64
ATTN_WIDTH = N_HEADS * HEAD_DIM
D_FF = ((8 * D_MODEL // 3 + 255) // 256) * 256
Q_BLOCK = 128
EPS = 1e-6

COL_SIZES = (2 * CONV_CH,
             ATTN_WIDTH,
             ATTN_WIDTH,
             ATTN_WIDTH,
             N_HEADS,
             D_MODEL,
             D_MODEL)
IN_COLS = sum(COL_SIZES)
COL_SPLITS = tuple(int(s) for s in np.cumsum(COL_SIZES)[:-1])


def rmsnorm(x, g):
    xf = x.astype(jnp.float32)
    inv = lax.rsqrt(jnp.mean(xf * xf, axis=-1, keepdims=True) + EPS)
    return (xf * inv).astype(x.dtype) * g

def layernorm(x, g, b):
    xf = x.astype(jnp.float32)
    mu = jnp.mean(xf, axis=-1, keepdims=True)
    var = jnp.mean(jnp.square(xf - mu), axis=-1, keepdims=True)
    return ((xf - mu) * lax.rsqrt(var + EPS)).astype(x.dtype) * g + b

def causal_depthwise_conv(a, w, b):
    out = lax.conv_general_dilated(
        a, w[:, None, :], window_strides=(1,), padding=[(CONV_WIDTH - 1, 0)],
        dimension_numbers=("NWC", "WIO", "NWC"), feature_group_count=CONV_CH)
    return out + b

def conformer_conv_branch(a_in, w_dw, b_dw, g_ln, b_ln, w_out):
    a = a_in[..., :CONV_CH] * jax.nn.sigmoid(a_in[..., CONV_CH:])
    a = causal_depthwise_conv(a, w_dw, b_dw)
    a = jax.nn.silu(layernorm(a, g_ln, b_ln))
    return a @ w_out

def forgetting_attention(q, k, v, f_logit, b_forget, g_q, g_k):
    B, S, _ = q.shape
    nb = S // Q_BLOCK
    def heads(t, g):
        t = t.reshape(B, S, N_HEADS, HEAD_DIM)
        if g is not None:
            t = rmsnorm(t, g)
        return t.transpose(0, 2, 1, 3)
    qh, kh, vh = heads(q, g_q), heads(k, g_k), heads(v, None)
    log_f = jax.nn.log_sigmoid(f_logit.astype(jnp.float32) + b_forget.astype(jnp.float32))
    c = jnp.cumsum(log_f, axis=1).transpose(0, 2, 1)
    scale = HEAD_DIM ** -0.5
    q_blocks = qh.reshape(B, N_HEADS, nb, Q_BLOCK, HEAD_DIM).transpose(2, 0, 1, 3, 4)
    c_blocks = c.reshape(B, N_HEADS, nb, Q_BLOCK).transpose(2, 0, 1, 3)
    k_pos = jnp.arange(S)

    def one_block(args):
        qi, ci, i = args
        s = jnp.einsum("bhqd,bhkd->bhqk", qi, kh).astype(jnp.float32) * scale
        s = s + ci[..., :, None] - c[:, :, None, :]
        q_pos = i * Q_BLOCK + jnp.arange(Q_BLOCK)
        s = jnp.where(k_pos[None, :] <= q_pos[:, None], s, -jnp.inf)
        p = jax.nn.softmax(s, axis=-1).astype(vh.dtype)
        return jnp.einsum("bhqk,bhkd->bhqd", p, vh)

    out = lax.map(one_block, (q_blocks, c_blocks, jnp.arange(nb)))
    return out.transpose(1, 0, 3, 2, 4).reshape(B, S, ATTN_WIDTH)

def first_inputs(seed: int = 0) -> dict:
    key = jax.random.key(seed)
    ks = jax.random.split(key, 20)
    f32 = jnp.float32
    def nrm(k, shape, fan_in):
        return jax.random.normal(k, shape, f32) * fan_in ** -0.5
    def gain(k, shape):
        return 1.0 + 0.02 * jax.random.normal(k, shape, f32)
    return {
        "x": jax.random.normal(ks[0], (BATCH, SEQ, D_MODEL), f32),
        "g_mix": gain(ks[1], (DEPTH, D_MODEL)),
        "w_in": nrm(ks[2], (DEPTH, D_MODEL, IN_COLS), D_MODEL),
        "b_forget": jax.random.uniform(ks[3], (DEPTH, N_HEADS), f32, 2.0, 5.0),
        "w_dw": nrm(ks[4], (DEPTH, CONV_WIDTH, CONV_CH), CONV_WIDTH),
        "b_dw": 0.02 * jax.random.normal(ks[5], (DEPTH, CONV_CH), f32),
        "g_conv_ln": gain(ks[6], (DEPTH, CONV_CH)),
        "b_conv_ln": 0.02 * jax.random.normal(ks[7], (DEPTH, CONV_CH), f32),
        "w_conv_out": nrm(ks[8], (DEPTH, CONV_CH, D_MODEL), CONV_CH),
        "g_q": gain(ks[9], (DEPTH, HEAD_DIM)),
        "g_k": gain(ks[10], (DEPTH, HEAD_DIM)),
        "w_attn_out": nrm(ks[11], (DEPTH, ATTN_WIDTH, D_MODEL), ATTN_WIDTH),
        "w_out": nrm(ks[12], (DEPTH, D_MODEL, D_MODEL), D_MODEL),
        "g_ffn": gain(ks[13], (DEPTH, D_MODEL)),
        "w_ffn_in": nrm(ks[14], (DEPTH, D_MODEL, 2 * D_FF), D_MODEL),
        "w_ffn_out": nrm(ks[15], (DEPTH, D_FF, D_MODEL), D_FF),
    }

def first_block(x, g_mix, w_in, b_forget, w_dw, b_dw, g_conv_ln, b_conv_ln, w_conv_out,
              g_q, g_k, w_attn_out, w_out, g_ffn, w_ffn_in, w_ffn_out):
    for l in range(DEPTH):
        h = rmsnorm(x, g_mix[l])
        proj = h @ w_in[l]
        a_in, q, k, v, f_logit, gate_a, gate_b = jnp.split(proj, COL_SPLITS, axis=-1)
        y_conv = conformer_conv_branch(a_in, w_dw[l], b_dw[l], g_conv_ln[l],
                                       b_conv_ln[l], w_conv_out[l])
        y_attn = forgetting_attention(q, k, v, f_logit, b_forget[l], g_q[l], g_k[l]) @ w_attn_out[l]
        merged = jax.nn.sigmoid(gate_a) * y_conv + jax.nn.sigmoid(gate_b) * y_attn
        x = x + merged @ w_out[l]
        h2 = rmsnorm(x, g_ffn[l])
        gu = h2 @ w_ffn_in[l]
        x = x + (jax.nn.silu(gu[..., :D_FF]) * gu[..., D_FF:]) @ w_ffn_out[l]
    return x


CTX_LEN = 256
GRID_W = 64
ATTN_HEADS = 4
ATTN_HEAD_DIM = 64
ATTN_V_DIM = 2 * ATTN_HEAD_DIM
ATTN_QK_W = ATTN_HEADS * 2 * ATTN_HEAD_DIM
ATTN_V_W = ATTN_HEADS * ATTN_V_DIM
CONV_W = 512
CONV_K = 3
MIX_W = ATTN_V_W + CONV_W
PROJ_W = 2 * ATTN_QK_W + ATTN_V_W + 3 * CONV_W
ROPE_BASE = 10000.0
ROT_AXIS = ATTN_HEAD_DIM // 2
N_EXPERTS = 16
CAP_FACTOR = 2
D_EXPERT = 1024


def rmsnorm_2(x, g):
    xf = x.astype(jnp.float32)
    y = xf * lax.rsqrt(jnp.mean(xf * xf, axis=-1, keepdims=True) + EPS)
    return (y * g.astype(jnp.float32)).astype(x.dtype)

def modulate(x, shift, scale):
    return x * (1 + scale) + shift

def axial_rope_tables(n_tok):
    rows = n_tok // GRID_W
    row = jnp.repeat(jnp.arange(rows, dtype=jnp.float32), GRID_W)
    col = jnp.tile(jnp.arange(GRID_W, dtype=jnp.float32), rows)
    inv = ROPE_BASE ** (-jnp.arange(0, ROT_AXIS, 2, dtype=jnp.float32) / ROT_AXIS)
    ang_r = row[:, None] * inv[None, :]
    ang_c = col[:, None] * inv[None, :]
    ang = jnp.concatenate([ang_r, ang_r, ang_c, ang_c], axis=-1)
    return jnp.cos(ang), jnp.sin(ang)

def apply_rope(x, cos, sin):
    q = ROT_AXIS // 2
    a, b, c2, d2 = x[..., :q], x[..., q:2 * q], x[..., 2 * q:3 * q], x[..., 3 * q:]
    rot = jnp.concatenate([-b, a, -d2, c2], axis=-1)
    cs = cos[None, :, None, None, :].astype(x.dtype)
    sn = sin[None, :, None, None, :].astype(x.dtype)
    return x * cs + rot * sn

def diff_attend(q, k, v, lam):
    s = jnp.einsum('bqhmd,bkhmd->bhmqk', q, k, preferred_element_type=jnp.float32)
    a = jax.nn.softmax(s * (1.0 / math.sqrt(ATTN_HEAD_DIM)), axis=-1)
    a = a[:, :, 0] - lam * a[:, :, 1]
    return jnp.einsum('bhqk,bkhe->bqhe', a.astype(v.dtype), v)

def latent_diff_attention(q, k_all, v_all, lam):
    b, t, h, _, d = q.shape
    nblk = t // Q_BLOCK
    qb = q.reshape(b, nblk, Q_BLOCK, h, 2, d).transpose(1, 0, 2, 3, 4, 5)
    o = lax.map(lambda qblk: diff_attend(qblk, k_all, v_all, lam), qb)
    return o.transpose(1, 0, 2, 3, 4).reshape(b, t, h, ATTN_V_DIM)

def split_proj(p):
    b, t, _ = p.shape
    i0 = ATTN_QK_W
    i1 = i0 + ATTN_QK_W
    i2 = i1 + ATTN_V_W
    i3 = i2 + CONV_W
    i4 = i3 + CONV_W
    q = p[..., :i0].reshape(b, t, ATTN_HEADS, 2, ATTN_HEAD_DIM)
    k = p[..., i0:i1].reshape(b, t, ATTN_HEADS, 2, ATTN_HEAD_DIM)
    v = p[..., i1:i2].reshape(b, t, ATTN_HEADS, ATTN_V_DIM)
    return q, k, v, p[..., i2:i3], p[..., i3:i4], p[..., i4:]

def short_conv(gb, gc, xc, conv_w):
    u = gc * xc
    y = lax.conv_general_dilated(u, conv_w[:, None, :].astype(u.dtype), window_strides=(1,),
                                 padding=((CONV_K // 2, CONV_K // 2),),
                                 dimension_numbers=('NWC', 'WIO', 'NWC'),
                                 feature_group_count=CONV_W)
    return gb * y

def head_out(o, subln_g, lam_init):
    b, t = o.shape[:2]
    return (rmsnorm_2(o, subln_g) * (1.0 - lam_init)).reshape(b, t, ATTN_V_W)

def hybrid_mixer(xn, xn_c, w_in, conv_w, lq1, lk1, lq2, lk2, subln_g, w_out, layer, need_ctx):
    lam_init = 0.8 - 0.6 * math.exp(-0.3 * layer)
    lam = (jnp.exp(jnp.sum(lq1.astype(jnp.float32) * lk1.astype(jnp.float32)))
           - jnp.exp(jnp.sum(lq2.astype(jnp.float32) * lk2.astype(jnp.float32))) + lam_init)
    t = xn.shape[1]
    cos, sin = axial_rope_tables(t)
    q, k, v, gb, gc, xc = split_proj(jnp.einsum('btd,dn->btn', xn, w_in))
    qc, kc, vc, gbc, gcc, xcc = split_proj(jnp.einsum('btd,dn->btn', xn_c, w_in))
    q = apply_rope(q, cos, sin)
    k = apply_rope(k, cos, sin)
    k_all = jnp.concatenate([kc, k], axis=1)
    v_all = jnp.concatenate([vc, v], axis=1)
    attn = head_out(latent_diff_attention(q, k_all, v_all, lam), subln_g, lam_init)
    conv = short_conv(gb, gc, xc, conv_w)
    out = jnp.einsum('btn,nd->btd', jnp.concatenate([attn, conv], axis=-1), w_out)
    out_c = None
    if need_ctx:
        attn_c = head_out(diff_attend(qc, kc, vc, lam), subln_g, lam_init)
        conv_c = short_conv(gbc, gcc, xcc, conv_w)
        out_c = jnp.einsum('btn,nd->btd', jnp.concatenate([attn_c, conv_c], axis=-1), w_out)
    return out, out_c

def ec_moe(x_tok, w_router, w_gate, w_up, w_down):
    t = x_tok.shape[1]
    cap = CAP_FACTOR * t // N_EXPERTS
    logits = jnp.einsum('btd,de->bte', x_tok, w_router, preferred_element_type=jnp.float32)
    aff = jax.nn.softmax(logits, axis=-1)
    g, idx = lax.top_k(jnp.swapaxes(aff, 1, 2), cap)
    xs = jax.vmap(lambda xt, ix: xt[ix])(x_tok, idx)
    hg = jnp.einsum('becd,edf->becf', xs, w_gate)
    hu = jnp.einsum('becd,edf->becf', xs, w_up)
    y = jnp.einsum('becf,efd->becd', jax.nn.silu(hg) * hu, w_down) * g[..., None].astype(xs.dtype)
    return jax.vmap(lambda ix, val: jnp.zeros((t, D_MODEL), val.dtype)
                    .at[ix.reshape(-1)].add(val.reshape(-1, D_MODEL)))(idx, y)

def second_inputs(seed: int = 0) -> dict:
    key = jax.random.key(seed)
    ks = jax.random.split(key, 24)
    f32 = jnp.float32
    nrm = lambda k, shape, s: jax.random.normal(k, shape, f32) * s
    gain = lambda k: 1.0 + 0.05 * jax.random.normal(k, (DEPTH, D_MODEL), f32)
    return {
        "x": nrm(ks[0], (BATCH, SEQ, D_MODEL), 1.0),
        "c": nrm(ks[1], (BATCH, D_MODEL), 1.0),
        "ctx": nrm(ks[2], (BATCH, CTX_LEN, D_MODEL), 1.0),
        "c_ctx": nrm(ks[3], (D_MODEL,), 1.0),
        "w_ada": nrm(ks[4], (DEPTH, D_MODEL, 6 * D_MODEL), 0.5 * D_MODEL ** -0.5),
        "b_ada": nrm(ks[5], (DEPTH, 6 * D_MODEL), 0.01),
        "norm_pre_mix": gain(ks[6]),
        "norm_post_mix": gain(ks[7]),
        "norm_pre_ffn": gain(ks[8]),
        "norm_post_ffn": gain(ks[9]),
        "w_in": nrm(ks[10], (DEPTH, D_MODEL, PROJ_W), D_MODEL ** -0.5),
        "conv_w": nrm(ks[11], (DEPTH, CONV_K, CONV_W), CONV_K ** -0.5),
        "lambda_q1": nrm(ks[12], (DEPTH, ATTN_HEAD_DIM), 0.1),
        "lambda_k1": nrm(ks[13], (DEPTH, ATTN_HEAD_DIM), 0.1),
        "lambda_q2": nrm(ks[14], (DEPTH, ATTN_HEAD_DIM), 0.1),
        "lambda_k2": nrm(ks[15], (DEPTH, ATTN_HEAD_DIM), 0.1),
        "subln_g": 1.0 + 0.05 * jax.random.normal(ks[16], (DEPTH, ATTN_V_DIM), f32),
        "w_out": nrm(ks[17], (DEPTH, MIX_W, D_MODEL), MIX_W ** -0.5),
        "w_router": nrm(ks[18], (DEPTH, D_MODEL, N_EXPERTS), D_MODEL ** -0.5),
        "w_gate": nrm(ks[19], (DEPTH, N_EXPERTS, D_MODEL, D_EXPERT), D_MODEL ** -0.5),
        "w_up": nrm(ks[20], (DEPTH, N_EXPERTS, D_MODEL, D_EXPERT), D_MODEL ** -0.5),
        "w_down": nrm(ks[21], (DEPTH, N_EXPERTS, D_EXPERT, D_MODEL), D_EXPERT ** -0.5),
    }

def second_block(x, c, ctx, c_ctx, w_ada, b_ada, norm_pre_mix, norm_post_mix, norm_pre_ffn,
              norm_post_ffn, w_in, conv_w, lambda_q1, lambda_k1, lambda_q2, lambda_k2,
              subln_g, w_out, w_router, w_gate, w_up, w_down):
    h = x
    hc = ctx
    for layer in range(DEPTH):
        need_ctx = layer < DEPTH - 1
        mod = jnp.einsum('bd,dn->bn', jax.nn.silu(c), w_ada[layer]) + b_ada[layer]
        mod_c = jnp.einsum('d,dn->n', jax.nn.silu(c_ctx), w_ada[layer]) + b_ada[layer]
        sh1, sc1, g1, sh2, sc2, g2 = [m[:, None, :] for m in jnp.split(mod, 6, axis=-1)]
        csh1, csc1, cg1, csh2, csc2, cg2 = jnp.split(mod_c, 6, axis=-1)
        xn = modulate(rmsnorm_2(h, norm_pre_mix[layer]), sh1, sc1)
        xn_c = modulate(rmsnorm_2(hc, norm_pre_mix[layer]), csh1, csc1)
        mix, mix_c = hybrid_mixer(xn, xn_c, w_in[layer], conv_w[layer], lambda_q1[layer],
                                  lambda_k1[layer], lambda_q2[layer], lambda_k2[layer],
                                  subln_g[layer], w_out[layer], layer, need_ctx)
        h = h + g1 * rmsnorm_2(mix, norm_post_mix[layer])
        if need_ctx:
            hc = hc + cg1 * rmsnorm_2(mix_c, norm_post_mix[layer])
        xn = modulate(rmsnorm_2(h, norm_pre_ffn[layer]), sh2, sc2)
        ff = ec_moe(xn, w_router[layer], w_gate[layer], w_up[layer], w_down[layer])
        h = h + g2 * rmsnorm_2(ff, norm_post_ffn[layer])
        if need_ctx:
            xn_c = modulate(rmsnorm_2(hc, norm_pre_ffn[layer]), csh2, csc2)
            ff_c = ec_moe(xn_c, w_router[layer], w_gate[layer], w_up[layer], w_down[layer])
            hc = hc + cg2 * rmsnorm_2(ff_c, norm_post_ffn[layer])
    return h


def setup_inputs(seed=0):
    out = dict(first_inputs(seed))
    for name, value in second_inputs(seed + 1).items():
        if name != "x":
            out[name + "_2"] = value
    return out


def reference(
    x, g_mix, w_in, b_forget, w_dw, b_dw, g_conv_ln, b_conv_ln, w_conv_out, g_q, g_k,
    w_attn_out, w_out, g_ffn, w_ffn_in, w_ffn_out, c_2, ctx_2, c_ctx_2, w_ada_2, b_ada_2,
    norm_pre_mix_2, norm_post_mix_2, norm_pre_ffn_2, norm_post_ffn_2, w_in_2, conv_w_2,
    lambda_q1_2, lambda_k1_2, lambda_q2_2, lambda_k2_2, subln_g_2, w_out_2, w_router_2,
    w_gate_2, w_up_2, w_down_2,
):
    x = first_block(
        x, g_mix, w_in, b_forget, w_dw, b_dw, g_conv_ln, b_conv_ln, w_conv_out, g_q, g_k,
        w_attn_out, w_out, g_ffn, w_ffn_in, w_ffn_out,
    )
    return second_block(
        x, c_2, ctx_2, c_ctx_2, w_ada_2, b_ada_2, norm_pre_mix_2, norm_post_mix_2,
        norm_pre_ffn_2, norm_post_ffn_2, w_in_2, conv_w_2, lambda_q1_2, lambda_k1_2,
        lambda_q2_2, lambda_k2_2, subln_g_2, w_out_2, w_router_2, w_gate_2, w_up_2, w_down_2,
    )


_drawn_inputs = setup_inputs


def setup_inputs(seed=0):
    import zlib

    import numpy as np

    out = dict(_drawn_inputs(seed))
    spreads = {}
    factors = {'g_conv_ln': 3.253,
     'b_conv_ln': 3.644,
     'g_q': 5.788,
     'g_k': 4.73,
     'norm_post_ffn_2': 4.774,
     'lambda_q1_2': 3.608,
     'lambda_q2_2': 8.0,
     'lambda_k2_2': 8.0,
     'subln_g_2': 5.965}
    for name, (base, spread) in spreads.items():
        noise = np.random.default_rng([zlib.crc32(name.encode()), seed]).standard_normal(out[name].shape)
        drawn = base * np.exp(spread * noise) if base else spread * noise
        out[name] = __import__('jax').numpy.asarray(drawn.astype(out[name].dtype))
    for name, factor in factors.items():
        out[name] = (out[name] * factor).astype(out[name].dtype)
    return out
```

```python
from contextlib import ExitStack

import numpy as np

import concourse.bass as bass
from concourse import mybir

ALU = mybir.AluOpType
ACT = mybir.ActivationFunctionType
F32 = mybir.dt.float32
U32 = mybir.dt.uint32
AX = mybir.AxisListType

P = 128
S = 1024
D = 1024
NT = S // P
EPS = 1e-6
NEG = -1e30
KB = 256
CAP = 128
NE = 16
CTX = 256
FF = 2816
NF = FF // P


class Queue:

    def __init__(self, engine, sem):
        self.engine, self.sem, self.count, self.seen = engine, sem, 0, {}

    def wait(self, *tickets):
        for t in tickets:
            if t is None:
                continue
            if isinstance(t, list):
                self.wait(*t)
                continue
            sem, value = t
            if self.seen.get(sem.name, 0) < value:
                self.seen[sem.name] = value
                self.engine.wait_ge(sem, value)

    def do(self, fn):
        self.count += 1
        fn(self.engine).then_inc(self.sem, 1)
        return self.sem, self.count

    def run(self, fn):
        fn(self.engine)


class Landing:

    def __init__(self, sem):
        self.sem, self.count = sem, 0

    def dma(self, queue, out, in_):
        self.count += 16
        queue.engine.dma_start(out, in_).then_inc(self.sem, 16)
        return self.sem, self.count


def program(nc, a, out):
    ctx = ExitStack()
    with ctx:
        _program(nc, ctx, a, out)


def _program(nc, ctx, a, out):
    sem = lambda n: ctx.enter_context(nc.semaphore(n))
    pe, dve, act, pool, sp = (
        Queue(e, sem(n)) for e, n in ((nc.tensor, "s_pe"), (nc.vector, "s_dve"), (nc.scalar, "s_act"),
                                      (nc.gpsimd, "s_pool"), (nc.sync, "s_sp")))
    big = ctx.enter_context(nc.sbuf_tensor("big", [P, 201 * KB], F32))
    misc = ctx.enter_context(nc.sbuf_tensor("misc", [P, 1728], F32))
    ps = ctx.enter_context(nc.psum_tensor("ps", [P, 8, 512], F32))
    xh_dram = nc.dram_tensor("xhat_scratch", [S, D], F32, kind="Internal").ap()
    ff_dram = nc.dram_tensor("ff_scratch", [S, D], F32, kind="Internal").ap()
    landings = {}

    def land(name):
        if name not in landings:
            landings[name] = Landing(sem("d_" + name))
        return landings[name]

    def reg(kb, *shape):
        n = int(np.prod(shape))
        o = int(kb * KB)
        v = big[:, o:o + n]
        if len(shape) == 2:
            v = v.rearrange("p (a b) -> p a b", a=shape[0])
        return v

    mpos = [0]

    def m(*shape):
        n = int(np.prod(shape))
        v = misc[:, mpos[0]:mpos[0] + n]
        mpos[0] += n
        assert mpos[0] <= 1728, mpos
        if len(shape) == 2:
            v = v.rearrange("p (a b) -> p a b", a=shape[0])
        return v

    NW = 4
    wbase = [153 + 12 * i for i in range(NW)]
    wfree = [None] * NW
    wnext = [0]

    def weights(parts, shape_kb=12):
        i = wnext[0] % NW
        wnext[0] += 1
        L = land(f"w{i}")
        sp.wait(wfree[i])
        views, t = [], None
        for off, (c, n), src in parts:
            v = big[:, wbase[i] * KB + off:wbase[i] * KB + off + c * n].rearrange("p (c n) -> p c n", c=c)
            assert off + c * n <= 12 * KB
            t = L.dma(sp, v, src)
            views.append(v)
        return i, views, t

    bfree = [None] * 8
    bnext = [0]

    def bank():
        b = bnext[0] % 8
        bnext[0] += 1
        pe.wait(bfree[b])
        return b

    def mm(o, l, r, start, stop, last):
        fn = lambda e: e.matmul(o, l, r, start=start, stop=stop, skip_group_check=True)
        return pe.do(fn) if last else pe.run(fn)

    def tr(o, i, ident_, last):
        fn = lambda e: e.transpose(o, i, ident_)
        return pe.do(fn) if last else pe.run(fn)

    turn = [0]

    def scaled_copy(o, i, scale, bias, waits):
        turn[0] += 1
        if turn[0] % 2:
            act.wait(*waits)
            return act.do(lambda e: e.activation(o, i, ACT.Identity, bias=bias if bias is not None else 0.0,
                                                 scale=scale))
        dve.wait(*waits)
        if bias is None:
            return dve.do(lambda e: e.tensor_scalar(o, i, scale, None, ALU.mult))
        return dve.do(lambda e: e.tensor_scalar(o, i, scale, bias, ALU.mult, ALU.add))

    def copy(o, i, waits):
        turn[0] += 1
        q = act if turn[0] % 2 else dve
        q.wait(*waits)
        if q is act:
            return act.do(lambda e: e.copy(o, i))
        return dve.do(lambda e: e.tensor_copy(o, i))

    ident = m(P)
    ones = m(P)
    tri = m(P)
    mask = m(P)
    nhalf = m(64)
    sel = m(P)
    zt = pool.do(lambda e: e.memset(misc[:, 0:1728], 0.0))
    pool.wait(zt)
    t_ident = pool.do(lambda e: e.affine_select(out=ident, in_=ident, compare_op=ALU.not_equal, fill=1.0, base=0,
                                                pattern=[[-1, P]], channel_multiplier=1))
    t_mask = pool.do(lambda e: e.affine_select(out=mask, in_=mask, compare_op=ALU.is_ge, fill=NEG, base=0,
                                               pattern=[[-1, P]], channel_multiplier=1))
    t_ones = pool.do(lambda e: e.memset(ones, 1.0))
    t_nhalf = pool.do(lambda e: e.memset(nhalf, -0.5))
    t_sel = pool.do(lambda e: e.memset(sel[0:1, :], 1.0))
    pool.wait(t_ones)
    t_tri = pool.do(lambda e: e.affine_select(out=tri, in_=ones, compare_op=ALU.is_ge, fill=0.0, base=0,
                                              pattern=[[1, P]], channel_multiplier=-1))
    consts = [t_ident, t_mask, t_ones, t_nhalf, t_sel, t_tri]

    rows_a = reg(64, P)
    rows_b = reg(64.5, P)
    colsA = m(56)
    colsB = m(124)
    bfb = m(8)
    gqk = m(2)
    L = land("rows")
    vec = lambda v: v.rearrange("o (c p) -> (o c) p", p=P)
    ra = 0
    where = {}
    for name in ("g_mix", "g_ffn", "norm_pre_mix_2", "norm_pre_ffn_2", "b_dw", "g_conv_ln", "b_conv_ln"):
        v = vec(a[name])
        where[name] = ra
        L.dma(act, rows_a[ra:ra + v.shape[0], :], v)
        ra += v.shape[0]
    where["conv_w"] = ra
    L.dma(act, rows_a[ra:ra + 12, :], a["conv_w_2"].rearrange("o w (c p) -> (o w c) p", p=P))
    ra += 12
    assert ra == 56
    t_rows = L.dma(act, rows_b[0:124, :], a["w_dw"].rearrange("o w (c p) -> (o w c) p", p=P))
    act.wait(zt, t_sel)
    L = land("small")
    L.dma(act, bfb, a["b_forget"].to_broadcast([P, 8]))
    L.dma(act, gqk[0:64, 0:1], a["g_q"].rearrange("o d -> d o"))
    t_small = L.dma(act, gqk[0:64, 1:2], a["g_k"].rearrange("o d -> d o"))
    dve.wait(zt)
    t_g1 = dve.do(lambda e: e.memset(gqk[64:66, :], 1.0))
    dve.wait(t_small)
    t_gq = dve.do(lambda e: e.tensor_scalar(gqk[0:64, 0:1], gqk[0:64, 0:1], 0.125, None, ALU.mult))
    pe.wait(t_rows, *consts)
    b = bank()
    tr(ps[:, b, 0:56], rows_a[0:56, :], ident[0:56, 0:56], False)
    t = tr(ps[:, b, 64:188], rows_b[0:124, :], ident[0:124, 0:124], True)
    dve.wait(t)
    dve.do(lambda e: e.tensor_copy(colsA, ps[:, b, 0:56]))
    t_cols = dve.do(lambda e: e.tensor_copy(colsB, ps[:, b, 64:188]))
    bfree[b] = t_cols
    col = lambda name, i: colsA[:, where[name] + i:where[name] + i + 1]
    act.wait(t_cols, t_gq, t_g1)

    ss = m(16)
    inv = m(16)

    def rms_inv(n0, n1, size, waits):
        dve.wait(*waits)
        t = dve.do(lambda e: e.tensor_scalar(ss[:, n0:n1], ss[:, n0:n1], 1.0 / size, EPS, ALU.mult, ALU.add))
        pool.wait(t, t_nhalf)
        return pool.do(lambda e: e.tensor_tensor(inv[:, n0:n1], ss[:, n0:n1], nhalf[:, 0:n1 - n0], ALU.pow))

    def norm_T(src, src_t, scratch, junk, dst, gains, biases, dst_free, ntile=NT, gain_t=None):
        t_ss = []
        for i in range(ntile):
            act.wait(src_t[i])
            t_ss.append(act.do(lambda e, i=i: e.activation(junk(i), src(i), ACT.Square, accum_out=ss[:, i:i + 1])))
        done = []
        step = min(4, ntile)
        for i0 in range(0, ntile, step):
            t_inv = rms_inv(i0, i0 + step, 1024.0, t_ss[i0:i0 + step])
            dve.wait(t_inv)
            for i in range(i0, i0 + step):
                t_xh = dve.do(lambda e, i=i: e.tensor_scalar(scratch(i), src(i), inv[:, i:i + 1], None, ALU.mult))
            pe.wait(t_xh)
            for f in range(8):
                b = bank()
                for i in range(i0, i0 + step):
                    t = tr(ps[:, b, (i - i0) * P:(i - i0 + 1) * P], scratch(i)[:, f * P:(f + 1) * P], ident,
                           i == i0 + step - 1)
                bfree[b] = scaled_copy(dst[:, f, i0 * P:(i0 + step) * P], ps[:, b, 0:step * P], gains(f),
                                       biases(f) if biases else None, [t, dst_free, gain_t])
                done.append(bfree[b])
        return done, t_ss

    HT = reg(0, 8, 1024)
    x_in = a["x"].rearrange("o s d -> (o s) d")
    xa = lambda i: reg(97 + 4 * i, D)
    xa_t = [land(f"xa{i % 4}").dma(sp, xa(i), x_in[i * P:(i + 1) * P, :]) if i < 4 else None for i in range(8)]
    for i in range(4, 8):
        xa_t[i] = land(f"xb{i}").dma(sp, xa(i), x_in[i * P:(i + 1) * P, :])
    w_in = a["w_in"][0].rearrange("(c p) n -> p c n", p=P)
    HT_done, _ = norm_T(xa, xa_t, lambda i: reg(32 + 4 * i, D), lambda i: reg(32 + 4 * i, D), HT,
                        lambda f: col("g_mix", f), None, None)

    CA = reg(64, 4, 1024)
    CO = reg(80, 4, 1024)
    t_glu = []
    for mt in range(4):
        s, (wa, wg), tw = weights([(0, (8, P), w_in[:, :, mt * P:(mt + 1) * P]),
                                   (1024, (8, P), w_in[:, :, 512 + mt * P:512 + (mt + 1) * P])])
        pe.wait(tw, HT_done)
        for hf in range(2):
            ba, bg = bank(), bank()
            for k in range(8):
                tg = mm(ps[:, bg, :], wg[:, k, :], HT[:, k, hf * 512:(hf + 1) * 512], k == 0, k == 7, k == 7)
            for k in range(8):
                ta = mm(ps[:, ba, :], wa[:, k, :], HT[:, k, hf * 512:(hf + 1) * 512], k == 0, k == 7, k == 7)
            c = CA[:, mt, hf * 512:(hf + 1) * 512]
            act.wait(tg, t_cols)
            t1 = act.do(lambda e, c=c, bg=bg: e.activation(c, ps[:, bg, :], ACT.Sigmoid))
            bfree[bg] = t1
            dve.wait(t1, ta)
            t2 = dve.do(lambda e, c=c, ba=ba: e.tensor_tensor(c, ps[:, ba, :], c, ALU.mult))
            bfree[ba] = t2
            t_glu.append(t2)
        wfree[s] = ta

    conv = {"n": 0, "t": [None] * 4}

    def conv_steps(n):
        for _ in range(n):
            k = conv["n"]
            if k >= 124:
                return
            conv["n"] += 1
            tap, ct = k // 4, k % 4
            w, sh = 30 - tap, tap
            wc = colsB[:, w * 4 + ct:w * 4 + ct + 1]
            if tap == 0:
                dve.wait(*t_glu, t_cols)
                t = dve.do(lambda e, ct=ct, wc=wc: e.tensor_scalar(CO[:, ct, :], CA[:, ct, :], wc,
                                                                   col("b_dw", ct), ALU.mult, ALU.add))
            else:
                dve.wait(conv["t"][ct])
                t = dve.do(lambda e, ct=ct, wc=wc, sh=sh: e.scalar_tensor_tensor(
                    out=CO[:, ct, sh:], in0=CA[:, ct, 0:S - sh], scalar=wc, in1=CO[:, ct, sh:],
                    op0=ALU.mult, op1=ALU.add))
            conv["t"][ct] = t

    zf, zb, lf, Lp, cc, ncc = m(64), m(64), m(64), m(8, 8), m(8, 8), m(8, 8)
    s, (wf,), tw = weights([(0, (8, 8), w_in[:, :, 2560:2568])])
    pe.wait(tw)
    b = bank()
    for i in range(NT):
        for k in range(8):
            t = mm(ps[:, b, i * 8:i * 8 + 8], HT[:, k, i * P:(i + 1) * P], wf[:, k, :], k == 0, k == 7,
                   i == 7 and k == 7)
    wfree[s] = t
    dve.wait(t, t_small)
    t = dve.do(lambda e: e.tensor_tensor(zf.rearrange("p (a b) -> p a b", a=8),
                                         ps[:, b, 0:64].rearrange("p (a b) -> p a b", a=8),
                                         bfb.rearrange("p (o b) -> p o b", o=1).to_broadcast([P, 8, 8]), ALU.add))
    bfree[b] = t
    dve.wait(t)
    t = dve.do(lambda e: e.tensor_scalar(zb, zf, -1.0, None, ALU.mult))
    dve.wait(t)
    t = dve.do(lambda e: e.tensor_tensor(zb, zb, zf, ALU.max))
    act.wait(t)
    t = act.do(lambda e: e.activation(zb, zb, ACT.Exp, scale=-1.0))
    act.wait(t)
    t = act.do(lambda e: e.activation(zb, zb, ACT.Ln, bias=1.0))
    dve.wait(t)
    t = dve.do(lambda e: e.scalar_tensor_tensor(out=lf, in0=zf, scalar=0.0, in1=zb, op0=ALU.min, op1=ALU.subtract))
    dve.wait(t, zt)
    for i in range(1, 8):
        t = dve.do(lambda e, i=i: e.tensor_tensor(Lp[:, i, :], Lp[:, i - 1, :], lf[:, (i - 1) * 8:i * 8], ALU.add))
        dve.wait(t)
    pe.wait(t)
    b = bank()
    mm(ps[:, b, 0:64], ones, Lp.rearrange("p a b -> p (a b)"), True, False, False)
    t = mm(ps[:, b, 0:64], tri, lf, False, True, True)
    dve.wait(t)
    dve.do(lambda e: e.tensor_copy(cc.rearrange("p a b -> p (a b)"), ps[:, b, 0:64]))
    t_cc = dve.do(lambda e: e.tensor_scalar(ncc.rearrange("p a b -> p (a b)"), ps[:, b, 0:64], -1.0, None, ALU.mult))
    bfree[b] = t_cc

    QT = [reg(32 + 16 * j, 2, 1024) for j in range(2)]
    KT = [reg(40 + 16 * j, 2, 1024) for j in range(2)]
    VV = [reg(97 + 4 * j, 8, P) for j in range(2)]
    OT = reg(105, 4, 1024)
    PB = [reg(121 + 4 * j, 1024) for j in range(2)]
    PT = [reg(129 + 4 * j, 8, P) for j in range(2)]
    QK = [reg(137 + 1.125 * j, 4, 66) for j in range(2)]
    OM = [reg(140 + 0.5 * j, P) for j in range(2)]
    SQ = [reg(141 + 1 * j, 256) for j in range(2)]
    st4 = [m(4), m(4)]
    iv4 = [m(4), m(4)]
    nmax = [m(1), m(1)]
    rsum = [m(1), m(1)]
    rinv = [m(1), m(1)]
    pool.wait(t_cc, *HT_done)
    for j in range(2):
        pool.do(lambda e, j=j: e.memset(QK[j][:, 0:2, 64:65], 1.0))
        t_aug = pool.do(lambda e, j=j: e.memset(QK[j][:, 2:4, 65:66], 1.0))
    qk_free = [None, None]
    sq_rd = [None, None]
    att_done = [None, None]
    OT_done = []
    pb_free, pt_free, om_free = [None, None], [None, None], [None, None]

    def project(g):
        buf = g % 2
        i_ = wnext[0] % NW
        wnext[0] += 1
        Lw = land(f"w{i_}")
        sp.wait(wfree[i_])
        w = big[:, wbase[i_] * KB:wbase[i_] * KB + 8 * 384].rearrange("p (c n) -> p c n", c=8)
        for q in range(3):
            tw = Lw.dma(sp, w[:, :, q * P:(q + 1) * P], w_in[:, :, 1024 + q * 512 + g * P:1024 + q * 512 + (g + 1) * P])
        pe.wait(tw)
        tt = []
        for i in range(NT):
            b = bank()
            for k in range(8):
                t = mm(ps[:, b, 0:384], HT[:, k, i * P:(i + 1) * P], w[:, k, :], k == 0, k == 7, k == 7)
            if i == NT - 1:
                wfree[i_] = t
            j = i % 2
            if i >= 2:
                turn_qk(buf, *tt[i - 2])
            act.wait(t, sq_rd[j], HT_done)
            t1 = act.do(lambda e, b=b, j=j: e.activation(SQ[j], ps[:, b, 0:256], ACT.Square))
            act.wait(att_done[buf])
            tv = act.do(lambda e, b=b, i=i: e.copy(VV[buf][:, i, :], ps[:, b, 256:384]))
            dve.wait(t1)
            t2 = dve.do(lambda e, j=j: e.tensor_reduce(st4[j], SQ[j].rearrange("p (h d) -> p h d", h=4), AX.X, ALU.add))
            sq_rd[j] = t2
            dve.wait(t2)
            t2 = dve.do(lambda e, j=j: e.tensor_scalar(st4[j], st4[j], 1.0 / 64, EPS, ALU.mult, ALU.add))
            pool.wait(t2)
            t3 = pool.do(lambda e, j=j: e.tensor_tensor(iv4[j], st4[j], nhalf[:, 0:4], ALU.pow))
            pool.wait(qk_free[j], t_aug)
            pool.do(lambda e, j=j, i=i: e.tensor_copy(QK[j][:, 0:2, 65:66],
                                                      cc[:, i, 2 * g:2 * g + 2].rearrange("p (h o) -> p h o", o=1)))
            t4 = pool.do(lambda e, j=j, i=i: e.tensor_copy(
                QK[j][:, 2:4, 64:65], ncc[:, i, 2 * g:2 * g + 2].rearrange("p (h o) -> p h o", o=1)))
            dve.wait(t3, qk_free[j], tv)
            t5 = dve.do(lambda e, j=j, b=b: e.tensor_tensor(
                QK[j][:, :, 0:64], ps[:, b, 0:256].rearrange("p (h d) -> p h d", h=4),
                iv4[j].rearrange("p (h o) -> p h o", o=1).to_broadcast([P, 4, 64]), ALU.mult))
            bfree[b] = [t5, tv]
            tt.append((i, j, t4, t5, tv))
            conv_steps(1)
        turn_qk(buf, *tt[6])
        return turn_qk(buf, *tt[7])

    def turn_qk(buf, i, j, t4, t5, tv):
        pe.wait(t4, t5)
        b = bank()
        for q in range(4):
            t = tr(ps[0:66, b, q * P:(q + 1) * P], QK[j][:, q, :], ident, q == 3)
        qk_free[j] = t
        sl = slice(i * P, (i + 1) * P)
        v = ps[0:66, b, :].rearrange("p (q n) -> p q n", q=4)
        act.wait(t, att_done[buf], t_gq, t_g1)
        ta = act.do(lambda e: e.activation(QT[buf][0:66, :, sl], v[:, 0:2, :], ACT.Copy, scale=gqk[0:66, 0:1]))
        ta2 = act.do(lambda e: e.activation(KT[buf][0:66, :, sl], v[:, 2:4, :], ACT.Copy, scale=gqk[0:66, 1:2]))
        bfree[b] = ta2
        return [ta2, tv]

    def attention(g, ready):
        buf = g % 2
        units = [(i, h) for i in range(NT) for h in range(2)]
        st = {}

        def qk(u):
            i, h = units[u]
            kw = (i + 1) * P
            b0 = 0 if u % 2 == 0 else 2
            pe.wait(bfree[b0], bfree[b0 + 1])
            for c0 in range(0, kw, 512):
                n = min(512, kw - c0)
                diag = c0 + n == kw
                o = ps[:, b0 + c0 // 512, 0:n]
                t = mm(o, QT[buf][0:66, h, i * P:(i + 1) * P], KT[buf][0:66, h, c0:c0 + n], True, not diag, False)
                if diag:
                    t = mm(o[:, n - P:n], ident, mask, False, True, True)
            j = u % 2
            sv = ps[:, b0:b0 + 2, :].rearrange("p a b -> p (a b)")[:, 0:kw]
            dve.wait(t)
            t1 = dve.do(lambda e: e.tensor_reduce(nmax[j], sv, AX.X, ALU.max, negate=True))
            act.wait(t1, pb_free[j])
            t2 = act.do(lambda e: e.activation(PB[j][:, 0:kw], sv, ACT.Exp, bias=nmax[j], accum_out=rsum[j]))
            bfree[b0] = bfree[b0 + 1] = t2
            st[u] = t2

        def turn_p(u):
            i, h = units[u]
            j = u % 2
            pe.wait(st[u])
            ts = []
            for c0 in range(0, i + 1, 4):
                n = min(4, i + 1 - c0)
                b = 4 + (c0 // 4)
                pe.wait(bfree[b])
                for c in range(n):
                    t = tr(ps[:, b, c * P:(c + 1) * P], PB[j][:, (c0 + c) * P:(c0 + c + 1) * P], ident, c == n - 1)
                bfree[b] = copy(PT[j][:, c0:c0 + n, :].rearrange("p a b -> p (a b)"), ps[:, b, 0:n * P],
                                [t, pt_free[j]])
                ts.append(bfree[b])
            pb_free[j] = t
            dve.wait(st[u])
            st[("r", u)] = dve.do(lambda e: e.reciprocal(rinv[j], rsum[j]))
            st[u] = (st[u], ts)

        def pv(u):
            i, h = units[u]
            j = u % 2
            te, ts = st[u]
            pe.wait(*ts)
            pe.wait(bfree[6])
            for c in range(i + 1):
                t = mm(ps[:, 6, 0:64], PT[j][:, c, :], VV[buf][:, c, h * 64:(h + 1) * 64], c == 0, c == i, c == i)
            pt_free[j] = t
            dve.wait(t, st[("r", u)], om_free[i % 2])
            bfree[6] = dve.do(lambda e: e.tensor_scalar(OM[i % 2][:, h * 64:(h + 1) * 64], ps[:, 6, 0:64], rinv[j],
                                                        None, ALU.mult))
            if h == 1:
                st[("o", i)] = bfree[6]
            conv_steps(2)

        def turn_o(i):
            pe.wait(st[("o", i)], bfree[7])
            t = tr(ps[:, 7, 0:P], OM[i % 2], ident, True)
            om_free[i % 2] = t
            act.wait(t)
            bfree[7] = act.do(lambda e: e.copy(OT[:, g, i * P:(i + 1) * P], ps[:, 7, 0:P]))
            OT_done.append(bfree[7])

        pe.wait(*ready)
        n = len(units)
        for u in range(n + 2):
            if u < n:
                qk(u)
            if u >= 2:
                pv(u - 2)
            if 1 <= u <= n:
                turn_p(u - 1)
            if u >= 4 and u % 2 == 0:
                turn_o((u - 4) // 2)
        turn_o(NT - 1)
        att_done[buf] = [(pe.sem, pe.count)]

    ready = project(0)
    for g in range(4):
        nxt = project(g + 1) if g < 3 else None
        attention(g, ready)
        ready = nxt
    conv_steps(200)

    t_conv = conv["t"]
    mean = []
    for hf in range(2):
        b = bank()
        pe.wait(*t_conv)
        for ct in range(4):
            t = mm(ps[:, b, :], ones, CO[:, ct, hf * 512:(hf + 1) * 512], ct == 0, ct == 3, ct == 3)
        dve.wait(t)
        for ct in range(4):
            v = CO[:, ct, hf * 512:(hf + 1) * 512]
            tc = dve.do(lambda e, v=v, b=b: e.scalar_tensor_tensor(out=v, in0=ps[:, b, :], scalar=-1.0 / 512, in1=v,
                                                                   op0=ALU.mult, op1=ALU.add))
            q = CA[:, ct, hf * 512:(hf + 1) * 512]
            act.wait(tc)
            tq = act.do(lambda e, v=v, q=q: e.activation(q, v, ACT.Square))
        bfree[b] = tc
        mean.append(tq)
    rs = reg(121, 1024)
    t_cn = []
    for hf in range(2):
        b = bank()
        pe.wait(mean[hf])
        for ct in range(4):
            t = mm(ps[:, b, :], ones, CA[:, ct, hf * 512:(hf + 1) * 512], ct == 0, ct == 3, ct == 3)
        r = rs[:, hf * 512:(hf + 1) * 512]
        dve.wait(t, pb_free[0], pb_free[1], pt_free[0], pt_free[1])
        t1 = dve.do(lambda e, r=r, b=b: e.tensor_scalar(r, ps[:, b, :], 1.0 / 512, EPS, ALU.mult, ALU.add))
        bfree[b] = t1
        act.wait(t1)
        t1 = act.do(lambda e, r=r: e.activation(r, r, ACT.Sqrt))
        dve.wait(t1)
        t1 = dve.do(lambda e, r=r: e.reciprocal(r, r))
        dve.wait(t1)
        for ct in range(4):
            v = CO[:, ct, hf * 512:(hf + 1) * 512]
            tm = dve.do(lambda e, v=v, r=r: e.tensor_tensor(v, v, r, ALU.mult))
            t_cn.append((ct, hf, v, tm))
    CN_done = []
    for ct, hf, v, tm in t_cn:
        act.wait(tm)
        CN_done.append(act.do(lambda e, ct=ct, v=v: e.activation(v, v, ACT.Silu, bias=col("b_conv_ln", ct),
                                                                 scale=col("g_conv_ln", ct))))

    MT = reg(32, 8, 1024)
    wco = a["w_conv_out"][0].rearrange("(c p) n -> p c n", p=P)
    wao = a["w_attn_out"][0].rearrange("(c p) n -> p c n", p=P)
    sg = [reg(121 + 2 * j, 512) for j in range(8)]
    sg_free = [None] * 8
    n = 0
    MT_done = []
    att_all = (pe.sem, pe.count)
    for mt in range(8):
        cs = slice(mt * P, (mt + 1) * P)
        s, (wga, wgb, wc, wo_), tw = weights([
            (0, (8, P), w_in[:, :, 2568 + mt * P:2568 + (mt + 1) * P]),
            (1024, (8, P), w_in[:, :, 3592 + mt * P:3592 + (mt + 1) * P]),
            (2048, (4, P), wco[:, :, cs]), (2560, (4, P), wao[:, :, cs])])
        pe.wait(tw)
        for hf in range(2):
            h_ = slice(hf * 512, (hf + 1) * 512)
            b0, b1, b2, b3 = bank(), bank(), bank(), bank()
            for k in range(8):
                t0 = mm(ps[:, b0, :], wga[:, k, :], HT[:, k, h_], k == 0, k == 7, k == 7)
            for k in range(8):
                t1 = mm(ps[:, b1, :], wgb[:, k, :], HT[:, k, h_], k == 0, k == 7, k == 7)
            pe.wait(*CN_done)
            for k in range(4):
                t2 = mm(ps[:, b2, :], wc[:, k, :], CO[:, k, h_], k == 0, k == 3, k == 3)
            pe.wait(*OT_done)
            for k in range(4):
                t3 = mm(ps[:, b3, :], wo_[:, k, :], OT[:, k, h_], k == 0, k == 3, k == 3)
            ja, jb = n % 8, (n + 1) % 8
            n += 2
            act.wait(t0, sg_free[ja], sg_free[jb], *CN_done)
            ta = act.do(lambda e, ja=ja, b0=b0: e.activation(sg[ja], ps[:, b0, :], ACT.Sigmoid))
            bfree[b0] = ta
            act.wait(t1)
            tb = act.do(lambda e, jb=jb, b1=b1: e.activation(sg[jb], ps[:, b1, :], ACT.Sigmoid))
            bfree[b1] = tb
            dve.wait(ta, t2)
            t4 = dve.do(lambda e, ja=ja, b2=b2: e.tensor_tensor(sg[ja], ps[:, b2, :], sg[ja], ALU.mult))
            bfree[b2] = t4
            dve.wait(tb, t3)
            t5 = dve.do(lambda e, jb=jb, b3=b3: e.tensor_tensor(sg[jb], ps[:, b3, :], sg[jb], ALU.mult))
            bfree[b3] = t5
            dve.wait(t4, t5, att_all)
            t6 = dve.do(lambda e, ja=ja, jb=jb, mt=mt, h_=h_: e.tensor_tensor(MT[:, mt, h_], sg[ja], sg[jb], ALU.add))
            sg_free[ja] = sg_free[jb] = t6
            MT_done.append(t6)
        wfree[s] = t3

    X = reg(0, 8, 1024)
    wout = a["w_out"][0].rearrange("(c p) n -> p c n", p=P)
    ws = [weights([(0, (8, 256), wout[:, :, q * 256:(q + 1) * 256])]) for q in range(4)]
    xt = [reg(97 + 4 * j, D) for j in range(4)]
    xt_free = [t3] * 4
    gates_done = t3
    X_t = []
    xt_load = []
    for i in range(NT):
        j = i % 4
        pool.wait(xt_free[j])
        if i < 4:
            pool.wait(gates_done)
        tx = land(f"xt{j}").dma(pool, xt[j], x_in[i * P:(i + 1) * P, :])
        te = []
        for q in range(4):
            s, (w,), tw = ws[q]
            pe.wait(tw, *MT_done)
            b = bank()
            for k in range(8):
                t = mm(ps[:, b, 0:256], MT[:, k, i * P:(i + 1) * P], w[:, k, :], k == 0, k == 7, k == 7)
            dve.wait(t, tx, gates_done)
            te.append(dve.do(lambda e, i=i, q=q, b=b, j=j: e.tensor_tensor(
                X[:, i, q * 256:(q + 1) * 256], ps[:, b, 0:256], xt[j][:, q * 256:(q + 1) * 256], ALU.add)))
            bfree[b] = te[-1]
            if i == NT - 1:
                wfree[s] = t
        xt_free[j] = te[-1]
        X_t.append(te[-1])
    wout_last = t

    H2 = reg(64, 8, 1024)
    scr = lambda i: reg(113 + 4 * i, D)
    H2_done, _ = norm_T(lambda i: X[:, i, :], X_t, scr, scr, H2, lambda f: col("g_ffn", f), None, None)

    wfi = a["w_ffn_in"][0].rearrange("(c p) n -> p c n", p=P)
    actT = lambda j: reg(32 + 4 * j, 1024) if j < 8 else reg(97 + 4 * (j - 8), 1024)
    AT_done = []
    t_scr = (pe.sem, pe.count)
    for f in range(NF):
        s, (wg, wu), tw = weights([(0, (8, P), wfi[:, :, f * P:(f + 1) * P]),
                                   (1024, (8, P), wfi[:, :, FF + f * P:FF + (f + 1) * P])])
        pe.wait(tw, *H2_done)
        for hf in range(2):
            h_ = slice(hf * 512, (hf + 1) * 512)
            bg, bu = bank(), bank()
            for k in range(8):
                tg = mm(ps[:, bg, :], wg[:, k, :], H2[:, k, h_], k == 0, k == 7, k == 7)
            for k in range(8):
                tu = mm(ps[:, bu, :], wu[:, k, :], H2[:, k, h_], k == 0, k == 7, k == 7)
            v = actT(f)[:, h_]
            act.wait(tg, wout_last, t_scr)
            t1 = act.do(lambda e, v=v, bg=bg: e.activation(v, ps[:, bg, :], ACT.Silu))
            bfree[bg] = t1
            dve.wait(t1, tu)
            t2 = dve.do(lambda e, v=v, bu=bu: e.tensor_tensor(v, ps[:, bu, :], v, ALU.mult))
            bfree[bu] = t2
            AT_done.append(t2)
        wfree[s] = tu
    wfo = a["w_ffn_out"][0].rearrange("(c p) n -> p c n", p=P)
    X3_t = [None] * NT
    for q in range(4):
        qs = slice(q * 256, (q + 1) * 256)
        s1, (wA,), tA = weights([(0, (11, 256), wfo[:, 0:11, qs])])
        s2, (wB,), tB = weights([(0, (11, 256), wfo[:, 11:22, qs])])
        pe.wait(tA, *AT_done)
        for i in range(NT):
            b = bank()
            for f in range(NF):
                if f == 11:
                    pe.wait(tB)
                w = wA[:, f, :] if f < 11 else wB[:, f - 11, :]
                t = mm(ps[:, b, 0:256], actT(f)[:, i * P:(i + 1) * P], w, f == 0, f == NF - 1, f == NF - 1)
            dve.wait(t)
            bfree[b] = dve.do(lambda e, i=i, b=b, qs=qs: e.tensor_tensor(X[:, i, qs], ps[:, b, 0:256], X[:, i, qs],
                                                                        ALU.add))
            X3_t[i] = bfree[b]
        wfree[s1] = wfree[s2] = t
    ffn_last = t

    wada = a["w_ada_2"][0].rearrange("(c p) n -> p c n", p=P)
    cv = m(16)
    modT = m(48, 2)
    G1 = reg(32, 1024)
    G2 = reg(36, 1024)
    rowt = [reg(40 + 2 * j, 512) for j in range(2)]
    rowb = [reg(44 + 2 * j, 512) for j in range(2)]
    crow = reg(48, P)
    L = land("crow")
    sp.wait(ffn_last)
    L.dma(sp, crow[0:8, :], a["c_2"].rearrange("o (c p) -> (o c) p", p=P))
    lams = reg(51, 256)
    for i, n in enumerate(("lambda_q1_2", "lambda_k1_2", "lambda_q2_2", "lambda_k2_2")):
        L.dma(sp, lams[:, i * 64:(i + 1) * 64], a[n].to_broadcast([P, 64]))
    t = L.dma(sp, crow[8:16, :], a["c_ctx_2"].rearrange("(c p) -> c p", p=P))
    t_crow = t
    act.wait(t)
    t = act.do(lambda e: e.activation(crow[0:16, :], crow[0:16, :], ACT.Silu))
    pe.wait(t)
    b = bank()
    t = tr(ps[:, b, 0:16], crow[0:16, :], ident[0:16, 0:16], True)
    dve.wait(t)
    t_cv = dve.do(lambda e: e.tensor_copy(cv.rearrange("p (k r) -> p r k", r=2),
                                          ps[:, b, 0:16].rearrange("p (r k) -> p r k", r=2)))
    bfree[b] = t_cv
    pe.wait(t_cv)
    gl = land("gb")
    gl.dma(sp, G1, a["norm_post_mix_2"].to_broadcast([P, 1024]))
    t_gb = gl.dma(sp, G2, a["norm_post_ffn_2"].to_broadcast([P, 1024]))
    rb_free = [None, None]
    row_free = [None, None]
    for n_ in range(24):
        j = n_ % 2
        ns = slice(n_ * 256, (n_ + 1) * 256)
        s, (w,), tw = weights([(0, (8, 256), wada[:, :, ns])])
        sp.wait(rb_free[j])
        tb = land(f"rb{j}").dma(sp, rowb[j][0:2, 0:256], a["b_ada_2"][:, ns].to_broadcast([2, 256]))
        pe.wait(tw)
        b = bank()
        for k in range(8):
            t = mm(ps[0:2, b, 0:256], cv[:, 2 * k:2 * k + 2], w[:, k, :], k == 0, k == 7, k == 7)
        wfree[s] = t
        dve.wait(t, tb, row_free[j])
        t = dve.do(lambda e, j=j, b=b: e.tensor_tensor(rowt[j][0:2, 0:256], ps[0:2, b, 0:256], rowb[j][0:2, 0:256],
                                                       ALU.add))
        bfree[b] = rb_free[j] = t
        pe.wait(t)
        b = bank()
        for q in range(2):
            t = tr(ps[:, b, q * 2:q * 2 + 2], rowt[j][0:2, q * P:(q + 1) * P], ident[0:2, 0:2], q == 1)
        dve.wait(t)
        t_mod = dve.do(lambda e, n_=n_, b=b: e.tensor_copy(modT[:, 2 * n_:2 * n_ + 2, :].rearrange("p a b -> p (a b)"),
                                                           ps[:, b, 0:4]))
        bfree[b] = t_mod
        chunk = n_ // 4
        if chunk in (2, 5):
            G = G1 if chunk == 2 else G2
            gs = slice((n_ % 4) * 256, (n_ % 4 + 1) * 256)
            b = bank()
            t = mm(ps[:, b, 0:256], sel[0:2, :], rowt[j][0:2, 0:256], True, True, True)
            dve.wait(t, t_gb)
            bfree[b] = dve.do(lambda e, b=b, G=G, gs=gs: e.tensor_tensor(G[:, gs], ps[:, b, 0:256], G[:, gs], ALU.mult))
            t_G = bfree[b]
        row_free[j] = t
    mg, mgc, mg2 = m(8), m(8), m(8)
    dve.wait(t_mod)

    def gain(dst, name, chunk, r):
        v = modT[:, chunk * 8:(chunk + 1) * 8, r:r + 1].rearrange("p a b -> p (a b)")
        g0 = colsA[:, where[name]:where[name] + 8]
        return dve.do(lambda e: e.scalar_tensor_tensor(out=dst, in0=v, scalar=1.0, in1=g0, op0=ALU.add, op1=ALU.mult))

    gain(mg, "norm_pre_mix_2", 1, 0)
    gain(mgc, "norm_pre_mix_2", 1, 1)
    t_mg = gain(mg2, "norm_pre_ffn_2", 4, 0)
    shift = lambda chunk, f, r: modT[:, chunk * 8 + f, r:r + 1]
    lamc = m(8)
    t_lams = t_crow
    dve.wait(t_lams)
    lt = reg(50, 128)
    t1 = dve.do(lambda e: e.tensor_tensor(lt[:, 0:64], lams[:, 0:64], lams[:, 64:128], ALU.mult))
    t2 = dve.do(lambda e: e.tensor_tensor(lt[:, 64:128], lams[:, 128:192], lams[:, 192:256], ALU.mult))
    dve.wait(t1, t2)
    t1 = dve.do(lambda e: e.tensor_reduce(lamc[:, 0:2], lt.rearrange("p (a b) -> p a b", a=2), AX.X, ALU.add))
    act.wait(t1)
    t1 = act.do(lambda e: e.activation(lamc[:, 2:4], lamc[:, 0:2], ACT.Exp))
    dve.wait(t1)
    t1 = dve.do(lambda e: e.tensor_tensor(lamc[:, 4:5], lamc[:, 3:4], lamc[:, 2:3], ALU.subtract))
    dve.wait(t1)
    t_lam = dve.do(lambda e: e.tensor_scalar(lamc[:, 5:6], lamc[:, 4:5], -0.2, None, ALU.add))
    nlam = lamc[:, 5:6]

    XC = reg(145, 8, CTX)
    xc = [reg(64 + 4 * j, D) for j in range(2)]
    sp.wait(ffn_last)
    cin = a["ctx_2"].rearrange("o s d -> (o s) d")
    xc_t = [land(f"xc{j}").dma(sp, xc[j], cin[j * P:(j + 1) * P, :]) for j in range(2)]
    cs_ = lambda i: reg(72 + 4 * i, D)
    XC_done, _ = norm_T(lambda i: xc[i], xc_t, cs_, cs_, XC, lambda f: mgc[:, f:f + 1], lambda f: shift(0, f, 1),
                        ffn_last, ntile=2, gain_t=t_mg)
    XN = reg(113, 8, 1024)
    dve.wait(*XC_done)
    act.wait(*XC_done)
    sc3 = lambda i: reg(64 + 4 * i, D)
    act.wait((pe.sem, pe.count))
    XN_done, _ = norm_T(lambda i: X[:, i, :], X3_t, sc3, sc3, XN, lambda f: mg[:, f:f + 1], lambda f: shift(0, f, 0),
                        ffn_last, gain_t=t_mg)
    t_sc3 = (pe.sem, pe.count)

    Q2 = reg(48, 4, 1024)
    K2 = reg(64, 4, 1280)
    V2 = reg(84, 10, 512)
    COS = reg(40, 1024)
    SIN = reg(44, 1024)
    QR = [reg(104 + 2 * j, 512) for j in range(4)]
    rot = m(P)
    sp.wait(t_G, t_lam, t_sc3)
    cl = land("cs")
    cl.dma(sp, COS, a["cos"])
    cl.dma(sp, rot, a["rot"])
    t_cs = cl.dma(sp, SIN, a["sin"])
    w2 = a["w_in_2"][0].rearrange("(c p) n -> p c n", p=P)
    qr_free = [None] * 4
    n = 0
    QK2_done = []
    for which, base, dst, off in (("q", 0, Q2, 0), ("k", 512, K2, CTX)):
        for mt in range(4):
            s, (w,), tw = weights([(0, (8, P), w2[:, :, base + mt * P:base + (mt + 1) * P])])
            pe.wait(tw, t_cs, *XN_done)
            for hf in range(2):
                h_ = slice(hf * 512, (hf + 1) * 512)
                j = n % 4
                n += 1
                b = bank()
                for k in range(8):
                    t = mm(ps[:, b, :], w[:, k, :], XN[:, k, h_], k == 0, k == 7, k == 7)
                act.wait(t, qr_free[j], t_sc3)
                t1 = act.do(lambda e, j=j, b=b: e.copy(QR[j], ps[:, b, :]))
                bfree[b] = t1
                pe.wait(t1)
                b = bank()
                t = mm(ps[:, b, :], rot, QR[j], True, True, True)
                d = dst[:, mt, off + hf * 512:off + (hf + 1) * 512]
                dve.wait(t, t_cs)
                t2 = dve.do(lambda e, d=d, b=b, h_=h_: e.tensor_tensor(d, ps[:, b, :], SIN[:, h_], ALU.mult))
                bfree[b] = t2
                t3 = dve.do(lambda e, j=j, h_=h_: e.tensor_tensor(QR[j], QR[j], COS[:, h_], ALU.mult))
                dve.wait(t2, t3)
                t4 = dve.do(lambda e, d=d, j=j: e.tensor_tensor(d, d, QR[j], ALU.add))
                qr_free[j] = t4
                QK2_done.append(t4)
            if which == "k":
                b = bank()
                pe.wait(*XC_done)
                for k in range(8):
                    t = mm(ps[:, b, 0:CTX], w[:, k, :], XC[:, k, :], k == 0, k == 7, k == 7)
                bfree[b] = copy(K2[:, mt, 0:CTX], ps[:, b, 0:CTX], [t])
                QK2_done.append(bfree[b])
            wfree[s] = t
    V2_done = []
    for q in range(2):
        s, (w,), tw = weights([(0, (8, 256), w2[:, :, 1024 + q * 256:1024 + (q + 1) * 256])])
        pe.wait(tw)
        for i in range(10):
            b = bank()
            for k in range(8):
                lhs = XC[:, k, i * P:(i + 1) * P] if i < 2 else XN[:, k, (i - 2) * P:(i - 1) * P]
                t = mm(ps[:, b, 0:256], lhs, w[:, k, :], k == 0, k == 7, k == 7)
            bfree[b] = copy(V2[:, i, q * 256:(q + 1) * 256], ps[:, b, 0:256], [t, t_sc3])
            V2_done.append(bfree[b])
        wfree[s] = t
    MXc = reg(104, 2, 1024)
    MXd = reg(145, 2, 1024)
    mixc = lambda ct: (MXc if ct < 2 else MXd)[:, ct % 2, :]
    U = [reg(40, 1024), reg(44, 1024)]
    u_free = [[*QK2_done], [*QK2_done]]
    v2_last = t
    MX_done = []
    for ct in range(4):
        s, (wb, wc_, wx), tw = weights([(0, (8, P), w2[:, :, 1536 + ct * P:1536 + (ct + 1) * P]),
                                        (1024, (8, P), w2[:, :, 2048 + ct * P:2048 + (ct + 1) * P]),
                                        (2048, (8, P), w2[:, :, 2560 + ct * P:2560 + (ct + 1) * P])])
        u = U[ct % 2]
        pe.wait(tw)
        tu = []
        tb_ = []
        for hf in range(2):
            h_ = slice(hf * 512, (hf + 1) * 512)
            bc, bx, bb = bank(), bank(), bank()
            for k in range(8):
                t1 = mm(ps[:, bc, :], wc_[:, k, :], XN[:, k, h_], k == 0, k == 7, k == 7)
            for k in range(8):
                t2 = mm(ps[:, bx, :], wx[:, k, :], XN[:, k, h_], k == 0, k == 7, k == 7)
            for k in range(8):
                t3 = mm(ps[:, bb, :], wb[:, k, :], XN[:, k, h_], k == 0, k == 7, k == 7)
            act.wait(t1, u_free[ct % 2])
            t4 = act.do(lambda e, u=u, h_=h_, bc=bc: e.copy(u[:, h_], ps[:, bc, :]))
            bfree[bc] = t4
            dve.wait(t4, t2, u_free[ct % 2])
            t5 = dve.do(lambda e, u=u, h_=h_, bx=bx: e.tensor_tensor(u[:, h_], ps[:, bx, :], u[:, h_], ALU.mult))
            bfree[bx] = t5
            tu.append(t5)
            tb_.append((bb, t3, h_))
        wfree[s] = t3
        o = mixc(ct)
        wcol = lambda w, ct=ct: col("conv_w", w * 4 + ct)
        dve.wait(*tu, v2_last)
        t = dve.do(lambda e, o=o, u=u, c=wcol(1): e.tensor_scalar(o, u, c, None, ALU.mult))
        dve.wait(t)
        t = dve.do(lambda e, o=o, u=u, c=wcol(0): e.scalar_tensor_tensor(out=o[:, 1:], in0=u[:, 0:S - 1], scalar=c,
                                                                        in1=o[:, 1:], op0=ALU.mult, op1=ALU.add))
        dve.wait(t)
        t = dve.do(lambda e, o=o, u=u, c=wcol(2): e.scalar_tensor_tensor(out=o[:, 0:S - 1], in0=u[:, 1:], scalar=c,
                                                                        in1=o[:, 0:S - 1], op0=ALU.mult, op1=ALU.add))
        u_free[ct % 2] = [t]
        dve.wait(t)
        for bb, tt_, h_ in tb_:
            dve.wait(tt_)
            t = dve.do(lambda e, o=o, h_=h_, bb=bb: e.tensor_tensor(o[:, h_], ps[:, bb, :], o[:, h_], ALU.mult))
            bfree[bb] = t
            MX_done.append(t)
    xn_last = (pe.sem, pe.count)

    MXa = reg(113, 4, 1024)
    PA = [[reg(129, 1280), reg(134, 1280)], [reg(139, 1280), reg(40, 1280)]]
    PT2 = reg(153 + 36, 10, P)
    OM2 = [reg(153 + 41 + 0.5 * j, P) for j in range(2)]
    m8 = [[m(1), m(1)], [m(1), m(1)]]
    s8 = [[m(1), m(1)], [m(1), m(1)]]
    r8 = [[m(2), m(2)], [m(2), m(2)]]
    sub_ss = [m(1), m(1)]
    sub_iv = [m(1), m(1)]
    subg = m(2)
    gsl = land("subg")
    t_sg = gsl.dma(sp, subg[:, 0:1], a["subln_g_2"].rearrange("o d -> d o"))
    dve.wait(t_sg)
    t_sg = dve.do(lambda e: e.tensor_scalar(subg[:, 1:2], subg[:, 0:1], 0.8, None, ALU.mult))
    SQ2 = reg(153 + 42.5, P)
    slot_free_all = [wfree[i] for i in range(NW)]
    act.wait(*[t for t in slot_free_all if t])
    dve.wait(*[t for t in slot_free_all if t])
    units = [(h, i) for h in range(4) for i in range(NT)]
    st = {}
    p_free = [xn_last, xn_last]
    pt2_free = [None]
    sq_free = [None]

    def qk2(u):
        h, i = units[u]
        j = u % 2
        ex = []
        for mp in range(2):
            b0 = 3 * mp
            pe.wait(bfree[b0], bfree[b0 + 1], bfree[b0 + 2])
            r = slice(mp * 64, mp * 64 + 64)
            for c0 in range(0, 1280, 512):
                n = min(512, 1280 - c0)
                t = mm(ps[:, b0 + c0 // 512, 0:n], Q2[r, h, i * P:(i + 1) * P], K2[r, h, c0:c0 + n], True, True,
                       c0 == 1024)
            sv = ps[:, b0:b0 + 3, :].rearrange("p a b -> p (a b)")[:, 0:1280]
            dve.wait(t)
            t1 = dve.do(lambda e, sv=sv, mp=mp: e.tensor_reduce(m8[j][mp], sv, AX.X, ALU.max, negate=True))
            dve.wait(t1)
            t1 = dve.do(lambda e, mp=mp: e.tensor_scalar(m8[j][mp], m8[j][mp], 0.125, None, ALU.mult))
            act.wait(t1, p_free[j])
            t2 = act.do(lambda e, sv=sv, mp=mp: e.activation(PA[j][mp], sv, ACT.Exp, bias=m8[j][mp], scale=0.125,
                                                             accum_out=s8[j][mp]))
            bfree[b0] = bfree[b0 + 1] = bfree[b0 + 2] = t2
            ex.append(t2)
        dve.wait(*ex)
        t0 = dve.do(lambda e: e.reciprocal(r8[j][0][:, 0:1], s8[j][0]))
        t1 = dve.do(lambda e: e.reciprocal(r8[j][1][:, 0:1], s8[j][1]))
        dve.wait(t1, t_lam)
        t1 = dve.do(lambda e: e.tensor_scalar(r8[j][1][:, 1:2], r8[j][1][:, 0:1], nlam, None, ALU.mult))
        dve.wait(t0)
        t2 = dve.do(lambda e: e.tensor_scalar(PA[j][0], PA[j][0], r8[j][0][:, 0:1], None, ALU.mult))
        dve.wait(t1, t2)
        st[u] = dve.do(lambda e: e.scalar_tensor_tensor(out=PA[j][0], in0=PA[j][1], scalar=r8[j][1][:, 1:2],
                                                        in1=PA[j][0], op0=ALU.mult, op1=ALU.add))

    tb67 = [0]

    def rest2(u):
        h, i = units[u]
        j = u % 2
        pe.wait(st[u])
        ts = []
        for c0 in (0, 4, 8):
            n = min(4, 10 - c0)
            b = 6 + tb67[0] % 2
            tb67[0] += 1
            pe.wait(bfree[b])
            for c in range(n):
                t = tr(ps[:, b, c * P:(c + 1) * P], PA[j][0][:, (c0 + c) * P:(c0 + c + 1) * P], ident, c == n - 1)
            bfree[b] = copy(PT2[:, c0:c0 + n, :].rearrange("p a b -> p (a b)"), ps[:, b, 0:n * P],
                            [t, pt2_free[0]])
            ts.append(bfree[b])
        p_free[j] = t
        b = 6 + tb67[0] % 2
        tb67[0] += 1
        pe.wait(bfree[b], *V2_done)
        for c in range(10):
            pe.wait(ts[c // 4])
            t = mm(ps[:, b, 0:P], PT2[:, c, :], V2[:, c, h * P:(h + 1) * P], c == 0, c == 9, c == 9)
        pt2_free[0] = t
        act.wait(t, sq_free[0])
        t1 = act.do(lambda e: e.activation(SQ2, ps[:, b, 0:P], ACT.Square, accum_out=sub_ss[j]))
        sq_free[0] = t1
        dve.wait(t1)
        t1 = dve.do(lambda e: e.tensor_scalar(sub_ss[j], sub_ss[j], 1.0 / P, EPS, ALU.mult, ALU.add))
        pool.wait(t1)
        t1 = pool.do(lambda e: e.tensor_tensor(sub_iv[j], sub_ss[j], nhalf[:, 0:1], ALU.pow))
        dve.wait(t1, st.get(("o", u - 2)))
        t1 = dve.do(lambda e: e.tensor_scalar(OM2[j], ps[:, b, 0:P], sub_iv[j], None, ALU.mult))
        bfree[b] = t1
        st[("m", u)] = t1

    MXa_done = []

    def fin2(u):
        h, i = units[u]
        j = u % 2
        b = 6 + tb67[0] % 2
        tb67[0] += 1
        pe.wait(st[("m", u)], bfree[b])
        t = tr(ps[:, b, 0:P], OM2[j], ident, True)
        st[("o", u)] = t
        act.wait(t, t_sg)
        bfree[b] = act.do(lambda e: e.activation(MXa[:, h, i * P:(i + 1) * P], ps[:, b, 0:P], ACT.Copy,
                                                 scale=subg[:, 1:2]))
        MXa_done.append(bfree[b])

    pe.wait(*QK2_done, *[x for x in bfree if x])
    dve.wait(xn_last, *MX_done)
    act.wait(xn_last, *MX_done)
    nu = len(units)
    qk2(0)
    for u in range(nu):
        if u + 1 < nu:
            qk2(u + 1)
        if u >= 1:
            fin2(u - 1)
        rest2(u)
    fin2(nu - 1)
    att2_last = (pe.sem, pe.count)

    wo2 = a["w_out_2"][0].rearrange("(c p) n -> p c n", p=P)
    for i in range(NW):
        wfree[i] = [wfree[i]] if wfree[i] else []
    wnext[0] = 0
    wfree[3] = [att2_last, *MXa_done[-2:]]
    ws = [weights([(0, (8, 256), wo2[:, :, q * 256:(q + 1) * 256])]) for q in range(4)]
    mixT = lambda k: MXa[:, k, :] if k < 4 else mixc(k - 4)
    junk = [reg(64 + 4 * j, 1024) for j in range(2)]
    tmp = [reg(72 + 4 * j, 1024) for j in range(2)]
    X4_t = []
    mst = [m(2), m(2)]
    junk_free = [None, None]
    for i in range(NT):
        j = i % 2
        banks = []
        for q in range(4):
            s, (w,), tw = ws[q]
            pe.wait(tw, *MXa_done, *MX_done)
            b0 = 2 * (i % 4) + q // 2
            if q % 2 == 0:
                pe.wait(bfree[b0])
            for k in range(8):
                t = mm(ps[:, b0, (q % 2) * 256:(q % 2) * 256 + 256], mixT(k)[:, i * P:(i + 1) * P], w[:, k, :],
                       k == 0, k == 7, k == 7)
            if i == NT - 1:
                wfree[s] = t
        b0 = 2 * (i % 4)
        v = ps[:, b0:b0 + 2, :].rearrange("p a b -> p (a b)")
        act.wait(t, att2_last, junk_free[j])
        t1 = act.do(lambda e, v=v, j=j: e.activation(junk[j], v, ACT.Square, accum_out=mst[j][:, 0:1]))
        dve.wait(t1)
        t1 = dve.do(lambda e, j=j: e.tensor_scalar(mst[j][:, 0:1], mst[j][:, 0:1], 1.0 / D, EPS, ALU.mult, ALU.add))
        pool.wait(t1)
        t1 = pool.do(lambda e, j=j: e.tensor_tensor(mst[j][:, 1:2], mst[j][:, 0:1], nhalf[:, 0:1], ALU.pow))
        dve.wait(t1, t_G, att2_last)
        t2 = dve.do(lambda e, v=v, j=j: e.scalar_tensor_tensor(out=tmp[j], in0=v, scalar=mst[j][:, 1:2], in1=G1,
                                                               op0=ALU.mult, op1=ALU.mult))
        bfree[b0] = bfree[b0 + 1] = t2
        dve.wait(t2)
        t3 = dve.do(lambda e, i=i, j=j: e.tensor_tensor(X[:, i, :], X[:, i, :], tmp[j], ALU.add))
        junk_free[j] = t2
        X4_t.append(t3)
    wo2_last = (pe.sem, pe.count)

    XM = reg(40, 8, 1024)
    sc4 = lambda i: reg(104 + 4 * i, D)
    act.wait(wo2_last)
    dve.wait(wo2_last, att2_last)
    XM_done, ss_t = norm_T(lambda i: X[:, i, :], X4_t, sc4, sc4, XM, lambda f: mg2[:, f:f + 1],
                           lambda f: shift(3, f, 0), [wo2_last, X4_t[-1]])
    lst = land("xhd")
    sp.wait((dve.sem, dve.count), XM_done)
    for i in range(NT):
        t_xh = lst.dma(sp, xh_dram[i * P:(i + 1) * P, :], sc4(i))
    zero = reg(168, 1024)
    dve.wait(wo2_last, att2_last)
    t = dve.do(lambda e: e.memset(zero, 0.0))
    sp.wait(t)
    lz = land("ffz")
    for i in range(NT):
        t_ffz = lz.dma(sp, ff_dram[i * P:(i + 1) * P, :], zero)

    wr = reg(136, 8, NE)
    t_wr = land("wr").dma(sp, wr, a["w_router_2"][0].rearrange("(c p) n -> p c n", p=P))
    affT = reg(172, 1024)
    w1_ = reg(176, 1024)
    lg = reg(180, 8, NE)
    mx8 = reg(181, 8)
    ix8 = reg(183.5, P).bitcast(U32)
    top = reg(182, P)
    ixf = reg(183, P)
    gT = m(NE)
    iT = m(NE).bitcast(U32)
    pe.wait(t_wr, *XM_done)
    b = bank()
    for i in range(NT):
        for k in range(8):
            t = mm(ps[:, b, i * NE:(i + 1) * NE], XM[:, k, i * P:(i + 1) * P], wr[:, k, :], k == 0, k == 7,
                   i == 7 and k == 7)
    v = ps[:, b, 0:P].rearrange("p (a b) -> p a b", a=8)
    bc = lambda x: x.rearrange("p (a o) -> p a o", o=1).to_broadcast([P, 8, NE])
    dve.wait(t)
    t = dve.do(lambda e: e.tensor_reduce(mx8, v, AX.X, ALU.max))
    dve.wait(t)
    t = dve.do(lambda e: e.tensor_tensor(lg, v, bc(mx8), ALU.subtract))
    bfree[b] = t
    act.wait(t)
    t = act.do(lambda e: e.activation(lg, lg, ACT.Exp))
    dve.wait(t)
    t = dve.do(lambda e: e.tensor_reduce(mx8, lg, AX.X, ALU.add))
    dve.wait(t)
    t = dve.do(lambda e: e.reciprocal(mx8, mx8))
    dve.wait(t)
    t = dve.do(lambda e: e.tensor_tensor(lg, lg, bc(mx8), ALU.mult))
    pe.wait(t)
    for hf in range(2):
        b = bank()
        for i in range(4):
            t = tr(ps[0:NE, b, i * P:(i + 1) * P], lg[:, hf * 4 + i, :], ident, i == 3)
        dve.wait(t)
        t = dve.do(lambda e, b=b, hf=hf: e.tensor_copy(affT[0:NE, hf * 512:(hf + 1) * 512], ps[0:NE, b, :]))
        bfree[b] = t
    dve.wait(t)
    src, dst = affT, w1_
    for r in range(CAP // 8):
        rs_ = slice(r * 8, r * 8 + 8)
        t = dve.do(lambda e, src=src, rs_=rs_: e.max(top[0:NE, rs_], src[0:NE, :]))
        dve.wait(t)
        dve.do(lambda e, src=src, rs_=rs_: e.max_index(ix8[0:NE, rs_], top[0:NE, rs_], src[0:NE, :]))
        t = dve.do(lambda e, src=src, dst=dst, rs_=rs_: e.match_replace(dst[0:NE, :], top[0:NE, rs_], src[0:NE, :],
                                                                        -1.0))
        dve.wait(t)
        src, dst = dst, src
    t = dve.do(lambda e: e.tensor_copy(ixf[0:NE, :], ix8[0:NE, :]))
    pe.wait(t)
    b = bank()
    tr(ps[:, b, 0:NE], top[0:NE, :], ident[0:NE, 0:NE], False)
    t = tr(ps[:, b, NE:2 * NE], ixf[0:NE, :], ident[0:NE, 0:NE], True)
    dve.wait(t)
    t_gT = dve.do(lambda e: e.tensor_copy(gT, ps[:, b, 0:NE]))
    t_iT = dve.do(lambda e: e.tensor_copy(iT, ps[:, b, NE:2 * NE]))
    bfree[b] = t_iT
    router_last = t_iT

    ring = [72 + 16 * j for j in range(6)]
    rfree = [[wo2_last, (pe.sem, pe.count)] for _ in range(6)]
    rn = [0]

    def eweights(src):
        j = rn[0] % 6
        rn[0] += 1
        sp.wait(rfree[j])
        v_ = reg(ring[j], 8, 512)
        return j, v_, land(f"e{j}").dma(sp, v_, src)

    for j in range(6):
        rfree[j] = [t_xh, t_ffz, wo2_last, (pe.sem, pe.count)]
    XS = [reg(40 + 4 * j, D) for j in range(2)]
    XST = [reg(48 + 4 * j, 8, P) for j in range(2)]
    HID = [reg(56 + 4 * j, D) for j in range(2)]
    HIT = [reg(64 + 4 * j, 8, P) for j in range(2)]
    YS = [reg(184 + 4 * j, D) for j in range(3)]
    wg2 = a["w_gate_2"][0].rearrange("e (c p) n -> e p c n", p=P)
    wu2 = a["w_up_2"][0].rearrange("e (c p) n -> e p c n", p=P)
    wd2 = a["w_down_2"][0].rearrange("e (c p) n -> e p c n", p=P)
    xs_t, xs_free = {}, [None, None]
    ys_t = [None] * 3
    sc_last = [None]
    scl_ = land("scat")

    def gather(e_):
        j = e_ % 2
        pool.wait(t_iT, t_xh, xs_free[j], (pe.sem, pe.count) if e_ < 2 else None)
        lg_ = land(f"xs{j}")
        lg_.count += 16
        pool.engine.indirect_dma_start(
            XS[j], None, xh_dram, bass.IndirectOffsetOnAxis(ap=iT[:, e_:e_ + 1], axis=0),
            bounds_check=S - 1).then_inc(lg_.sem, 16)
        xs_t[e_] = (lg_.sem, lg_.count)

    gather(0)
    gather(1)
    for e_ in range(NE):
        j = e_ % 2
        wts = []
        for w_ in (wg2, wu2):
            for q in range(2):
                wts.append(eweights(w_[e_, :, :, q * 512:(q + 1) * 512]))
        pe.wait(xs_t[e_])
        done = []
        for g_ in range(2):
            b = bank()
            for f in range(4):
                t = tr(ps[:, b, f * P:(f + 1) * P], XS[j][:, (g_ * 4 + f) * P:(g_ * 4 + f + 1) * P], ident, f == 3)
            tt_ = []
            for f in range(4):
                ff_ = g_ * 4 + f
                q_ = act if g_ == 0 else dve
                q_.wait(t)
                o, i_, ga_, sh_ = XST[j][:, ff_, :], ps[:, b, f * P:(f + 1) * P], mg2[:, ff_:ff_ + 1], shift(3, ff_, 0)
                if q_ is act:
                    tt_.append(act.do(lambda e, o=o, i_=i_, ga_=ga_, sh_=sh_: e.activation(o, i_, ACT.Identity,
                                                                                          bias=sh_, scale=ga_)))
                else:
                    tt_.append(dve.do(lambda e, o=o, i_=i_, ga_=ga_, sh_=sh_: e.tensor_scalar(o, i_, ga_, sh_,
                                                                                             ALU.mult, ALU.add)))
            bfree[b] = tt_[-1]
            done.append(tt_[-1])
        xs_free[j] = t
        pe.wait(*done)
        bs = []
        for n_, (sl_, w_, tw) in enumerate(wts):
            b = bank()
            pe.wait(tw)
            for k in range(8):
                t = mm(ps[:, b, :], XST[j][:, k, :], w_[:, k, :], k == 0, k == 7, k == 7)
            rfree[sl_] = t
            bs.append((b, t))
        th = []
        for q in range(2):
            h_ = HID[j][:, q * 512:(q + 1) * 512]
            act.wait(bs[q][1])
            t1 = act.do(lambda e, h_=h_, b=bs[q][0]: e.activation(h_, ps[:, b, :], ACT.Silu))
            bfree[bs[q][0]] = t1
            dve.wait(t1, bs[2 + q][1])
            t2 = dve.do(lambda e, h_=h_, b=bs[2 + q][0]: e.tensor_tensor(h_, ps[:, b, :], h_, ALU.mult))
            bfree[bs[2 + q][0]] = t2
            th.append(t2)
        dn = [eweights(wd2[e_, :, :, q * 512:(q + 1) * 512]) for q in range(2)]
        td = []
        for g_ in range(2):
            pe.wait(th[g_])
            b = bank()
            for f in range(4):
                t = tr(ps[:, b, f * P:(f + 1) * P], HID[j][:, (g_ * 4 + f) * P:(g_ * 4 + f + 1) * P], ident, f == 3)
            bfree[b] = copy(HIT[j][:, g_ * 4:g_ * 4 + 4, :].rearrange("p a b -> p (a b)"), ps[:, b, :], [t])
            td.append(bfree[b])
        pe.wait(*td)
        jy = e_ % 3
        ty = []
        for q in range(2):
            sl_, w_, tw = dn[q]
            b = bank()
            pe.wait(tw)
            for k in range(8):
                t = mm(ps[:, b, :], HIT[j][:, k, :], w_[:, k, :], k == 0, k == 7, k == 7)
            rfree[sl_] = t
            o = YS[jy][:, q * 512:(q + 1) * 512]
            bfree[b] = scaled_copy(o, ps[:, b, :], gT[:, e_:e_ + 1], None, [t, ys_t[jy], t_gT])
            ty.append(bfree[b])
        pool.wait(*ty, t_ffz, sc_last[0])
        scl_.count += 16
        pool.engine.indirect_dma_start(
            ff_dram, bass.IndirectOffsetOnAxis(ap=iT[:, e_:e_ + 1], axis=0), YS[jy], None,
            bounds_check=S - 1, compute_op=ALU.add).then_inc(scl_.sem, 16)
        sc_last[0] = ys_t[jy] = (scl_.sem, scl_.count)
        if e_ + 2 < NE:
            gather(e_ + 2)

    out2 = out.rearrange("o s d -> (o s) d")
    pe_last = (pe.sem, pe.count)
    lo = land("out")
    for i in range(NT):
        f_ = reg(72 + 4 * i, D)
        sp.wait(sc_last[0], pe_last)
        tf = land(f"f{i}").dma(sp, f_, ff_dram[i * P:(i + 1) * P, :])
        act.wait(tf, pe_last)
        jk = reg(104 + 4 * i, D)
        t1 = act.do(lambda e, i=i, f_=f_, jk=jk: e.activation(jk, f_, ACT.Square, accum_out=ss[:, i:i + 1]))
        t_inv = rms_inv(i, i + 1, 1024.0, [t1])
        dve.wait(t_inv)
        t2 = dve.do(lambda e, i=i, f_=f_: e.scalar_tensor_tensor(out=f_, in0=f_, scalar=inv[:, i:i + 1], in1=G2,
                                                                op0=ALU.mult, op1=ALU.mult))
        dve.wait(t2)
        t3 = dve.do(lambda e, i=i, f_=f_: e.tensor_tensor(f_, f_, X[:, i, :], ALU.add))
        act.wait(t3)
        t_out = lo.dma(act, out2[i * P:(i + 1) * P, :], f_)
    sp.wait(t_out)


_INS = ["x", "g_mix", "w_in", "b_forget", "w_dw", "b_dw", "g_conv_ln", "b_conv_ln", "w_conv_out", "g_q", "g_k",
        "w_attn_out", "w_out", "g_ffn", "w_ffn_in", "w_ffn_out", "c_2", "ctx_2", "c_ctx_2", "w_ada_2", "b_ada_2",
        "norm_pre_mix_2", "norm_post_mix_2", "norm_pre_ffn_2", "norm_post_ffn_2", "w_in_2", "conv_w_2",
        "lambda_q1_2", "lambda_k1_2", "lambda_q2_2", "lambda_k2_2", "subln_g_2", "w_out_2", "w_router_2",
        "w_gate_2", "w_up_2", "w_down_2"]


def _tables():
    f = np.float32
    row = np.repeat(np.arange(16, dtype=f), 64)
    colv = np.tile(np.arange(64, dtype=f), 16)
    iv = (f(10000.0) ** (-np.arange(0, 32, 2, dtype=f) / f(32))).astype(f)
    ar, ac = row[:, None] * iv[None, :], colv[:, None] * iv[None, :]
    ang = np.concatenate([ar, ar, ac, ac], axis=-1)
    cos, sin = np.cos(ang).astype(f), np.sin(ang).astype(f)
    rot = np.zeros((128, 128), f)
    for b in range(0, 128, 32):
        for i in range(16):
            rot[b + 16 + i, b + i] = -1.0
            rot[b + i, b + 16 + i] = 1.0
    two = lambda t: np.ascontiguousarray(np.concatenate([t.T, t.T], axis=0))
    return {"cos": two(cos), "sin": two(sin), "rot": rot}


def kernel(**inputs):
    import concourse.bacc as _bacc
    from concourse.bass_utils import run_bass_kernel_spmd as _run

    nc = _bacc.Bacc("TRN2", target_bir_lowering=False, num_devices=1)
    arrays, args = {}, {}
    every = {n: inputs[n] for n in _INS}
    every.update(_tables())
    for name, v in every.items():
        v = np.ascontiguousarray(v)
        arrays[f"in_{name}_dram"] = v
        args[name] = nc.dram_tensor(f"in_{name}_dram", v.shape, mybir.dt.from_np(v.dtype), kind="ExternalInput").ap()
    o = nc.dram_tensor("out_0_dram", (1, S, D), F32, kind="ExternalOutput").ap()
    program(nc, args, o)
    r = _run(nc, [arrays], core_ids=[0])
    return r.results[0]["out_0_dram"]
```

```python
from contextlib import ExitStack

import numpy as np

import concourse.bass as bass
from concourse import mybir

ALU = mybir.AluOpType
ACT = mybir.ActivationFunctionType
F32 = mybir.dt.float32
F32R = mybir.dt.float32r
U32 = mybir.dt.uint32
AX = mybir.AxisListType

P = 128
S = 1024
D = 1024
NT = S // P
EPS = 1e-6
NEG = -1e30
KB = 256
CAP = 128
NE = 16
CTX = 256
FF = 2816
NF = FF // P
MISC = 1720


class Queue:

    def __init__(self, engine, sem):
        self.engine, self.sem, self.count, self.seen = engine, sem, 0, {}

    def wait(self, *tickets):
        for t in tickets:
            if t is None:
                continue
            if isinstance(t, list):
                self.wait(*t)
                continue
            sem, value = t
            if self.seen.get(sem.name, 0) < value:
                self.seen[sem.name] = value
                self.engine.wait_ge(sem, value)

    def do(self, fn):
        self.count += 1
        fn(self.engine).then_inc(self.sem, 1)
        return self.sem, self.count

    def run(self, fn):
        fn(self.engine)


class Landing:

    def __init__(self, sem):
        self.sem, self.count = sem, 0

    def dma(self, queue, out, in_):
        self.count += 16
        queue.engine.dma_start(out, in_).then_inc(self.sem, 16)
        return self.sem, self.count


def program(nc, a, out):
    ctx = ExitStack()
    with ctx:
        _program(nc, ctx, a, out)


def _program(nc, ctx, a, out):
    sem = lambda n: ctx.enter_context(nc.semaphore(n))
    pe, dve, act, pool, sp = (
        Queue(e, sem(n)) for e, n in ((nc.tensor, "s_pe"), (nc.vector, "s_dve"), (nc.scalar, "s_act"),
                                      (nc.gpsimd, "s_pool"), (nc.sync, "s_sp")))
    base = (nc.sbuf_base + 31) // 32 * 32
    misc = nc.alloc_sbuf_tensor_at("misc", [P, MISC], F32, offset=base + 201 * 1024)
    cvR = nc.alloc_sbuf_tensor_at("cvr", [P, 32], F32R, offset=base + 201 * 1024 + MISC * 4)
    ps = ctx.enter_context(nc.psum_tensor("ps", [P, 8, 512], F32))
    dram = lambda n, *shape: nc.dram_tensor(n, shape, F32, kind="Internal").ap()
    xh_dram, ff_dram, x3_dram, mod_dram = (dram("xhat_scratch", S, D), dram("ff_scratch", S, D),
                                           dram("x3_scratch", S, D), dram("mod_scratch", 4, 6 * D))
    landings = {}

    def land(name):
        if name not in landings:
            landings[name] = Landing(sem("d_" + name))
        return landings[name]

    places = {}

    def view(dtype, kb, shape):
        n = int(np.prod(shape))
        o = int(kb * 1024)
        assert o + 4 * n <= 201 * 1024
        name = f"{'r' if dtype == F32R else 'f'}{o}_{n}"
        if name not in places:
            places[name] = nc.alloc_sbuf_tensor_at(name, [P, n], dtype, offset=base + o)
        v = places[name][:, 0:n]
        if len(shape) == 2:
            v = v.rearrange("p (a b) -> p a b", a=shape[0])
        return v

    reg = lambda kb, *shape: view(F32, kb, shape)
    regR = lambda kb, *shape: view(F32R, kb, shape)
    pair = lambda hi, lo, *shape: (regR(hi, *shape), regR(lo, *shape))
    mpos = [0]

    def m(*shape):
        n = int(np.prod(shape))
        v = misc[:, mpos[0]:mpos[0] + n]
        mpos[0] += n
        assert mpos[0] <= MISC, mpos
        if len(shape) == 2:
            v = v.rearrange("p (a b) -> p a b", a=shape[0])
        return v

    pe_now = lambda: (pe.sem, pe.count)
    everyone = lambda: [(q.sem, q.count) for q in (pe, dve, act, pool) if q.count]

    bfree = [None] * 8
    bnext = [0]

    def bank():
        b = bnext[0] % 8
        bnext[0] += 1
        pe.wait(bfree[b])
        return b

    def mm(o, l, r, start, stop, last):
        fn = lambda e: e.matmul(o, l, r, start=start, stop=stop, skip_group_check=True)
        return pe.do(fn) if last else pe.run(fn)

    def mm3(o, l, r, start, stop, last):
        mm(o, l[0], r[0], start, False, False)
        mm(o, l[0], r[1], False, False, False)
        return mm(o, l[1], r[0], False, stop, last)

    at = lambda p, *idx: (p[0][idx], p[1][idx])

    def tr(o, i, ident_, last):
        fn = lambda e: e.transpose(o, i, ident_)
        return pe.do(fn) if last else pe.run(fn)

    def split(src, dst, waits, free=None):
        hi, lo = dst
        act.wait(*waits)
        act.wait(free)
        t = act.do(lambda e: e.activation(hi, src, ACT.Copy))
        dve.wait(*waits)
        dve.wait(t, free)
        return dve.do(lambda e: e.tensor_tensor(lo, src, hi.bitcast(F32), ALU.subtract))

    def split_psum(src, dst, scale, waits, free=None):
        hi, lo = dst
        act.wait(*waits)
        act.wait(free)
        if scale is None:
            t = act.do(lambda e: e.activation(hi, src, ACT.Copy))
        else:
            t = act.do(lambda e: e.activation(hi, src, ACT.Copy, scale=scale))
        dve.wait(*waits)
        dve.wait(t, free)
        if scale is None:
            return dve.do(lambda e: e.tensor_tensor(lo, src, hi.bitcast(F32), ALU.subtract))
        return dve.do(lambda e: e.scalar_tensor_tensor(out=lo, in0=src, scalar=scale, in1=hi.bitcast(F32),
                                                       op0=ALU.mult, op1=ALU.subtract))

    wparts = regR(169, 3, 2048)

    class Stream:

        def __init__(self, raw, parts, size, name, start=None):
            self.raw, self.parts, self.size, self.name = raw, parts, size, name
            self.specs, self.loaded, self.made, self.used = [], 0, 0, 0
            self.landed, self.ready = {}, {}
            self.raw_free, self.part_free = [start] * len(raw), [start] * len(parts)

        def add(self, *specs):
            self.specs += specs

        def load(self):
            while self.loaded < len(self.specs) and self.loaded < self.made + len(self.raw):
                i, r = self.loaded, self.loaded % len(self.raw)
                self.loaded += 1
                sp.wait(self.raw_free[r])
                off = 0
                for c, n, src in self.specs[i]:
                    v = reg(self.raw[r], self.size)[:, off:off + c * n]
                    self.landed[i] = land(f"{self.name}{r}").dma(sp, v.rearrange("p (c n) -> p c n", c=c), src)
                    off += c * n
                assert off <= self.size

        def slot(self, p_):
            if self.parts == [169, 177, 185]:
                both = wparts[:, p_, :]
            else:
                both = regR(self.parts[p_], 2 * self.size)
            return both[:, 0:self.size], both[:, self.size:2 * self.size]

        def make(self, ahead):
            self.load()
            while (self.made < len(self.specs) and self.made <= self.used + ahead
                   and self.part_free[self.made % len(self.parts)] != "in use"):
                i, r, p_ = self.made, self.made % len(self.raw), self.made % len(self.parts)
                n = sum(c * k for c, k, _ in self.specs[i])
                src = reg(self.raw[r], self.size)[:, 0:n]
                dst = tuple(x[:, 0:n] for x in self.slot(p_))
                t = split(src, dst, [self.landed[i]], self.part_free[p_])
                self.ready[i] = t
                self.raw_free[r] = t
                self.part_free[p_] = "in use"
                self.made += 1
                self.load()

        def get(self, ahead=2):
            self.make(ahead)
            i = self.used
            self.used += 1
            assert i in self.ready
            pe.wait(self.ready[i])
            out_, off = [], 0
            for c, n, _ in self.specs[i]:
                out_.append(tuple(x[:, off:off + c * n].rearrange("p (c n) -> p c n", c=c)
                                  for x in self.slot(i % len(self.parts))))
                off += c * n
            return i % len(self.parts), out_

        def done(self, slot, ticket, ahead=1):
            self.part_free[slot] = ticket

    ident = m(P)
    ones = m(P)
    tri = m(P)
    mask = m(P)
    nhalf = m(64)
    zt = pool.do(lambda e: e.memset(misc[:, 0:MISC], 0.0))
    pool.wait(zt)
    t_ident = pool.do(lambda e: e.affine_select(out=ident, in_=ident, compare_op=ALU.not_equal, fill=1.0, base=0,
                                                pattern=[[-1, P]], channel_multiplier=1))
    t_mask = pool.do(lambda e: e.affine_select(out=mask, in_=mask, compare_op=ALU.is_ge, fill=NEG, base=0,
                                               pattern=[[-1, P]], channel_multiplier=1))
    t_ones = pool.do(lambda e: e.memset(ones, 1.0))
    t_nhalf = pool.do(lambda e: e.memset(nhalf, -0.5))
    pool.wait(t_ones)
    t_tri = pool.do(lambda e: e.affine_select(out=tri, in_=ones, compare_op=ALU.is_ge, fill=0.0, base=0,
                                              pattern=[[1, P]], channel_multiplier=-1))
    consts = [t_ident, t_mask, t_ones, t_nhalf, t_tri]

    x_in = a["x"].rearrange("o s d -> (o s) d")
    xa = lambda i: reg(64 + 4 * i, D)
    xa_t = [land(f"x{i}").dma(sp, xa(i), x_in[i * P:(i + 1) * P, :]) for i in range(8)]
    w_in = a["w_in"][0].rearrange("(c p) n -> p c n", p=P)
    ws = Stream([153, 157, 161], [169, 177, 185], 1024, "w")
    for mt in range(4):
        ws.add([(8, P, w_in[:, :, 512 + mt * P:512 + (mt + 1) * P])], [(8, P, w_in[:, :, mt * P:(mt + 1) * P])])
    ws.add([(8, 8, w_in[:, :, 2560:2568])])
    ws.load()
    rows_a = reg(104, P)
    rows_b = reg(104.5, P)
    crow = reg(105, P)
    colsA = m(56)
    colsB = m(124)
    bfb = m(8)
    gqk = m(2)
    L = land("rows")
    vec = lambda v: v.rearrange("o (c p) -> (o c) p", p=P)
    ra = 0
    where = {}
    for name in ("g_mix", "g_ffn", "norm_pre_mix_2", "norm_pre_ffn_2", "b_dw", "g_conv_ln", "b_conv_ln"):
        v = vec(a[name])
        where[name] = ra
        L.dma(act, rows_a[ra:ra + v.shape[0], :], v)
        ra += v.shape[0]
    where["conv_w"] = ra
    L.dma(act, rows_a[ra:ra + 12, :], a["conv_w_2"].rearrange("o w (c p) -> (o w c) p", p=P))
    ra += 12
    assert ra == 56
    L.dma(act, crow[0:8, :], a["c_2"].rearrange("o (c p) -> (o c) p", p=P))
    L.dma(act, crow[8:16, :], a["c_ctx_2"].rearrange("(c p) -> c p", p=P))
    t_rows = L.dma(act, rows_b[0:124, :], a["w_dw"].rearrange("o w (c p) -> (o w c) p", p=P))
    act.wait(zt)
    L = land("small")
    L.dma(act, bfb, a["b_forget"].to_broadcast([P, 8]))
    L.dma(act, gqk[0:64, 0:1], a["g_q"].rearrange("o d -> d o"))
    t_small = L.dma(act, gqk[0:64, 1:2], a["g_k"].rearrange("o d -> d o"))
    dve.wait(zt)
    t_g1 = dve.do(lambda e: e.memset(gqk[64:66, :], 1.0))
    dve.wait(t_small)
    t_gq = dve.do(lambda e: e.tensor_scalar(gqk[0:64, 0:1], gqk[0:64, 0:1], 0.125, None, ALU.mult))
    pe.wait(t_rows, *consts)
    act.wait(t_rows)
    b = bank()
    tr(ps[:, b, 0:56], rows_a[0:56, :], ident[0:56, 0:56], False)
    tr(ps[:, b, 64:188], rows_b[0:124, :], ident[0:124, 0:124], False)
    t = tr(ps[:, b, 192:208], crow[0:16, :], ident[0:16, 0:16], True)
    dve.wait(t)
    dve.do(lambda e: e.tensor_copy(colsA, ps[:, b, 0:56]))
    t_cols = dve.do(lambda e: e.tensor_copy(colsB, ps[:, b, 64:188]))
    cf = m(8, 2)
    act.wait(t_cols)
    t = act.do(lambda e: e.activation(cf.rearrange("p k r -> p r k"),
                                      ps[:, b, 192:208].rearrange("p (r k) -> p r k", r=2), ACT.Silu))
    bfree[b] = t
    cv = cvR[:, 0:32].rearrange("p (k r) -> p k r", r=4)
    act.wait(t)
    t = act.do(lambda e: e.activation(cv[:, :, 0:2], cf, ACT.Copy))
    dve.wait(t)
    t_cv = dve.do(lambda e: e.tensor_tensor(cv[:, :, 2:4], cf, cv[:, :, 0:2].bitcast(F32), ALU.subtract))
    col = lambda name, i: colsA[:, where[name] + i:where[name] + i + 1]
    act.wait(t_cols, t_gq, t_g1)

    ss4 = m(8, 4)
    ss = m(8)
    inv = m(8)

    def rms_inv(n0, n1, size, waits):
        dve.wait(*waits)
        t = dve.do(lambda e: e.tensor_scalar(ss[:, n0:n1], ss[:, n0:n1], 1.0 / size, EPS, ALU.mult, ALU.add))
        pool.wait(t, t_nhalf)
        return pool.do(lambda e: e.tensor_tensor(inv[:, n0:n1], ss[:, n0:n1], nhalf[:, 0:n1 - n0], ALU.pow))

    def xhat(src, scratch, i0, i1, t_inv):
        dve.wait(t_inv)
        for i in range(i0, i1):
            t = dve.do(lambda e: e.tensor_scalar(scratch(i), src(i), inv[:, i:i + 1], None, ALU.mult))
        return t

    def turned(scratch, dst, i0, i1, gains, biases, temps, t_xh, dst_free, gain_t=None):
        done = []
        pe.wait(t_xh)
        n = (i1 - i0) * P
        for f in range(8):
            b = bank()
            for i in range(i0, i1):
                t = tr(ps[:, b, (i - i0) * P:(i - i0 + 1) * P], scratch(i)[:, f * P:(f + 1) * P], ident, i == i1 - 1)
            d = at(dst, slice(None), f, slice(i0 * P, i1 * P))
            if biases is None:
                bfree[b] = split_psum(ps[:, b, 0:n], d, gains(f), [t, gain_t], dst_free)
                done.append(bfree[b])
            else:
                k = f % len(temps)
                v = temps[k][0][:, 0:n]
                dve.wait(t, gain_t, temps[k][1])
                t = dve.do(lambda e: e.tensor_scalar(v, ps[:, b, 0:n], gains(f), biases(f), ALU.mult, ALU.add))
                bfree[b] = t
                temps[k][1] = split(v, d, [t], dst_free)
                done.append(temps[k][1])
        return done

    HT = pair(0, 32, 8, 1024)
    t_ss = []
    for i in range(8):
        act.wait(xa_t[i], t_ss[i - 2] if i > 1 else None)
        t_ss.append(act.do(lambda e: e.activation(reg(96 + 4 * (i % 2), D), xa(i), ACT.Square,
                                                  accum_out=ss[:, i:i + 1])))
    HT_done = []
    for i0 in (0, 4):
        t_inv = rms_inv(i0, i0 + 4, 1024.0, t_ss[i0:i0 + 4])
        t_xh = xhat(xa, xa, i0, i0 + 4, t_inv)
        HT_done.append(turned(xa, HT, i0, i0 + 4, lambda f: col("g_mix", f), None, None, t_xh, None))
    xa_last = pe_now()

    CA = reg(121, 4, 1024)
    CO = reg(137, 4, 1024)
    t_glu = []
    for mt in range(4):
        c = CA[:, mt, :]
        s, (wg,) = ws.get()
        for hf in range(2):
            pe.wait(HT_done[hf])
            h_ = slice(hf * 512, (hf + 1) * 512)
            b = bank()
            for k in range(8):
                t = mm3(ps[:, b, :], at(wg, slice(None), k), at(HT, slice(None), k, h_), k == 0, k == 7, k == 7)
            act.wait(t)
            t1 = act.do(lambda e: e.activation(c[:, h_], ps[:, b, :], ACT.Sigmoid))
            bfree[b] = t1
        ws.done(s, t)
        s, (wa,) = ws.get()
        for hf in range(2):
            h_ = slice(hf * 512, (hf + 1) * 512)
            b = bank()
            for k in range(8):
                t = mm3(ps[:, b, :], at(wa, slice(None), k), at(HT, slice(None), k, h_), k == 0, k == 7, k == 7)
            dve.wait(t1, t)
            t2 = dve.do(lambda e: e.tensor_tensor(c[:, h_], ps[:, b, :], c[:, h_], ALU.mult))
            bfree[b] = t2
            t_glu.append(t2)
        ws.done(s, t)

    conv = {"n": 0, "t": [None] * 4}

    def conv_steps(n):
        for _ in range(n):
            k = conv["n"]
            if k >= 124:
                return
            conv["n"] += 1
            tap, ct = k // 4, k % 4
            w, sh = 30 - tap, tap
            wc = colsB[:, w * 4 + ct:w * 4 + ct + 1]
            if tap == 0:
                dve.wait(*t_glu)
                t = dve.do(lambda e: e.tensor_scalar(CO[:, ct, :], CA[:, ct, :], wc, col("b_dw", ct), ALU.mult,
                                                     ALU.add))
            else:
                dve.wait(conv["t"][ct])
                t = dve.do(lambda e: e.scalar_tensor_tensor(out=CO[:, ct, sh:], in0=CA[:, ct, 0:S - sh], scalar=wc,
                                                            in1=CO[:, ct, sh:], op0=ALU.mult, op1=ALU.add))
            conv["t"][ct] = t

    zf, zb, lf, Lp, cc, ncc = m(64), m(64), m(64), m(8, 8), m(8, 8), m(8, 8)
    s, (wf,) = ws.get()
    pe.wait(*HT_done)
    b = bank()
    for i in range(NT):
        for k in range(8):
            t = mm3(ps[:, b, i * 8:i * 8 + 8], at(HT, slice(None), k, slice(i * P, (i + 1) * P)),
                    at(wf, slice(None), k), k == 0, k == 7, i == 7 and k == 7)
    ws.done(s, t)
    dve.wait(t, t_small)
    t = dve.do(lambda e: e.tensor_tensor(zf.rearrange("p (a b) -> p a b", a=8),
                                         ps[:, b, 0:64].rearrange("p (a b) -> p a b", a=8),
                                         bfb.rearrange("p (o b) -> p o b", o=1).to_broadcast([P, 8, 8]), ALU.add))
    bfree[b] = t
    dve.wait(t)
    t = dve.do(lambda e: e.tensor_scalar(zb, zf, -1.0, None, ALU.mult))
    dve.wait(t)
    t = dve.do(lambda e: e.tensor_tensor(zb, zb, zf, ALU.max))
    act.wait(t)
    t = act.do(lambda e: e.activation(zb, zb, ACT.Exp, scale=-1.0))
    act.wait(t)
    t = act.do(lambda e: e.activation(zb, zb, ACT.Ln, bias=1.0))
    dve.wait(t)
    t = dve.do(lambda e: e.scalar_tensor_tensor(out=lf, in0=zf, scalar=0.0, in1=zb, op0=ALU.min, op1=ALU.subtract))
    dve.wait(t)
    for i in range(1, 8):
        t = dve.do(lambda e: e.tensor_tensor(Lp[:, i, :], Lp[:, i - 1, :], lf[:, (i - 1) * 8:i * 8], ALU.add))
        dve.wait(t)
    t_lp = t

    QT = reg(64, 2, 1024)
    KT = reg(72, 2, 1024)
    VV = reg(80, 8, P)
    QK = [reg(84 + 1.03125 * j, 4, 66) for j in range(2)]
    SQ = [reg(86.0625 + 1 * j, 256) for j in range(2)]
    OM = [reg(88.0625, P), m(P)]
    PB = [reg(89 + 4 * j, 1024) for j in range(2)]
    PT = [reg(97 + 4 * j, 8, P) for j in range(2)]
    OT = reg(105, 4, 1024)
    st4 = [m(4), m(4)]
    iv4 = [m(4), m(4)]
    nmax = [m(1), m(1)]
    rsum = [m(1), m(1)]
    rinv = [m(1), m(1)]
    pool.wait(xa_last)
    for j in range(2):
        pool.do(lambda e: e.memset(QK[j][:, 0:2, 64:65], 1.0))
        t_aug = pool.do(lambda e: e.memset(QK[j][:, 2:4, 65:66], 1.0))
    qk_free = [None, None]
    sq_rd = [None, None]
    att_done = [xa_last]
    OT_done = []
    pb_free, pt_free, om_free = [None, None], [None, None], [None, None]
    for g in range(4):
        for q in range(3):
            ws.add([(8, P, w_in[:, :, 1024 + q * 512 + g * P:1024 + q * 512 + (g + 1) * P])])
    ws.load()

    def cumulate():
        pe.wait(t_lp)
        b = bank()
        mm(ps[:, b, 0:64], ones, Lp.rearrange("p a b -> p (a b)"), True, False, False)
        t = mm(ps[:, b, 0:64], tri, lf, False, True, True)
        dve.wait(t)
        dve.do(lambda e: e.tensor_copy(cc.rearrange("p a b -> p (a b)"), ps[:, b, 0:64]))
        t_cc = dve.do(lambda e: e.tensor_scalar(ncc.rearrange("p a b -> p (a b)"), ps[:, b, 0:64], -1.0, None,
                                                ALU.mult))
        bfree[b] = t_cc
        pool.wait(t_cc)

    def project(g):
        slots = [ws.get(2 - q)[0] for q in range(3)]
        assert sorted(slots) == [0, 1, 2]
        w = lambda k: (wparts[:, :, k * P:(k + 1) * P], wparts[:, :, 1024 + k * P:1024 + (k + 1) * P])
        seg = dict(enumerate(slots))
        tt = []
        for i in range(NT):
            b = bank()
            for k in range(8):
                t = mm3(ps[:, b, 0:384], at(HT, slice(None), k, slice(i * P, (i + 1) * P)), w(k), k == 0, k == 7,
                        k == 7)
            if i == NT - 1:
                for s_ in range(3):
                    ws.done(s_, t)
            if g == 0 and i == 0:
                cumulate()
            j = i % 2
            if i >= 2:
                turn_qk(*tt[i - 2])
            pq, pk, pv_ = (ps[:, b, seg[q] * P:(seg[q] + 1) * P] for q in range(3))
            act.wait(t, sq_rd[j], xa_last)
            act.do(lambda e: e.activation(SQ[j][:, 0:P], pq, ACT.Square))
            t1 = act.do(lambda e: e.activation(SQ[j][:, P:2 * P], pk, ACT.Square))
            act.wait(*att_done)
            tv = act.do(lambda e: e.copy(VV[:, i, :], pv_))
            dve.wait(t1)
            t2 = dve.do(lambda e: e.tensor_reduce(st4[j], SQ[j].rearrange("p (h d) -> p h d", h=4), AX.X, ALU.add))
            sq_rd[j] = t2
            dve.wait(t2)
            t2 = dve.do(lambda e: e.tensor_scalar(st4[j], st4[j], 1.0 / 64, EPS, ALU.mult, ALU.add))
            pool.wait(t2)
            t3 = pool.do(lambda e: e.tensor_tensor(iv4[j], st4[j], nhalf[:, 0:4], ALU.pow))
            pool.wait(qk_free[j], t_aug)
            hs = lambda x: x[:, i, 2 * g:2 * g + 2].rearrange("p (h o) -> p h o", o=1)
            pool.do(lambda e: e.tensor_copy(QK[j][:, 0:2, 65:66], hs(cc)))
            t4 = pool.do(lambda e: e.tensor_copy(QK[j][:, 2:4, 64:65], hs(ncc)))
            dve.wait(t3, qk_free[j], tv)
            for q, src in ((0, pq), (1, pk)):
                t5 = dve.do(lambda e: e.tensor_tensor(
                    QK[j][:, 2 * q:2 * q + 2, 0:64], src.rearrange("p (h d) -> p h d", h=2),
                    iv4[j][:, 2 * q:2 * q + 2].rearrange("p (h o) -> p h o", o=1).to_broadcast([P, 2, 64]),
                    ALU.mult))
            bfree[b] = [t5, tv]
            tt.append((i, j, t4, t5, tv))
            conv_steps(2)
        turn_qk(*tt[6])
        return turn_qk(*tt[7])

    def turn_qk(i, j, t4, t5, tv):
        pe.wait(t4, t5)
        b = bank()
        for q in range(4):
            t = tr(ps[0:66, b, q * P:(q + 1) * P], QK[j][:, q, :], ident, q == 3)
        qk_free[j] = t
        sl = slice(i * P, (i + 1) * P)
        v = ps[0:66, b, :].rearrange("p (q n) -> p q n", q=4)
        act.wait(t, *att_done)
        act.do(lambda e: e.activation(QT[0:66, :, sl], v[:, 0:2, :], ACT.Copy, scale=gqk[0:66, 0:1]))
        ta = act.do(lambda e: e.activation(KT[0:66, :, sl], v[:, 2:4, :], ACT.Copy, scale=gqk[0:66, 1:2]))
        bfree[b] = ta
        return [ta, tv]

    def attention(g, ready):
        units = [(i, h) for i in range(NT) for h in range(2)]
        st = {}

        def qk(u):
            i, h = units[u]
            kw = (i + 1) * P
            b0 = 0 if u % 2 == 0 else 2
            pe.wait(bfree[b0], bfree[b0 + 1])
            for c0 in range(0, kw, 512):
                n = min(512, kw - c0)
                diag = c0 + n == kw
                o = ps[:, b0 + c0 // 512, 0:n]
                t = mm(o, QT[0:66, h, i * P:(i + 1) * P], KT[0:66, h, c0:c0 + n], True, not diag, False)
                if diag:
                    t = mm(o[:, n - P:n], ident, mask, False, True, True)
            j = u % 2
            sv = ps[:, b0:b0 + 2, :].rearrange("p a b -> p (a b)")[:, 0:kw]
            dve.wait(t)
            t1 = dve.do(lambda e: e.tensor_reduce(nmax[j], sv, AX.X, ALU.max, negate=True))
            act.wait(t1, pb_free[j])
            t2 = act.do(lambda e: e.activation(PB[j][:, 0:kw], sv, ACT.Exp, bias=nmax[j], accum_out=rsum[j]))
            bfree[b0] = bfree[b0 + 1] = t2
            st[u] = t2

        def turn_p(u):
            i, h = units[u]
            j = u % 2
            pe.wait(st[u])
            ts = []
            for c0 in range(0, i + 1, 4):
                n = min(4, i + 1 - c0)
                b = 4 + (c0 // 4)
                pe.wait(bfree[b])
                for c in range(n):
                    t = tr(ps[:, b, c * P:(c + 1) * P], PB[j][:, (c0 + c) * P:(c0 + c + 1) * P], ident, c == n - 1)
                q = act if c0 == 0 else dve
                q.wait(t, pt_free[j])
                o, i_ = PT[j][:, c0:c0 + n, :].rearrange("p a b -> p (a b)"), ps[:, b, 0:n * P]
                bfree[b] = (act.do(lambda e: e.copy(o, i_)) if c0 == 0 else
                            dve.do(lambda e: e.tensor_copy(o, i_)))
                ts.append(bfree[b])
            pb_free[j] = t
            dve.wait(st[u])
            st[("r", u)] = dve.do(lambda e: e.reciprocal(rinv[j], rsum[j]))
            st[u] = (st[u], ts)

        def pv(u):
            i, h = units[u]
            j = u % 2
            te, ts = st[u]
            pe.wait(*ts)
            pe.wait(bfree[6])
            for c in range(i + 1):
                t = mm(ps[:, 6, 0:64], PT[j][:, c, :], VV[:, c, h * 64:(h + 1) * 64], c == 0, c == i, c == i)
            pt_free[j] = t
            dve.wait(t, st[("r", u)], om_free[i % 2])
            bfree[6] = dve.do(lambda e: e.tensor_scalar(OM[i % 2][:, h * 64:(h + 1) * 64], ps[:, 6, 0:64], rinv[j],
                                                        None, ALU.mult))
            if h == 1:
                st[("o", i)] = bfree[6]

        def turn_o(i):
            pe.wait(st[("o", i)], bfree[7])
            t = tr(ps[:, 7, 0:P], OM[i % 2], ident, True)
            om_free[i % 2] = t
            act.wait(t)
            bfree[7] = act.do(lambda e: e.copy(OT[:, g, i * P:(i + 1) * P], ps[:, 7, 0:P]))
            OT_done.append(bfree[7])

        pe.wait(*ready)
        n = len(units)
        for u in range(n + 2):
            if u < n:
                qk(u)
            if u >= 2:
                pv(u - 2)
            if 1 <= u <= n:
                turn_p(u - 1)
            if u >= 4 and u % 2 == 0:
                turn_o((u - 4) // 2)
            if u % 2:
                conv_steps(1)
        turn_o(NT - 1)
        att_done[:] = [pe_now()]

    for g in range(4):
        attention(g, project(g))
    att1_last = pe_now()

    GA = reg(64, 8, 1024)
    wco = a["w_conv_out"][0].rearrange("(c p) n -> p c n", p=P)
    wao = a["w_attn_out"][0].rearrange("(c p) n -> p c n", p=P)
    for mt in range(8):
        ws.add([(8, P, w_in[:, :, 2568 + mt * P:2568 + (mt + 1) * P])])
    for mt in range(8):
        cs = slice(mt * P, (mt + 1) * P)
        ws.add([(8, P, w_in[:, :, 3592 + mt * P:3592 + (mt + 1) * P])],
               [(4, P, wco[:, :, cs]), (4, P, wao[:, :, cs])])
    ws.load()
    GA_done = []
    for mt in range(8):
        s, (w,) = ws.get()
        for hf in range(2):
            h_ = slice(hf * 512, (hf + 1) * 512)
            b = bank()
            for k in range(8):
                t = mm3(ps[:, b, :], at(w, slice(None), k), at(HT, slice(None), k, h_), k == 0, k == 7, k == 7)
            act.wait(t, att1_last)
            bfree[b] = act.do(lambda e: e.activation(GA[:, mt, h_], ps[:, b, :], ACT.Sigmoid))
            GA_done.append(bfree[b])
        ws.done(s, t)
        conv_steps(7)
        if mt == 5:
            conv_steps(200)
            t_conv = conv["t"]
            mean = []
            for hf in range(2):
                b = bank()
                pe.wait(*t_conv)
                for ct in range(4):
                    t = mm(ps[:, b, :], ones, CO[:, ct, hf * 512:(hf + 1) * 512], ct == 0, ct == 3, ct == 3)
                dve.wait(t)
                for ct in range(4):
                    v = CO[:, ct, hf * 512:(hf + 1) * 512]
                    tc = dve.do(lambda e: e.scalar_tensor_tensor(out=v, in0=ps[:, b, :], scalar=-1.0 / 512, in1=v,
                                                                 op0=ALU.mult, op1=ALU.add))
                    q = CA[:, ct, hf * 512:(hf + 1) * 512]
                    act.wait(tc)
                    tq = act.do(lambda e: e.activation(q, v, ACT.Square))
                bfree[b] = tc
                mean.append(tq)
    rs = reg(96, 1024)
    CN = (lambda ct: view(F32R, 100 if ct == 0 else 193 + 4 * (ct - 1) if ct < 3 else 165, [1024]),
          lambda ct: view(F32R, 137 + 4 * ct, [1024]))
    CN_done = []
    OTh, OTl = view(F32R, 121, [4, 1024]), view(F32R, 105, [4, 1024])
    t_cn = []
    for hf in range(2):
        b = bank()
        pe.wait(mean[hf])
        for ct in range(4):
            t = mm(ps[:, b, :], ones, CA[:, ct, hf * 512:(hf + 1) * 512], ct == 0, ct == 3, ct == 3)
        r = rs[:, hf * 512:(hf + 1) * 512]
        dve.wait(t, att1_last)
        t1 = dve.do(lambda e: e.tensor_scalar(r, ps[:, b, :], 1.0 / 512, EPS, ALU.mult, ALU.add))
        bfree[b] = t1
        act.wait(t1)
        t1 = act.do(lambda e: e.activation(r, r, ACT.Sqrt))
        dve.wait(t1)
        t1 = dve.do(lambda e: e.reciprocal(r, r))
        dve.wait(t1)
        for ct in range(4):
            v = CO[:, ct, hf * 512:(hf + 1) * 512]
            tm = dve.do(lambda e: e.tensor_tensor(v, v, r, ALU.mult))
            t_cn.append((ct, hf, v, tm))
    ln_last = pe_now()
    OS_done = []
    for c in range(4):
        OS_done.append(split(OT[:, c, :], (OTh[:, c, :], OTl[:, c, :]), [*OT_done, ln_last]))
    for ct, hf, v, tm in t_cn:
        act.wait(tm)
        t = act.do(lambda e: e.activation(v, v, ACT.Silu, bias=col("b_conv_ln", ct), scale=col("g_conv_ln", ct)))
        h_ = slice(hf * 512, (hf + 1) * 512)
        CN_done.append(split(v, (CN[0](ct)[:, h_], CN[1](ct)[:, h_]), [t, att1_last]))

    sg = [reg(96 + 2 * j, 512) for j in range(2)]
    sg_free = [tm, tm]
    n = 0
    M_done = []
    for mt in range(8):
        s0, (wb_,) = ws.get()
        gbs = []
        for hf in range(2):
            h_ = slice(hf * 512, (hf + 1) * 512)
            b = bank()
            for k in range(8):
                t = mm3(ps[:, b, :], at(wb_, slice(None), k), at(HT, slice(None), k, h_), k == 0, k == 7, k == 7)
            act.wait(t, sg_free[hf])
            tb = act.do(lambda e: e.activation(sg[hf], ps[:, b, :], ACT.Sigmoid))
            bfree[b] = tb
            gbs.append(tb)
        ws.done(s0, t)
        s1, (wc_, wa_) = ws.get()
        for hf in range(2):
            h_ = slice(hf * 512, (hf + 1) * 512)
            b2, b3 = bank(), bank()
            pe.wait(*CN_done, *OS_done)
            for k in range(4):
                t2 = mm3(ps[:, b2, :], at(wc_, slice(None), k), (CN[0](k)[:, h_], CN[1](k)[:, h_]), k == 0, k == 3,
                         k == 3)
            for k in range(4):
                t3 = mm3(ps[:, b3, :], at(wa_, slice(None), k), (OTh[:, k, h_], OTl[:, k, h_]), k == 0, k == 3,
                         k == 3)
            ga = GA[:, mt, h_]
            dve.wait(t2, *GA_done)
            t4 = dve.do(lambda e: e.tensor_tensor(ga, ps[:, b2, :], ga, ALU.mult))
            bfree[b2] = t4
            dve.wait(gbs[hf], t3)
            t5 = dve.do(lambda e: e.tensor_tensor(sg[hf], ps[:, b3, :], sg[hf], ALU.mult))
            bfree[b3] = t5
            dve.wait(t4, t5)
            t6 = dve.do(lambda e: e.tensor_tensor(ga, ga, sg[hf], ALU.add))
            sg_free[hf] = t6
            M_done.append(t6)
        ws.done(s1, t3)
    merge_last = pe_now()

    X = reg(105, 8, 1024)
    pool.wait(merge_last)
    X_in = [land(f"xr{i}").dma(pool, X[:, i, :], x_in[i * P:(i + 1) * P, :]) for i in range(8)]
    MS = pair(0, 32, 8, 1024)
    wout = a["w_out"][0].rearrange("(c p) n -> p c n", p=P)
    for q in range(4):
        for k in (0, 4):
            ws.add([(4, 256, wout[:, k:k + 4, q * 256:(q + 1) * 256])])
    ws.make(1)
    MS_done = [split(GA[:, k, :], at(MS, slice(None), k), [M_done[2 * k + 1]], merge_last) for k in range(8)]

    def residual(q, i, b, waits, square):
        qs = slice(q * 256, (q + 1) * 256)
        dve.wait(*waits)
        bfree[b] = dve.do(lambda e: e.tensor_tensor(X[:, i, qs], ps[:, b, 0:256], X[:, i, qs], ALU.add))
        if square:
            act.wait(bfree[b], jk_t[i % 2])
            jk_t[i % 2] = act.do(lambda e: e.activation(jk[i % 2], X[:, i, qs], ACT.Square,
                                                        accum_out=ss4[:, i, q:q + 1]))
            return jk_t[i % 2]

    jk, jk_t = [reg(165, 256), reg(166, 256)], [None, None]
    X_t = {}
    for q in range(4):
        s0, (w0,) = ws.get()
        s1, (w1,) = ws.get(1)
        for i in range(NT):
            b = bank()
            for k in range(8):
                if q == 0 and i == 0:
                    pe.wait(MS_done[k])
                w = at(w0, slice(None), k) if k < 4 else at(w1, slice(None), k - 4)
                t = mm3(ps[:, b, 0:256], at(MS, slice(None), k, slice(i * P, (i + 1) * P)), w, k == 0, k == 7,
                        k == 7)
            if i == NT - 1:
                ws.done(s0, t)
                ws.done(s1, t)
            X_t[i] = residual(q, i, b, [t, X_in[i]], True)
            if i == NT - 1:
                ws.make(0)

    def norm_start(scratch, free):
        out_ = []
        for i0 in (0, 4):
            for i in range(i0, i0 + 4):
                dve.wait(X_t[i])
            t = dve.do(lambda e: e.tensor_reduce(ss[:, i0:i0 + 4], ss4[:, i0:i0 + 4, :], AX.X, ALU.add))
            t_inv = rms_inv(i0, i0 + 4, 1024.0, [t])
            dve.wait(free)
            out_.append(xhat(lambda i: X[:, i, :], scratch, i0, i0 + 4, t_inv))
        return out_

    wfi = a["w_ffn_in"][0].rearrange("(c p) n -> p c n", p=P)
    wfo = a["w_ffn_out"][0].rearrange("(c p) n -> p c n", p=P)
    wada = a["w_ada_2"][0].rearrange("(c p) n -> p c n", p=P)
    groups = [range(0, 6), range(6, 12), range(12, 17), range(17, 22)]
    nada = 0
    for fs in groups:
        for f in fs:
            ws.add([(8, P, wfi[:, :, f * P:(f + 1) * P])], [(8, P, wfi[:, :, FF + f * P:FF + (f + 1) * P])])
            for _ in range(2 if f in (20, 21) else 1):
                for k in (0, 4):
                    ws.add([(4, 256, wada[:, k:k + 4, nada * 256:(nada + 1) * 256])])
                nada += 1
        for q in range(4):
            qs = slice(q * 256, (q + 1) * 256)
            f0, f1 = fs[0], fs[-1] + 1
            ws.add([(3, 256, wfo[:, f0:f0 + 3, qs])], [(f1 - f0 - 3, 256, wfo[:, f0 + 3:f1, qs])])
    assert nada == 24
    ws.load()
    H2 = pair(0, 32, 8, 1024)
    scr = lambda i: reg(64 + 4 * i, D)
    t_xh = norm_start(scr, None)
    H2_free = pe_now()
    H2_done = [turned(scr, H2, i0, i0 + 4, lambda f: col("g_ffn", f), None, None, t_xh[i0 // 4], H2_free)
               for i0 in (0, 4)]
    scr_last = pe_now()

    slots6 = [64, 72, 80, 88, 96, 137]
    ft = [[reg(145 + 2 * j, 512), None] for j in range(4)]
    nt_ = [0]
    arow = [reg(104, 256), reg(167, 256)]
    arow_free = [None, None]
    an = [0]
    mod_t = []

    def ada():
        n_ = an[0]
        an[0] += 1
        j = n_ % 2
        s0, (w0,) = ws.get()
        s1, (w1,) = ws.get(1)
        b = bank()
        pe.wait(t_cv)
        for k in range(8):
            w = at(w0, slice(None), k) if k < 4 else at(w1, slice(None), k - 4)
            mm(ps[0:4, b, 0:256], cv[:, k, 0:4], w[0], k == 0, False, False)
            t = mm(ps[0:2, b, 0:256], cv[:, k, 0:2], w[1], False, k == 7, k == 7)
        ws.done(s0, t)
        ws.done(s1, t)
        dve.wait(t, arow_free[j])
        t = dve.do(lambda e: e.tensor_copy(arow[j][0:4, :], ps[0:4, b, 0:256]))
        bfree[b] = t
        pool.wait(t)
        arow_free[j] = land(f"mod{j}").dma(pool, mod_dram[:, n_ * 256:(n_ + 1) * 256], arow[j][0:4, :])
        mod_t[:] = (mod_t + [arow_free[j]])[-2:]

    for gi, fs in enumerate(groups):
        A = [pair(slots6[j], slots6[j] + 4, 1024) for j in range(len(fs))]
        a_free = pe_now()
        A_done = []
        for fi, f in enumerate(fs):
            s0, (wg,) = ws.get()
            vs = []
            for hf in range(2):
                pe.wait(H2_done[hf])
                h_ = slice(hf * 512, (hf + 1) * 512)
                v = ft[nt_[0] % 4]
                nt_[0] += 1
                b = bank()
                for k in range(8):
                    t = mm3(ps[:, b, :], at(wg, slice(None), k), at(H2, slice(None), k, h_), k == 0, k == 7, k == 7)
                act.wait(t, v[1])
                t1 = act.do(lambda e: e.activation(v[0], ps[:, b, :], ACT.Silu))
                bfree[b] = t1
                vs.append((v, t1, h_))
            ws.done(s0, t)
            s1, (wu,) = ws.get()
            for v, t1, h_ in vs:
                b = bank()
                for k in range(8):
                    t = mm3(ps[:, b, :], at(wu, slice(None), k), at(H2, slice(None), k, h_), k == 0, k == 7, k == 7)
                dve.wait(t1, t)
                t2 = dve.do(lambda e: e.tensor_tensor(v[0], ps[:, b, :], v[0], ALU.mult))
                bfree[b] = t2
                v[1] = split(v[0], (A[fi][0][:, h_], A[fi][1][:, h_]), [t2], a_free)
                A_done.append(v[1])
            ws.done(s1, t)
            for _ in range(2 if f in (20, 21) else 1):
                ada()
        last = gi == len(groups) - 1
        nf = len(fs)
        for q in range(4):
            s0, (w0,) = ws.get()
            s1, (w1,) = ws.get(1)
            pe.wait(*A_done)
            for i in range(NT):
                b = bank()
                for f in range(nf):
                    w = at(w0, slice(None), f) if f < 3 else at(w1, slice(None), f - 3)
                    t = mm3(ps[:, b, 0:256], (A[f][0][:, i * P:(i + 1) * P], A[f][1][:, i * P:(i + 1) * P]), w,
                            f == 0, f == nf - 1, f == nf - 1)
                if i == NT - 1:
                    ws.done(s0, t)
                    ws.done(s1, t)
                X_t[i] = residual(q, i, b, [t, X_t[i] if gi == 0 and q == 0 else None], last)
                if i == NT - 1:
                    ws.make(0)
    ffn_last = pe_now()

    w2 = a["w_in_2"][0].rearrange("(c p) n -> p c n", p=P)
    kspec = lambda mt: [(8, P, w2[:, :, 512 + mt * P:512 + (mt + 1) * P])]
    vspec = lambda q: ([(4, 256, w2[:, 0:4, 1024 + q * 256:1024 + (q + 1) * 256])],
                       [(4, 256, w2[:, 4:8, 1024 + q * 256:1024 + (q + 1) * 256])])
    ws.add(*[kspec(mt) for mt in range(4)], *vspec(0), *vspec(1))
    ws.add(*[[(8, P, w2[:, :, mt * P:(mt + 1) * P])] for mt in range(4)], *[kspec(mt) for mt in range(4)],
           *vspec(0), *vspec(1))
    for ct in range(4):
        for o in (2048, 2560, 1536):
            ws.add([(8, P, w2[:, :, o + ct * P:o + (ct + 1) * P])])
    ws.load()

    mrow = [reg(104, P), reg(104.5, P), reg(167, P)]
    modT = m(48)
    mg, mgc, mg2 = m(8), m(8), m(8)
    pool.wait(*mod_t, ffn_last)
    lm = land("mrow")
    for r, (hi, lo) in enumerate(((0, 2), (1, 3))):
        for part, row in ((mrow[0], hi), (mrow[1], lo)):
            for n_, (d0, c0) in enumerate(((0, 0), (16, 3))[:2 - r]):
                src = mod_dram[row:row + 1, c0 * D:(c0 + 2) * D].rearrange("o (c p) -> (o c) p", p=P)
                lm.dma(pool, part[32 * r + d0:32 * r + d0 + 16, :], src)
    for d0, c0 in ((0, 0), (16, 3), (32, 0)):
        t = lm.dma(pool, mrow[2][d0:d0 + 16, :],
                   a["b_ada_2"][:, c0 * D:(c0 + 2) * D].rearrange("o (c p) -> (o c) p", p=P))
    dve.wait(t)
    t = dve.do(lambda e: e.tensor_tensor(mrow[0][0:48, :], mrow[0][0:48, :], mrow[1][0:48, :], ALU.add))
    dve.wait(t)
    t = dve.do(lambda e: e.tensor_tensor(mrow[0][0:48, :], mrow[0][0:48, :], mrow[2][0:48, :], ALU.add))
    pe.wait(t)
    b = bank()
    t = tr(ps[:, b, 0:48], mrow[0][0:48, :], ident[0:48, 0:48], True)
    dve.wait(t)
    t = dve.do(lambda e: e.tensor_copy(modT, ps[:, b, 0:48]))
    bfree[b] = t
    dve.wait(t)

    def gain(dst, name, c0):
        g0 = colsA[:, where[name]:where[name] + 8]
        return dve.do(lambda e: e.scalar_tensor_tensor(out=dst, in0=modT[:, c0:c0 + 8], scalar=1.0, in1=g0,
                                                       op0=ALU.add, op1=ALU.mult))

    gain(mg, "norm_pre_mix_2", 8)
    gain(mgc, "norm_pre_mix_2", 40)
    t_mg = gain(mg2, "norm_pre_ffn_2", 24)
    shift = lambda c0, f: modT[:, c0 + f:c0 + f + 1]

    iC = [m(1), m(1)]
    xc = [reg(96 + 4 * j, D) for j in range(2)]
    cin = a["ctx_2"].rearrange("o s d -> (o s) d")
    XC = pair(137, 145, 8, CTX)
    t_scC = []
    for j in range(2):
        tx = land(f"xc{j}").dma(pool, xc[j], cin[j * P:(j + 1) * P, :])
        act.wait(tx, ffn_last)
        t = act.do(lambda e: e.activation(reg(193 + 4 * j, D), xc[j], ACT.Square, accum_out=iC[j]))
        dve.wait(t)
        t = dve.do(lambda e: e.tensor_scalar(iC[j], iC[j], 1.0 / D, EPS, ALU.mult, ALU.add))
        pool.wait(t)
        t = pool.do(lambda e: e.tensor_tensor(iC[j], iC[j], nhalf[:, 0:1], ALU.pow))
        dve.wait(t)
        t_scC.append(dve.do(lambda e: e.tensor_scalar(xc[j], xc[j], iC[j], None, ALU.mult)))
    tmps = [[reg(193, 512), t_scC[1]], [reg(195, 512), t_scC[1]]]
    XC_done = turned(lambda i: xc[i], XC, 0, 2, lambda f: mgc[:, f:f + 1], lambda f: shift(32, f), tmps, t_scC,
                     ffn_last, t_mg)
    scr3 = lambda i: reg(64 + 4 * i, D)
    t_xh = norm_start(scr3, ffn_last)
    K2c = reg(193, 4, CTX)
    V2c = reg(197, 2, 512)
    kc_done = []
    for mt in range(4):
        s, (w,) = ws.get()
        pe.wait(*XC_done)
        b = bank()
        for k in range(8):
            t = mm3(ps[:, b, 0:CTX], at(w, slice(None), k), at(XC, slice(None), k), k == 0, k == 7, k == 7)
        ws.done(s, t)
        act.wait(t, *XC_done)
        bfree[b] = act.do(lambda e: e.copy(K2c[:, mt, :], ps[:, b, 0:CTX]))
        kc_done.append(bfree[b])
    for q in range(2):
        s0, (w0,) = ws.get()
        s1, (w1,) = ws.get(1)
        for i in range(2):
            b = bank()
            for k in range(8):
                w = at(w0, slice(None), k) if k < 4 else at(w1, slice(None), k - 4)
                t = mm3(ps[:, b, 0:256], at(XC, slice(None), k, slice(i * P, (i + 1) * P)), w, k == 0, k == 7, k == 7)
            act.wait(t)
            bfree[b] = act.do(lambda e: e.copy(V2c[:, i, q * 256:(q + 1) * 256], ps[:, b, 0:256]))
            kc_done.append(bfree[b])
        ws.done(s0, t)
        ws.done(s1, t)
    xc_last = pe_now()

    XN = pair(0, 32, 8, 1024)
    tmps = [[reg(96 + 2 * j, 512), xc_last] for j in range(4)]
    XN_done = [turned(scr3, XN, i0, i0 + 4, lambda f: mg[:, f:f + 1], lambda f: shift(0, f), tmps, t_xh[i0 // 4],
                      ffn_last, t_mg) for i0 in (0, 4)]
    scr3_last = pe_now()
    lx3 = land("x3out")
    pool.wait(*[X_t[i] for i in range(8)], t_xh)
    for i in range(8):
        t_x3 = lx3.dma(pool, x3_dram[i * P:(i + 1) * P, :], X[:, i, :])

    Q2 = reg(64, 4, 1024)
    K2 = reg(105, 4, 1024)
    V2 = reg(121, 8, 512)
    COS = reg(137, 1024)
    SIN = reg(141, 1024)
    QR = [reg(96 + 2 * j, 512) for j in range(4)]
    rot = m(P)
    pool.wait(xc_last)
    cl = land("cs")
    cl.dma(pool, COS, a["cos"])
    cl.dma(pool, rot, a["rot"])
    t_cs = cl.dma(pool, SIN, a["sin"])
    qr_free = [XN_done[1][-1]] * 4
    n = 0
    QK2_done = []
    pend = []

    def rope(j, t1, d, h_):
        pe.wait(t1, t_cs)
        b = bank()
        t = mm(ps[:, b, :], rot, QR[j], True, True, True)
        dve.wait(t, t_cs, t_x3)
        t2 = dve.do(lambda e: e.tensor_tensor(d, ps[:, b, :], SIN[:, h_], ALU.mult))
        bfree[b] = t2
        t3 = dve.do(lambda e: e.tensor_tensor(QR[j], QR[j], COS[:, h_], ALU.mult))
        dve.wait(t2, t3)
        t4 = dve.do(lambda e: e.tensor_tensor(d, d, QR[j], ALU.add))
        qr_free[j] = t4
        QK2_done.append(t4)

    for dst in (Q2, K2):
        for mt in range(4):
            s, (w,) = ws.get()
            for hf in range(2):
                h_ = slice(hf * 512, (hf + 1) * 512)
                j = n % 4
                n += 1
                pe.wait(XN_done[hf])
                b = bank()
                for k in range(8):
                    t = mm3(ps[:, b, :], at(w, slice(None), k), at(XN, slice(None), k, h_), k == 0, k == 7, k == 7)
                act.wait(t, qr_free[j])
                sc_ = 0.125 if dst is Q2 else 1.0
                t1 = act.do(lambda e: e.activation(QR[j], ps[:, b, :], ACT.Copy, scale=sc_))
                bfree[b] = t1
                if pend:
                    rope(*pend.pop())
                pend.append((j, t1, dst[:, mt, h_], h_))
            ws.done(s, t)
    V2_done = []
    for q in range(2):
        s0, (w0,) = ws.get()
        s1, (w1,) = ws.get(1)
        for i in range(8):
            b = bank()
            for k in range(8):
                w = at(w0, slice(None), k) if k < 4 else at(w1, slice(None), k - 4)
                t = mm3(ps[:, b, 0:256], at(XN, slice(None), k, slice(i * P, (i + 1) * P)), w, k == 0, k == 7, k == 7)
            if pend:
                rope(*pend.pop())
            act.wait(t, t_x3)
            bfree[b] = act.do(lambda e: e.copy(V2[:, i, q * 256:(q + 1) * 256], ps[:, b, 0:256]))
            V2_done.append(bfree[b])
        ws.done(s0, t)
        ws.done(s1, t)

    stacks = [dict(Q=[regR(o, 1024), regR(o + 4, 1024)], K=[regR(o + 8, 1280), regR(o + 13, 1280)],
                   L=regR(o + 18, 1280)) for o in (80, 137)]
    lo_half, hi_half = slice(0, 64), slice(64, 128)

    def build(h, free):
        sk = stacks[h % 2]
        out_ = []
        for mp, (own, other) in enumerate(((lo_half, hi_half), (hi_half, lo_half))):
            q_, qs, ks, kl = Q2[own, h, :], sk["Q"][mp], sk["K"][mp], sk["L"]
            act.wait(free, QK2_done, kc_done)
            t1 = act.do(lambda e: e.activation(qs[own, :], q_, ACT.Copy))
            dve.wait(t1)
            out_.append(dve.do(lambda e: e.tensor_tensor(qs[other, :], q_, qs[own, :].bitcast(F32), ALU.subtract)))
            for k_, c in ((K2[own, h, :], slice(0, 1024)), (K2c[own, h, :], slice(1024, 1280))):
                t1 = act.do(lambda e: e.activation(ks[own, c], k_, ACT.Copy))
                dve.wait(t1)
                out_.append(dve.do(lambda e: e.tensor_tensor(kl[own, c], k_, ks[own, c].bitcast(F32),
                                                             ALU.subtract)))
                out_.append(act.do(lambda e: e.activation(ks[other, c], k_, ACT.Copy)))
        return out_

    SK_done = {0: build(0, None)}

    CV = lambda ct: reg(137 + 4 * ct, 1024)
    u = reg(165, 1024)
    u_free = [QK2_done]
    CV_done = []
    for ct in range(4):
        o = CV(ct)
        ps_ = []
        t4s, t5s = [], []
        for n_ in range(3):
            s, (w,) = ws.get()
            for hf in range(2):
                pe.wait(XN_done[hf])
                h_ = slice(hf * 512, (hf + 1) * 512)
                b = bank()
                for k in range(8):
                    t = mm3(ps[:, b, :], at(w, slice(None), k), at(XN, slice(None), k, h_), k == 0, k == 7, k == 7)
                if n_ == 0:
                    act.wait(t, u_free[0])
                    bfree[b] = act.do(lambda e: e.copy(u[:, h_], ps[:, b, :]))
                    t4s.append(bfree[b])
                elif n_ == 1:
                    dve.wait(t, t4s[hf])
                    bfree[b] = dve.do(lambda e: e.tensor_tensor(u[:, h_], ps[:, b, :], u[:, h_], ALU.mult))
                    t5s.append(bfree[b])
                else:
                    ps_.append((b, t, h_))
            ws.done(s, t)
            if n_ == 1:
                wcol = lambda w_: col("conv_w", w_ * 4 + ct)
                dve.wait(*t5s, scr3_last)
                t = dve.do(lambda e: e.tensor_scalar(o, u, wcol(1), None, ALU.mult))
                dve.wait(t)
                t = dve.do(lambda e: e.scalar_tensor_tensor(out=o[:, 1:], in0=u[:, 0:S - 1], scalar=wcol(0),
                                                            in1=o[:, 1:], op0=ALU.mult, op1=ALU.add))
                dve.wait(t)
                tc = dve.do(lambda e: e.scalar_tensor_tensor(out=o[:, 0:S - 1], in0=u[:, 1:], scalar=wcol(2),
                                                             in1=o[:, 0:S - 1], op0=ALU.mult, op1=ALU.add))
                u_free[0] = tc
        for b, t, h_ in ps_:
            dve.wait(t, tc)
            bfree[b] = dve.do(lambda e: e.tensor_tensor(o[:, h_], ps[:, b, :], o[:, h_], ALU.mult))
            CV_done.append(bfree[b])

    xn_last = pe_now()
    assert ws.used == len(ws.specs)
    w_idle = ws.ready[len(ws.specs) - 1]

    MX = pair(0, 32, 8, 1024)
    PA = [[reg(160 + 10 * j, 1280), reg(165 + 10 * j, 1280)] for j in range(3)]
    PTa = [reg(64, 8, P), reg(105, 8, P)]
    PTb = [reg(103, 2, P), reg(104, 2, P)]
    OM2 = [reg(190 + 0.5 * j, P) for j in range(2)]
    SQ2 = reg(191, P)
    lams = reg(103, 256)
    lt = reg(104, 128)
    lamc = m(8)
    pairs = lambda n: [[m(1), m(1)] for _ in range(n)]
    m8, s8, r8 = pairs(3), pairs(3), pairs(3)
    sub_ss = [m(1), m(1)]
    subg = m(2)
    pool.wait(QK2_done)
    gsl = land("subg")
    gsl.dma(pool, subg[:, 0:1], a["subln_g_2"].rearrange("o d -> d o"))
    for i, nm in enumerate(("lambda_q1_2", "lambda_k1_2", "lambda_q2_2", "lambda_k2_2")):
        t_sg = gsl.dma(pool, lams[:, i * 64:(i + 1) * 64], a[nm].to_broadcast([P, 64]))
    dve.wait(t_sg)
    t_sg = dve.do(lambda e: e.tensor_scalar(subg[:, 1:2], subg[:, 0:1], 0.8, None, ALU.mult))
    t1 = dve.do(lambda e: e.tensor_tensor(lt[:, 0:64], lams[:, 0:64], lams[:, 64:128], ALU.mult))
    t2 = dve.do(lambda e: e.tensor_tensor(lt[:, 64:128], lams[:, 128:192], lams[:, 192:256], ALU.mult))
    dve.wait(t1, t2)
    t1 = dve.do(lambda e: e.tensor_reduce(lamc[:, 0:2], lt.rearrange("p (a b) -> p a b", a=2), AX.X, ALU.add))
    act.wait(t1)
    t1 = act.do(lambda e: e.activation(lamc[:, 2:4], lamc[:, 0:2], ACT.Exp))
    dve.wait(t1)
    t1 = dve.do(lambda e: e.tensor_tensor(lamc[:, 4:5], lamc[:, 3:4], lamc[:, 2:3], ALU.subtract))
    dve.wait(t1)
    t_lam = dve.do(lambda e: e.tensor_scalar(lamc[:, 5:6], lamc[:, 4:5], -0.2, None, ALU.add))
    nlam = lamc[:, 5:6]
    MXc_done = [split(CV(ct), at(MX, slice(None), 4 + ct), [*CV_done], xn_last) for ct in range(4)]
    SK_done[1] = build(1, MXc_done)
    Xt = lambda i: reg(80 + 4 * i, D) if i < 4 else reg(137 + 4 * (i - 4), D)
    G1, G2 = reg(96, D), reg(125, D)
    X3_in = []

    def x3_back(i0, i1, free):
        pool.wait(free)
        for i in range(i0, i1):
            X3_in.append(land(f"xr{i}").dma(pool, Xt(i), x3_dram[i * P:(i + 1) * P, :]))

    def mod_row(dst, chunk, norm, tmp, free, name):
        pool.wait(*free)
        lg = land(name)
        cs = slice(chunk * D, (chunk + 1) * D)
        lg.dma(pool, dst, mod_dram[0:1, cs].to_broadcast([P, D]))
        lg.dma(pool, tmp[0], mod_dram[2:3, cs].to_broadcast([P, D]))
        lg.dma(pool, tmp[1], a["b_ada_2"][:, cs].to_broadcast([P, D]))
        t = lg.dma(pool, tmp[2], a[norm].to_broadcast([P, D]))
        dve.wait(t)
        t = dve.do(lambda e: e.tensor_tensor(dst, dst, tmp[0], ALU.add))
        dve.wait(t)
        t = dve.do(lambda e: e.tensor_tensor(dst, dst, tmp[1], ALU.add))
        dve.wait(t)
        return dve.do(lambda e: e.tensor_tensor(dst, dst, tmp[2], ALU.mult))

    units = [(h, i) for h in range(4) for i in range(NT)]
    st = {}
    p_free, pt2_free, om2_free = [None] * 3, [None] * 2, [None] * 2
    sq_free = [None]

    def scores(u, mp):
        h, i = units[u]
        j = u % 3
        sk = stacks[h % 2]
        b0 = 3 * mp
        pe.wait(bfree[b0], bfree[b0 + 1], bfree[b0 + 2], SK_done[h])
        r = slice(mp * 64, mp * 64 + 64)
        q_ = sk["Q"][mp][:, i * P:(i + 1) * P]
        for c in range(3):
            cs = slice(c * 512, min(c * 512 + 512, 1280))
            o = ps[:, b0 + c, 0:cs.stop - cs.start]
            mm(o, q_, sk["K"][mp][:, cs], True, False, False)
            t = mm(o, q_[r, :], sk["L"][r, cs], False, True, c == 2)
        sv = ps[:, b0:b0 + 3, :].rearrange("p a b -> p (a b)")[:, 0:1280]
        dve.wait(t)
        t1 = dve.do(lambda e: e.tensor_reduce(m8[j][mp], sv, AX.X, ALU.max, negate=True))
        st[("x", u, mp)] = (sv, t1)

    def expo(u, mp):
        j, b0 = u % 3, 3 * mp
        sv, t1 = st[("x", u, mp)]
        act.wait(t1, p_free[j], w_idle)
        t2 = act.do(lambda e: e.activation(PA[j][mp], sv, ACT.Exp, bias=m8[j][mp], accum_out=s8[j][mp]))
        bfree[b0] = bfree[b0 + 1] = bfree[b0 + 2] = t2
        st[("e", u, mp)] = t2

    def combine(u):
        j = u % 3
        r_, s_ = r8[j], s8[j]
        dve.wait(st[("e", u, 0)], st[("e", u, 1)], t_lam)
        t1 = dve.do(lambda e: e.reciprocal(r_[1], s_[1]))
        st[("r", u)] = dve.do(lambda e: e.reciprocal(r_[0], s_[0]))
        dve.wait(t1)
        t1 = dve.do(lambda e: e.tensor_scalar(r_[1], r_[1], s_[0], nlam, ALU.mult, ALU.mult))
        dve.wait(t1)
        st[u] = dve.do(lambda e: e.scalar_tensor_tensor(out=PA[j][0], in0=PA[j][1], scalar=r_[1],
                                                        in1=PA[j][0], op0=ALU.mult, op1=ALU.add))

    tb67 = [0]

    def bank67():
        b = 6 + tb67[0] % 2
        tb67[0] += 1
        pe.wait(bfree[b])
        return b

    def turn_p2(u, groups_):
        j = u % 2
        pe.wait(st[u])
        for c0 in groups_:
            n = min(4, 10 - c0)
            b = bank67()
            for c in range(n):
                t = tr(ps[:, b, c * P:(c + 1) * P], PA[u % 3][0][:, (c0 + c) * P:(c0 + c + 1) * P], ident, c == n - 1)
            o = PTa[j][:, c0:c0 + n, :] if c0 < 8 else PTb[j]
            o, i_ = o.rearrange("p a b -> p (a b)"), ps[:, b, 0:n * P]
            act.wait(t, pt2_free[j], SK_done[0], SK_done[1])
            bfree[b] = act.do(lambda e: e.copy(o, i_))
            st[("t", u, c0)] = bfree[b]
        p_free[u % 3] = t

    def pv2(u):
        h, i = units[u]
        j = u % 2
        b = bank67()
        for c in range(10):
            pe.wait(st[("t", u, c // 4 * 4)])
            v_ = V2[:, c, h * P:(h + 1) * P] if c < 8 else V2c[:, c - 8, h * P:(h + 1) * P]
            w_ = PTa[j][:, c, :] if c < 8 else PTb[j][:, c - 8, :]
            t = mm(ps[:, b, 0:P], w_, v_, c == 0, c == 9, c == 9)
        pt2_free[j] = t
        act.wait(t, st[("r", u)], om2_free[j])
        bfree[b] = act.do(lambda e: e.activation(OM2[j], ps[:, b, 0:P], ACT.Copy, scale=r8[u % 3][0]))
        act.wait(bfree[b], sq_free[0])
        t1 = act.do(lambda e: e.activation(SQ2, OM2[j], ACT.Square, accum_out=sub_ss[j]))
        sq_free[0] = t1
        pool.wait(t1)
        t1 = pool.do(lambda e: e.tensor_scalar(sub_ss[j], sub_ss[j], 1.0 / P, EPS, ALU.mult, ALU.add))
        pool.wait(t1)
        t1 = pool.do(lambda e: e.tensor_tensor(sub_ss[j], sub_ss[j], nhalf[:, 0:1], ALU.pow))
        pool.wait(t1)
        st[("m", u)] = pool.do(lambda e: e.tensor_scalar(OM2[j], OM2[j], sub_ss[j], None, ALU.mult))

    MXa_done = []

    def fin2(u):
        h, i = units[u]
        j = u % 2
        b = bank67()
        pe.wait(st[("m", u)])
        t = tr(ps[:, b, 0:P], OM2[j], ident, True)
        om2_free[j] = t
        bfree[b] = split_psum(ps[:, b, 0:P], at(MX, slice(None), h, slice(i * P, (i + 1) * P)), subg[:, 1:2],
                              [t, t_sg])
        MXa_done.append(bfree[b])

    wo2 = a["w_out_2"][0].rearrange("(c p) n -> p c n", p=P)
    wo = Stream([68, 72, 76, 109, 113], [121, 129, 153, 161, 169, 177, 185, 193], 1024, "o", None)
    wo.add(*[[(1, 1024, wo2[:, k:k + 1, :])] for k in range(8)])
    gtmp = [reg(72, D), reg(76, D), reg(113, D)]

    pe.wait(*QK2_done, *V2_done, *kc_done, *[x for x in bfree if x])
    nu = len(units)
    for u in range(nu + 3):
        if u < nu:
            scores(u, 0)
        if 2 <= u <= nu + 1:
            turn_p2(u - 2, (0, 4))
        if 1 <= u <= nu:
            combine(u - 1)
        if u < nu:
            expo(u, 0)
            scores(u, 1)
        if 2 <= u <= nu + 1:
            turn_p2(u - 2, (8,))
        if u >= 3:
            fin2(u - 3)
        if u < nu:
            expo(u, 1)
        if 2 <= u <= nu + 1:
            pv2(u - 2)
        if u in (NT + 1, 2 * NT + 1):
            h = u // NT + 1
            SK_done[h] = build(h, pe_now())
        if u == 3 * NT + 1:
            b0_free = pe_now()
            x3_back(0, 4, b0_free)
            t_G1 = mod_row(G1, 2, "norm_post_mix_2", gtmp, [b0_free, SK_done[3]], "g1")
            wo.raw_free = [t_G1] * 5
            wo.load()
    att2_last = pe_now()
    x3_back(4, 8, att2_last)

    wo.part_free = [[att2_last, *MXa_done[-1:]]] * 8
    wo.make(8)
    wv = [wo.get(8)[1][0] for _ in range(8)]
    tmp = [reg(64, D), reg(105, D)]
    junk = [reg(100, D), reg(117, D)]
    scr4 = lambda i: reg((68, 72, 76, 109)[i], D) if i < 4 else reg(121 + 4 * (i - 4), D)
    mst = [m(2), m(2)]
    tmp_free = [att2_last, att2_last]
    X4_t = []
    for i in range(NT):
        j = i % 2
        b0 = 2 * (i % 4)
        pe.wait(bfree[b0], bfree[b0 + 1], *MXa_done, *MXc_done)
        for q in range(2):
            for k in range(8):
                t = mm3(ps[:, b0 + q, :], at(MX, slice(None), k, slice(i * P, (i + 1) * P)),
                        at(wv[k], slice(None), 0, slice(q * 512, (q + 1) * 512)), k == 0, k == 7, k == 7)
        v = ps[:, b0:b0 + 2, :].rearrange("p a b -> p (a b)")
        act.wait(t, att2_last, X4_t[i - 2] if i > 1 else None)
        t1 = act.do(lambda e: e.activation(junk[j], v, ACT.Square, accum_out=mst[j][:, 0:1]))
        dve.wait(t1)
        t1 = dve.do(lambda e: e.tensor_scalar(mst[j][:, 0:1], mst[j][:, 0:1], 1.0 / D, EPS, ALU.mult, ALU.add))
        pool.wait(t1)
        t1 = pool.do(lambda e: e.tensor_tensor(mst[j][:, 1:2], mst[j][:, 0:1], nhalf[:, 0:1], ALU.pow))
        dve.wait(t1, t_G1, tmp_free[j])
        t2 = dve.do(lambda e: e.scalar_tensor_tensor(out=tmp[j], in0=v, scalar=mst[j][:, 1:2], in1=G1,
                                                     op0=ALU.mult, op1=ALU.mult))
        bfree[b0] = bfree[b0 + 1] = t2
        dve.wait(t2, X3_in[i])
        t3 = dve.do(lambda e: e.tensor_tensor(Xt(i), Xt(i), tmp[j], ALU.add))
        tmp_free[j] = t3
        act.wait(t3, t1)
        X4_t.append(act.do(lambda e: e.activation(junk[j], Xt(i), ACT.Square, accum_out=ss[:, i:i + 1])))
    wo2_last = pe_now()

    XM = pair(0, 32, 8, 1024)
    lst = land("xhd")
    for i0 in (0, 4):
        t_inv = rms_inv(i0, i0 + 4, 1024.0, X4_t[i0:i0 + 4])
        if i0:
            dve.wait(wo2_last)
        else:
            dve.wait(*[wo.ready[k] for k in range(8)])
        t_xh = xhat(Xt, scr4, i0, i0 + 4, t_inv)
        pool.wait(t_xh)
        for i in range(i0, i0 + 4):
            t_xhd = lst.dma(pool, xh_dram[i * P:(i + 1) * P, :], scr4(i))
        if i0 == 0:
            t_xh0 = t_xh
    tmps = [[reg(o, 512), X4_t] for o in (64, 66, 105, 107)]
    XM_done = turned(scr4, XM, 0, 4, lambda f: mg2[:, f:f + 1], lambda f: shift(16, f), tmps, t_xh0, wo2_last)
    XM_done += turned(scr4, XM, 4, 8, lambda f: mg2[:, f:f + 1], lambda f: shift(16, f), tmps, t_xh, wo2_last)
    scr4_last = pe_now()
    zero = reg(117, D)
    dve.wait(X4_t)
    t = dve.do(lambda e: e.memset(zero, 0.0))
    pool.wait(t)
    lz = land("ffz")
    for i in range(NT):
        t_ffz = lz.dma(pool, ff_dram[i * P:(i + 1) * P, :], zero)

    es = Stream([153, 161, 169, 177, 185, 193], [0, 16, 32], 2048, "e", None)
    es.raw_free = [wo2_last] * 6
    for e_ in range(NE):
        for nm in ("w_gate_2", "w_up_2", "w_down_2"):
            w = a[nm][0, e_].rearrange("(c p) n -> p c n", p=P)
            for q in range(2):
                for k in (0, 4):
                    es.add([(4, 512, w[:, k:k + 4, q * 512:(q + 1) * 512])])
    es.load()

    wr = reg(72, 8, NE)
    wrs = pair(72.5, 73, 8, NE)
    pool.wait(scr4_last, t_xhd)
    t_wr = land("wr").dma(pool, wr, a["w_router_2"][0].rearrange("(c p) n -> p c n", p=P))
    t_wr = split(wr, wrs, [t_wr, scr4_last, t_xhd])
    affT = reg(105, 1024)
    w1_ = reg(109, 1024)
    lg = reg(74, 8, NE)
    mx8 = reg(74.5, 8)
    ix8 = reg(75, P).bitcast(U32)
    top = reg(75.5, P)
    ixf = reg(76, P)
    gT = m(NE)
    iT = m(NE).bitcast(U32)
    pe.wait(t_wr, *XM_done)
    b = bank()
    for i in range(NT):
        for k in range(8):
            t = mm3(ps[:, b, i * NE:(i + 1) * NE], at(XM, slice(None), k, slice(i * P, (i + 1) * P)),
                    at(wrs, slice(None), k), k == 0, k == 7, i == 7 and k == 7)
    router_mm = t
    v = ps[:, b, 0:P].rearrange("p (a b) -> p a b", a=8)
    bc = lambda x: x.rearrange("p (a o) -> p a o", o=1).to_broadcast([P, 8, NE])
    dve.wait(t)
    t = dve.do(lambda e: e.tensor_reduce(mx8, v, AX.X, ALU.max))
    dve.wait(t)
    t = dve.do(lambda e: e.tensor_tensor(lg, v, bc(mx8), ALU.subtract))
    bfree[b] = t
    act.wait(t)
    t = act.do(lambda e: e.activation(lg, lg, ACT.Exp))
    dve.wait(t)
    t = dve.do(lambda e: e.tensor_reduce(mx8, lg, AX.X, ALU.add))
    dve.wait(t)
    t = dve.do(lambda e: e.reciprocal(mx8, mx8))
    dve.wait(t)
    t = dve.do(lambda e: e.tensor_tensor(lg, lg, bc(mx8), ALU.mult))
    pe.wait(t)
    for hf in range(2):
        b = bank()
        for i in range(4):
            t = tr(ps[0:NE, b, i * P:(i + 1) * P], lg[:, hf * 4 + i, :], ident, i == 3)
        dve.wait(t, scr4_last, t_xhd)
        t = dve.do(lambda e: e.tensor_copy(affT[0:NE, hf * 512:(hf + 1) * 512], ps[0:NE, b, :]))
        bfree[b] = t
    dve.wait(t)
    src, dst = affT, w1_
    for r in range(CAP // 8):
        rs_ = slice(r * 8, r * 8 + 8)
        t = dve.do(lambda e: e.max(top[0:NE, rs_], src[0:NE, :]))
        dve.wait(t)
        dve.do(lambda e: e.max_index(ix8[0:NE, rs_], top[0:NE, rs_], src[0:NE, :]))
        t = dve.do(lambda e: e.match_replace(dst[0:NE, :], top[0:NE, rs_], src[0:NE, :], -1.0))
        dve.wait(t)
        src, dst = dst, src
    t = dve.do(lambda e: e.tensor_copy(ixf[0:NE, :], ix8[0:NE, :]))
    pe.wait(t)
    b = bank()
    tr(ps[:, b, 0:NE], top[0:NE, :], ident[0:NE, 0:NE], False)
    t = tr(ps[:, b, NE:2 * NE], ixf[0:NE, :], ident[0:NE, 0:NE], True)
    dve.wait(t)
    t_gT = dve.do(lambda e: e.tensor_copy(gT, ps[:, b, 0:NE]))
    t_iT = dve.do(lambda e: e.tensor_copy(iT, ps[:, b, NE:2 * NE]))
    bfree[b] = t_iT
    route_last = pe_now()
    es.part_free = [router_mm] * 3

    XS = [reg(96 + 4 * j, D) for j in range(2)]
    XST = [pair(48 + 8 * j, 52 + 8 * j, 8, P) for j in range(2)]
    HIT = [pair(64 + 8 * j, 68 + 8 * j, 8, P) for j in range(2)]
    HID = [reg(105 + 4 * j, D) for j in range(2)]
    YS = [reg(113 + 4 * j, D) for j in range(3)]
    vt = [[reg(129 + 2 * j, 512), None] for j in range(4)]
    xs_t, xs_free, hid_t, down_t = {}, [None, None], {}, {}
    ys_t = [None] * 3
    sc_last = [None]
    scl_ = land("scat")

    def gather(e_):
        j = e_ % 2
        pool.wait(t_iT, t_xhd, xs_free[j], wo2_last)
        lg_ = land(f"xs{j}")
        lg_.count += 16
        pool.engine.indirect_dma_start(
            XS[j], None, xh_dram, bass.IndirectOffsetOnAxis(ap=iT[:, e_:e_ + 1], axis=0),
            bounds_check=S - 1).then_inc(lg_.sem, 16)
        xs_t[e_] = (lg_.sem, lg_.count)

    xst_t = {}

    def expert_x(e_):
        j = e_ % 2
        pe.wait(xs_t[e_])
        tt_ = []
        for g_ in range(2):
            b = bank()
            for f in range(4):
                t = tr(ps[:, b, f * P:(f + 1) * P], XS[j][:, (g_ * 4 + f) * P:(g_ * 4 + f + 1) * P], ident, f == 3)
            v = vt[g_]
            vv = v[0].rearrange("p (f n) -> p f n", f=4)
            act.wait(t, v[1], t_gT)
            for f in range(4):
                ff_ = g_ * 4 + f
                t2 = act.do(lambda e: e.activation(vv[:, f, :], ps[:, b, f * P:(f + 1) * P], ACT.Identity,
                                                   bias=shift(16, ff_), scale=mg2[:, ff_:ff_ + 1]))
            bfree[b] = t2
            v[1] = split(vv, at(XST[j], slice(None), slice(g_ * 4, g_ * 4 + 4)), [t2],
                         [hid_t.get(e_ - 2), router_mm])
            tt_.append(v[1])
        xs_free[j] = t
        xst_t[e_] = tt_

    gather(0)
    gather(1)
    expert_x(0)
    for e_ in range(NE):
        j = e_ % 2
        pe.wait(*xst_t[e_])
        bs = []
        for n_ in range(4):
            b = bank()
            for k0 in (0, 4):
                s, (w,) = es.get(2)
                for k in range(4):
                    t = mm3(ps[:, b, :], at(XST[j], slice(None), k0 + k), at(w, slice(None), k), k0 + k == 0,
                            k0 + k == 7, k == 3)
                es.done(s, t)
            bs.append((b, t))
            if n_ < 2:
                h_ = HID[j][:, n_ * 512:(n_ + 1) * 512]
                act.wait(t, route_last)
                t1 = act.do(lambda e: e.activation(h_, ps[:, b, :], ACT.Silu))
                bfree[b] = t1
                bs[n_] = t1
            else:
                h_ = HID[j][:, (n_ - 2) * 512:(n_ - 1) * 512]
                dve.wait(bs[n_ - 2], t)
                t2 = dve.do(lambda e: e.tensor_tensor(h_, ps[:, b, :], h_, ALU.mult))
                bfree[b] = t2
                bs[n_] = t2
        hid_t[e_] = t
        if e_ + 1 < NE:
            expert_x(e_ + 1)
        if e_ + 2 < NE:
            gather(e_ + 2)
        td = []
        for g_ in range(2):
            pe.wait(bs[2 + g_])
            b = bank()
            for f in range(4):
                t = tr(ps[:, b, f * P:(f + 1) * P], HID[j][:, (g_ * 4 + f) * P:(g_ * 4 + f + 1) * P], ident, f == 3)
            bfree[b] = split_psum(ps[:, b, :], tuple(x.rearrange("p a b -> p (a b)") for x in
                                                     at(HIT[j], slice(None), slice(g_ * 4, g_ * 4 + 4))), None, [t],
                                  [route_last, t_ffz, down_t.get(e_ - 2)])
            td.append(bfree[b])
        jy = e_ % 3
        ty = []
        for q in range(2):
            b = bank()
            for k0 in (0, 4):
                s, (w,) = es.get(2)
                pe.wait(td[k0 // 4])
                for k in range(4):
                    t = mm3(ps[:, b, :], at(HIT[j], slice(None), k0 + k), at(w, slice(None), k), k0 + k == 0,
                            k0 + k == 7, k == 3)
                es.done(s, t)
            o = YS[jy][:, q * 512:(q + 1) * 512]
            act.wait(t, ys_t[jy], t_gT, route_last)
            bfree[b] = act.do(lambda e: e.activation(o, ps[:, b, :], ACT.Copy, scale=gT[:, e_:e_ + 1]))
            ty.append(bfree[b])
        down_t[e_] = t
        pool.wait(*ty, t_ffz, sc_last[0])
        scl_.count += 16
        pool.engine.indirect_dma_start(
            ff_dram, bass.IndirectOffsetOnAxis(ap=iT[:, e_:e_ + 1], axis=0), YS[jy], None,
            bounds_check=S - 1, compute_op=ALU.add).then_inc(scl_.sem, 16)
        sc_last[0] = ys_t[jy] = (scl_.sem, scl_.count)

    out2 = out.rearrange("o s d -> (o s) d")
    pe_last = pe_now()
    t_G2 = mod_row(G2, 5, "norm_post_ffn_2", [reg(153 + 4 * i, D) for i in range(3)],
                   [route_last, *[es.ready[len(es.specs) - 1 - i] for i in range(6)]], "g2")
    lo = land("out")
    for i in range(NT):
        f_ = reg(4 * i, D)
        sp.wait(sc_last[0], pe_last)
        tf = land(f"f{i}").dma(sp, f_, ff_dram[i * P:(i + 1) * P, :])
        act.wait(tf, pe_last, jk_t[i % 2])
        jk2 = reg(32 + 4 * (i % 2), D)
        t1 = jk_t[i % 2] = act.do(lambda e: e.activation(jk2, f_, ACT.Square, accum_out=ss[:, i:i + 1]))
        t_inv = rms_inv(i, i + 1, 1024.0, [t1])
        dve.wait(t_inv, t_G2)
        t2 = dve.do(lambda e: e.scalar_tensor_tensor(out=f_, in0=f_, scalar=inv[:, i:i + 1], in1=G2,
                                                     op0=ALU.mult, op1=ALU.mult))
        dve.wait(t2)
        t3 = dve.do(lambda e: e.tensor_tensor(f_, f_, Xt(i), ALU.add))
        act.wait(t3)
        t_out = lo.dma(act, out2[i * P:(i + 1) * P, :], f_)
    sp.wait(t_out)


_INS = ["x", "g_mix", "w_in", "b_forget", "w_dw", "b_dw", "g_conv_ln", "b_conv_ln", "w_conv_out", "g_q", "g_k",
        "w_attn_out", "w_out", "g_ffn", "w_ffn_in", "w_ffn_out", "c_2", "ctx_2", "c_ctx_2", "w_ada_2", "b_ada_2",
        "norm_pre_mix_2", "norm_post_mix_2", "norm_pre_ffn_2", "norm_post_ffn_2", "w_in_2", "conv_w_2",
        "lambda_q1_2", "lambda_k1_2", "lambda_q2_2", "lambda_k2_2", "subln_g_2", "w_out_2", "w_router_2",
        "w_gate_2", "w_up_2", "w_down_2"]


def _tables():
    f = np.float32
    row = np.repeat(np.arange(16, dtype=f), 64)
    colv = np.tile(np.arange(64, dtype=f), 16)
    iv = (f(10000.0) ** (-np.arange(0, 32, 2, dtype=f) / f(32))).astype(f)
    ar, ac = row[:, None] * iv[None, :], colv[:, None] * iv[None, :]
    ang = np.concatenate([ar, ar, ac, ac], axis=-1)
    cos, sin = np.cos(ang).astype(f), np.sin(ang).astype(f)
    rot = np.zeros((128, 128), f)
    for b in range(0, 128, 32):
        for i in range(16):
            rot[b + 16 + i, b + i] = -1.0
            rot[b + i, b + 16 + i] = 1.0
    two = lambda t: np.ascontiguousarray(np.concatenate([t.T, t.T], axis=0))
    return {"cos": two(cos), "sin": two(sin), "rot": rot}


def kernel(**inputs):
    import concourse.bacc as _bacc
    from concourse.bass_utils import run_bass_kernel_spmd as _run

    nc = _bacc.Bacc("TRN2", target_bir_lowering=False, num_devices=1)
    arrays, args = {}, {}
    every = {n: inputs[n] for n in _INS}
    every.update(_tables())
    for name, v in every.items():
        v = np.ascontiguousarray(v)
        arrays[f"in_{name}_dram"] = v
        args[name] = nc.dram_tensor(f"in_{name}_dram", v.shape, mybir.dt.from_np(v.dtype), kind="ExternalInput").ap()
    o = nc.dram_tensor("out_0_dram", (1, S, D), F32, kind="ExternalOutput").ap()
    program(nc, args, o)
    r = _run(nc, [arrays], core_ids=[0])
    return r.results[0]["out_0_dram"]
```

```python
from contextlib import ExitStack

import numpy as np

import concourse.bass as bass
from concourse import mybir

ALU = mybir.AluOpType
ACT = mybir.ActivationFunctionType
F32 = mybir.dt.float32
F32R = mybir.dt.float32r
U32 = mybir.dt.uint32
AX = mybir.AxisListType

P = 128
S = 1024
D = 1024
NT = S // P
EPS = 1e-6
NEG = -1e30
KB = 256
CAP = 128
NE = 16
CTX = 256
FF = 2816
NF = FF // P
MISC = 1720


class Queue:

    def __init__(self, engine, sem):
        self.engine, self.sem, self.count, self.seen = engine, sem, 0, {}

    def wait(self, *tickets):
        for t in tickets:
            if t is None:
                continue
            if isinstance(t, list):
                self.wait(*t)
                continue
            sem, value = t
            if self.seen.get(sem.name, 0) < value:
                self.seen[sem.name] = value
                self.engine.wait_ge(sem, value)

    def do(self, fn):
        self.count += 1
        fn(self.engine).then_inc(self.sem, 1)
        return self.sem, self.count

    def run(self, fn):
        fn(self.engine)


class Landing:

    def __init__(self, sem):
        self.sem, self.count = sem, 0

    def dma(self, queue, out, in_):
        self.count += 16
        queue.engine.dma_start(out, in_).then_inc(self.sem, 16)
        return self.sem, self.count


def program(nc, a, out):
    ctx = ExitStack()
    with ctx:
        _program(nc, ctx, a, out)


def _program(nc, ctx, a, out):
    sem = lambda n: ctx.enter_context(nc.semaphore(n))
    pe, dve, act, pool, sp = (
        Queue(e, sem(n)) for e, n in ((nc.tensor, "s_pe"), (nc.vector, "s_dve"), (nc.scalar, "s_act"),
                                      (nc.gpsimd, "s_pool"), (nc.sync, "s_sp")))
    base = (nc.sbuf_base + 31) // 32 * 32
    misc = nc.alloc_sbuf_tensor_at("misc", [P, MISC], F32, offset=base + 201 * 1024)
    cvR = nc.alloc_sbuf_tensor_at("cvr", [P, 32], F32R, offset=base + 201 * 1024 + MISC * 4)
    ps = ctx.enter_context(nc.psum_tensor("ps", [P, 8, 512], F32))
    dram = lambda n, *shape: nc.dram_tensor(n, shape, F32, kind="Internal").ap()
    xh_dram, ff_dram, x3_dram, mod_dram = (dram("xhat_scratch", S, D), dram("ff_scratch", S, D),
                                           dram("x3_scratch", S, D), dram("mod_scratch", 4, 6 * D))
    landings = {}

    def land(name):
        if name not in landings:
            landings[name] = Landing(sem("d_" + name))
        return landings[name]

    places = {}

    def view(dtype, kb, shape):
        n = int(np.prod(shape))
        o = int(kb * 1024)
        assert o + 4 * n <= 201 * 1024
        name = f"{'r' if dtype == F32R else 'f'}{o}_{n}"
        if name not in places:
            places[name] = nc.alloc_sbuf_tensor_at(name, [P, n], dtype, offset=base + o)
        v = places[name][:, 0:n]
        if len(shape) == 2:
            v = v.rearrange("p (a b) -> p a b", a=shape[0])
        return v

    reg = lambda kb, *shape: view(F32, kb, shape)
    regR = lambda kb, *shape: view(F32R, kb, shape)
    pair = lambda hi, lo, *shape: (regR(hi, *shape), regR(lo, *shape))
    mpos = [0]

    def m(*shape):
        n = int(np.prod(shape))
        v = misc[:, mpos[0]:mpos[0] + n]
        mpos[0] += n
        assert mpos[0] <= MISC, mpos
        if len(shape) == 2:
            v = v.rearrange("p (a b) -> p a b", a=shape[0])
        return v

    pe_now = lambda: (pe.sem, pe.count)
    everyone = lambda: [(q.sem, q.count) for q in (pe, dve, act, pool) if q.count]

    bfree = [None] * 8
    bnext = [0]

    def bank():
        b = bnext[0] % 8
        bnext[0] += 1
        pe.wait(bfree[b])
        return b

    def mm(o, l, r, start, stop, last):
        fn = lambda e: e.matmul(o, l, r, start=start, stop=stop, skip_group_check=True)
        return pe.do(fn) if last else pe.run(fn)

    def mm3(o, l, r, start, stop, last):
        mm(o, l[0], r[0], start, False, False)
        mm(o, l[0], r[1], False, False, False)
        return mm(o, l[1], r[0], False, stop, last)

    at = lambda p, *idx: (p[0][idx], p[1][idx])

    def tr(o, i, ident_, last):
        fn = lambda e: e.transpose(o, i, ident_)
        return pe.do(fn) if last else pe.run(fn)

    def split(src, dst, waits, free=None, low=dve):
        hi, lo = dst
        act.wait(*waits)
        act.wait(free)
        t = act.do(lambda e: e.activation(hi, src, ACT.Copy))
        low.wait(*waits)
        low.wait(t, free)
        return low.do(lambda e: e.tensor_tensor(lo, src, hi.bitcast(F32), ALU.subtract))

    def split_psum(src, dst, scale, waits, free=None):
        hi, lo = dst
        act.wait(*waits)
        act.wait(free)
        if scale is None:
            t = act.do(lambda e: e.activation(hi, src, ACT.Copy))
        else:
            t = act.do(lambda e: e.activation(hi, src, ACT.Copy, scale=scale))
        dve.wait(*waits)
        dve.wait(t, free)
        if scale is None:
            return dve.do(lambda e: e.tensor_tensor(lo, src, hi.bitcast(F32), ALU.subtract))
        return dve.do(lambda e: e.scalar_tensor_tensor(out=lo, in0=src, scalar=scale, in1=hi.bitcast(F32),
                                                       op0=ALU.mult, op1=ALU.subtract))

    wparts = regR(169, 3, 2048)

    class Stream:

        def __init__(self, raw, parts, size, name, start=None):
            self.raw, self.parts, self.size, self.name = raw, parts, size, name
            self.specs, self.loaded, self.made, self.used = [], 0, 0, 0
            self.landed, self.ready = {}, {}
            self.raw_free, self.part_free = [start] * len(raw), [start] * len(parts)
            self.free, self.retired, self.where = list(range(len(parts))), [], {}

        def add(self, *specs):
            self.specs += specs

        def load(self):
            while self.loaded < len(self.specs) and self.loaded < self.made + len(self.raw):
                i, r = self.loaded, self.loaded % len(self.raw)
                self.loaded += 1
                sp.wait(self.raw_free[r])
                off = 0
                for c, n, src in self.specs[i]:
                    v = reg(self.raw[r], self.size)[:, off:off + c * n]
                    self.landed[i] = land(f"{self.name}{r}").dma(sp, v.rearrange("p (c n) -> p c n", c=c), src)
                    off += c * n
                assert off <= self.size

        def slot(self, p_):
            if self.parts[p_] in (169, 177, 185) and self.size == 1024 and self.name == "w":
                both = wparts[:, p_, :]
            else:
                both = regR(self.parts[p_], 2 * self.size)
            return both[:, 0:self.size], both[:, self.size:2 * self.size]

        def lend(self, kb, ticket):
            self.parts.append(kb)
            self.part_free.append(ticket)
            self.free.append(len(self.parts) - 1)

        def retire(self, p_):
            self.retired.append(p_)
            self.free = [x for x in self.free if x != p_]

        def make(self, ahead, low=dve):
            self.load()
            while self.made < len(self.specs) and self.made <= self.used + ahead and self.free:
                i, r, p_ = self.made, self.made % len(self.raw), self.free.pop(0)
                self.where[i] = p_
                n = sum(c * k for c, k, _ in self.specs[i])
                src = reg(self.raw[r], self.size)[:, 0:n]
                dst = tuple(x[:, 0:n] for x in self.slot(p_))
                t = split(src, dst, [self.landed[i]], self.part_free[p_], low)
                self.ready[i] = t
                self.raw_free[r] = t
                self.made += 1
                self.load()

        def get(self, ahead=3):
            self.make(ahead)
            i = self.used
            self.used += 1
            assert i in self.ready
            pe.wait(self.ready[i])
            out_, off = [], 0
            for c, n, _ in self.specs[i]:
                out_.append(tuple(x[:, off:off + c * n].rearrange("p (c n) -> p c n", c=c)
                                  for x in self.slot(self.where[i])))
                off += c * n
            return self.where[i], out_

        def done(self, slot, ticket):
            self.part_free[slot] = ticket
            if slot not in self.retired:
                self.free.append(slot)

    ident = m(P)
    ones = m(P)
    tri = m(P)
    mask = m(P)
    nhalf = m(64)
    zt = pool.do(lambda e: e.memset(misc[:, 0:MISC], 0.0))
    pool.wait(zt)
    t_ident = pool.do(lambda e: e.affine_select(out=ident, in_=ident, compare_op=ALU.not_equal, fill=1.0, base=0,
                                                pattern=[[-1, P]], channel_multiplier=1))
    t_mask = pool.do(lambda e: e.affine_select(out=mask, in_=mask, compare_op=ALU.is_ge, fill=NEG, base=0,
                                               pattern=[[-1, P]], channel_multiplier=1))
    t_ones = pool.do(lambda e: e.memset(ones, 1.0))
    t_nhalf = pool.do(lambda e: e.memset(nhalf, -0.5))
    pool.wait(t_ones)
    t_tri = pool.do(lambda e: e.affine_select(out=tri, in_=ones, compare_op=ALU.is_ge, fill=0.0, base=0,
                                              pattern=[[1, P]], channel_multiplier=-1))
    consts = [t_ident, t_mask, t_ones, t_nhalf, t_tri]

    x_in = a["x"].rearrange("o s d -> (o s) d")
    xa = lambda i: reg(64 + 4 * i, D)
    xa_t = [land(f"x{i}").dma(sp, xa(i), x_in[i * P:(i + 1) * P, :]) for i in range(8)]
    w_in = a["w_in"][0].rearrange("(c p) n -> p c n", p=P)
    ws = Stream([153, 157, 161], [169, 177, 185], 1024, "w")
    for mt in range(4):
        ws.add([(8, P, w_in[:, :, 512 + mt * P:512 + (mt + 1) * P])], [(8, P, w_in[:, :, mt * P:(mt + 1) * P])])
    ws.add([(8, 8, w_in[:, :, 2560:2568])])
    for g in range(4):
        for q in range(3):
            ws.add([(8, P, w_in[:, :, 1024 + q * 512 + g * P:1024 + q * 512 + (g + 1) * P])])
    wco = a["w_conv_out"][0].rearrange("(c p) n -> p c n", p=P)
    wao = a["w_attn_out"][0].rearrange("(c p) n -> p c n", p=P)
    for mt in range(8):
        ws.add([(8, P, w_in[:, :, 2568 + mt * P:2568 + (mt + 1) * P])])
    for mt in range(8):
        cs = slice(mt * P, (mt + 1) * P)
        ws.add([(8, P, w_in[:, :, 3592 + mt * P:3592 + (mt + 1) * P])],
               [(4, P, wco[:, :, cs]), (4, P, wao[:, :, cs])])
    wout = a["w_out"][0].rearrange("(c p) n -> p c n", p=P)
    for q in range(4):
        for k in (0, 4):
            ws.add([(4, 256, wout[:, k:k + 4, q * 256:(q + 1) * 256])])
    wfi = a["w_ffn_in"][0].rearrange("(c p) n -> p c n", p=P)
    wfo = a["w_ffn_out"][0].rearrange("(c p) n -> p c n", p=P)
    wada = a["w_ada_2"][0].rearrange("(c p) n -> p c n", p=P)
    groups = [range(0, 6), range(6, 12), range(12, 17), range(17, 22)]
    nada = 0
    for fs in groups:
        for f in fs:
            halves = [[(4, 256, wada[:, k:k + 4, nada * 256:(nada + 1) * 256])] for k in (0, 4)]
            ws.add([(8, P, wfi[:, :, f * P:(f + 1) * P])], halves[0],
                   [(8, P, wfi[:, :, FF + f * P:FF + (f + 1) * P])], halves[1])
            nada += 1
            if f in (20, 21):
                ws.add(*[[(4, 256, wada[:, k:k + 4, nada * 256:(nada + 1) * 256])] for k in (0, 4)])
                nada += 1
        for q in range(4):
            qs = slice(q * 256, (q + 1) * 256)
            f0, f1 = fs[0], fs[-1] + 1
            ws.add([(3, 256, wfo[:, f0:f0 + 3, qs])], [(f1 - f0 - 3, 256, wfo[:, f0 + 3:f1, qs])])
    assert nada == 24
    w2 = a["w_in_2"][0].rearrange("(c p) n -> p c n", p=P)
    kspec = lambda mt: [(8, P, w2[:, :, 512 + mt * P:512 + (mt + 1) * P])]
    vspec = lambda q: ([(4, 256, w2[:, 0:4, 1024 + q * 256:1024 + (q + 1) * 256])],
                       [(4, 256, w2[:, 4:8, 1024 + q * 256:1024 + (q + 1) * 256])])
    ws.add(*[kspec(mt) for mt in range(4)], *vspec(0), *vspec(1))
    ws.add(*[[(8, P, w2[:, :, mt * P:(mt + 1) * P])] for mt in range(4)], *[kspec(mt) for mt in range(4)],
           *vspec(0), *vspec(1))
    for ct in range(4):
        for o in (2048, 2560, 1536):
            ws.add([(8, P, w2[:, :, o + ct * P:o + (ct + 1) * P])])
    rows_a = reg(104, P)
    rows_b = reg(104.5, P)
    crow = reg(105, P)
    colsA = m(56)
    colsB = m(124)
    bfb = m(8)
    gqk = m(2)
    L = land("rows")
    vec = lambda v: v.rearrange("o (c p) -> (o c) p", p=P)
    ra = 0
    where = {}
    for name in ("g_mix", "g_ffn", "norm_pre_mix_2", "norm_pre_ffn_2", "b_dw", "g_conv_ln", "b_conv_ln"):
        v = vec(a[name])
        where[name] = ra
        L.dma(sp, rows_a[ra:ra + v.shape[0], :], v)
        ra += v.shape[0]
    where["conv_w"] = ra
    L.dma(sp, rows_a[ra:ra + 12, :], a["conv_w_2"].rearrange("o w (c p) -> (o w c) p", p=P))
    ra += 12
    assert ra == 56
    L.dma(sp, crow[0:8, :], a["c_2"].rearrange("o (c p) -> (o c) p", p=P))
    L.dma(sp, crow[8:16, :], a["c_ctx_2"].rearrange("(c p) -> c p", p=P))
    t_rows = L.dma(sp, rows_b[0:124, :], a["w_dw"].rearrange("o w (c p) -> (o w c) p", p=P))
    ws.load()
    sp.wait(zt)
    L = land("small")
    L.dma(sp, bfb, a["b_forget"].to_broadcast([P, 8]))
    L.dma(sp, gqk[0:64, 0:1], a["g_q"].rearrange("o d -> d o"))
    t_small = L.dma(sp, gqk[0:64, 1:2], a["g_k"].rearrange("o d -> d o"))
    ss4 = m(8, 4)
    ss = m(8)
    inv = m(8)

    def rms_inv(n0, n1, size, waits):
        dve.wait(*waits)
        t = dve.do(lambda e: e.tensor_scalar(ss[:, n0:n1], ss[:, n0:n1], 1.0 / size, EPS, ALU.mult, ALU.add))
        pool.wait(t, t_nhalf)
        return pool.do(lambda e: e.tensor_tensor(inv[:, n0:n1], ss[:, n0:n1], nhalf[:, 0:n1 - n0], ALU.pow))

    def xhat(src, scratch, i0, i1, t_inv):
        dve.wait(t_inv)
        for i in range(i0, i1):
            t = dve.do(lambda e: e.tensor_scalar(scratch(i), src(i), inv[:, i:i + 1], None, ALU.mult))
        return t

    t_ss = []
    for i in range(8):
        act.wait(zt, xa_t[i], t_ss[i - 2] if i > 1 else None)
        t_ss.append(act.do(lambda e: e.activation(reg(96 + 4 * (i % 2), D), xa(i), ACT.Square,
                                                  accum_out=ss[:, i:i + 1])))
    x_hat = []
    for i0 in (0, 4):
        t_inv = rms_inv(i0, i0 + 4, 1024.0, t_ss[i0:i0 + 4])
        x_hat.append(xhat(xa, xa, i0, i0 + 4, t_inv))
    dve.wait(zt)
    t_g1 = dve.do(lambda e: e.memset(gqk[64:66, :], 1.0))
    dve.wait(t_small)
    t_gq = dve.do(lambda e: e.tensor_scalar(gqk[0:64, 0:1], gqk[0:64, 0:1], 0.125, None, ALU.mult))
    pe.wait(t_rows, *consts)
    act.wait(t_rows)
    b = bank()
    tr(ps[:, b, 0:56], rows_a[0:56, :], ident[0:56, 0:56], False)
    tr(ps[:, b, 64:188], rows_b[0:124, :], ident[0:124, 0:124], False)
    t = tr(ps[:, b, 192:208], crow[0:16, :], ident[0:16, 0:16], True)
    dve.wait(t)
    dve.do(lambda e: e.tensor_copy(colsA, ps[:, b, 0:56]))
    t_cols = dve.do(lambda e: e.tensor_copy(colsB, ps[:, b, 64:188]))
    cf = m(8, 2)
    bfree[b] = t_cf = dve.do(lambda e: e.tensor_copy(cf.rearrange("p k r -> p r k"),
                                                     ps[:, b, 192:208].rearrange("p (r k) -> p r k", r=2)))
    col = lambda name, i: colsA[:, where[name] + i:where[name] + i + 1]
    act.wait(t_cols, t_gq, t_g1)

    def turned(scratch, dst, i0, i1, gains, biases, temps, t_xh, dst_free, gain_t=None):
        done, late = [], []

        def low():
            k, v, d, t_hi = late.pop()
            dve.wait(t_hi)
            temps[k][1] = dve.do(lambda e: e.tensor_tensor(d[1], v, d[0].bitcast(F32), ALU.subtract))
            done.append(temps[k][1])

        pe.wait(t_xh)
        n = (i1 - i0) * P
        for f in range(8):
            b = bank()
            for i in range(i0, i1):
                t = tr(ps[:, b, (i - i0) * P:(i - i0 + 1) * P], scratch(i)[:, f * P:(f + 1) * P], ident, i == i1 - 1)
            d = at(dst, slice(None), f, slice(i0 * P, i1 * P))
            if biases is None:
                bfree[b] = split_psum(ps[:, b, 0:n], d, gains(f), [t, gain_t], dst_free)
                done.append(bfree[b])
            else:
                k = f % len(temps)
                v = temps[k][0][:, 0:n]
                dve.wait(t, gain_t, temps[k][1])
                t = dve.do(lambda e: e.tensor_scalar(v, ps[:, b, 0:n], gains(f), biases(f), ALU.mult, ALU.add))
                bfree[b] = t
                act.wait(t, dst_free)
                t_hi = act.do(lambda e: e.activation(d[0], v, ACT.Copy))
                if late:
                    low()
                late.append((k, v, d, t_hi))
                dve.wait(dst_free)
        if late:
            low()
        return done

    HT = pair(0, 32, 8, 1024)
    HT_done = []
    for i0 in (0, 4):
        if i0:
            ws.make(2)
        t_xh = x_hat[i0 // 4]
        HT_done.append(turned(xa, HT, i0, i0 + 4, lambda f: col("g_mix", f), None, None, t_xh, None))
    xa_last = pe_now()

    zero = reg(113, D)
    t = pool.do(lambda e: e.memset(zero, 0.0))
    pool.wait(t)
    lz = land("ffz")
    for i in range(NT):
        t_ffz = lz.dma(pool, ff_dram[i * P:(i + 1) * P, :], zero)
    CA = reg(121, 4, 1024)
    CO = reg(137, 4, 1024)
    t_glu = []
    for mt in range(4):
        c = CA[:, mt, :]
        s, (wg,) = ws.get()
        for hf in range(2):
            pe.wait(HT_done[hf])
            h_ = slice(hf * 512, (hf + 1) * 512)
            b = bank()
            for k in range(8):
                t = mm3(ps[:, b, :], at(wg, slice(None), k), at(HT, slice(None), k, h_), k == 0, k == 7, k == 7)
            act.wait(t)
            t1 = act.do(lambda e: e.activation(c[:, h_], ps[:, b, :], ACT.Sigmoid))
            bfree[b] = t1
        ws.done(s, t)
        s, (wa,) = ws.get()
        for hf in range(2):
            h_ = slice(hf * 512, (hf + 1) * 512)
            b = bank()
            for k in range(8):
                t = mm3(ps[:, b, :], at(wa, slice(None), k), at(HT, slice(None), k, h_), k == 0, k == 7, k == 7)
            dve.wait(t1, t)
            t2 = dve.do(lambda e: e.tensor_tensor(c[:, h_], ps[:, b, :], c[:, h_], ALU.mult))
            bfree[b] = t2
            t_glu.append(t2)
        ws.done(s, t)

    conv = {"n": 0, "t": [None] * 4}

    def conv_steps(n):
        for _ in range(n):
            k = conv["n"]
            if k >= 124:
                return
            conv["n"] += 1
            tap, ct = k // 4, k % 4
            w, sh = 30 - tap, tap
            wc = colsB[:, w * 4 + ct:w * 4 + ct + 1]
            if tap == 0:
                dve.wait(*t_glu)
                t = dve.do(lambda e: e.tensor_scalar(CO[:, ct, :], CA[:, ct, :], wc, col("b_dw", ct), ALU.mult,
                                                     ALU.add))
            else:
                dve.wait(conv["t"][ct])
                t = dve.do(lambda e: e.scalar_tensor_tensor(out=CO[:, ct, sh:], in0=CA[:, ct, 0:S - sh], scalar=wc,
                                                            in1=CO[:, ct, sh:], op0=ALU.mult, op1=ALU.add))
            conv["t"][ct] = t

    act.wait(t_cf)
    t = act.do(lambda e: e.activation(cf, cf, ACT.Silu))
    cv = cvR[:, 0:32].rearrange("p (k r) -> p k r", r=4)
    act.wait(t)
    t = act.do(lambda e: e.activation(cv[:, :, 0:2], cf, ACT.Copy))
    dve.wait(t)
    t_cv = dve.do(lambda e: e.tensor_tensor(cv[:, :, 2:4], cf, cv[:, :, 0:2].bitcast(F32), ALU.subtract))

    zf, zb, lf, Lp, cc, ncc = m(64), m(64), m(64), m(8, 8), m(8, 8), m(8, 8)
    s, (wf,) = ws.get()
    pe.wait(*HT_done)
    fgT = reg(105, 1024)
    for hf in range(2):
        b = bank()
        for k in range(8):
            t = mm3(ps[0:8, b, :], at(wf, slice(None), k), at(HT, slice(None), k, slice(hf * 512, hf * 512 + 512)),
                    k == 0, k == 7, k == 7)
        act.wait(t)
        bfree[b] = t_fg = act.do(lambda e: e.copy(fgT[0:8, hf * 512:(hf + 1) * 512], ps[0:8, b, :]))
    ws.done(s, t)
    pe.wait(t_fg)
    b = bank()
    for i in range(NT):
        t = tr(ps[:, b, i * 8:i * 8 + 8], fgT[0:8, i * P:(i + 1) * P], ident[0:8, 0:8], i == 7)
    dve.wait(t, t_small)
    t = dve.do(lambda e: e.tensor_tensor(zf.rearrange("p (a b) -> p a b", a=8),
                                         ps[:, b, 0:64].rearrange("p (a b) -> p a b", a=8),
                                         bfb.rearrange("p (o b) -> p o b", o=1).to_broadcast([P, 8, 8]), ALU.add))
    bfree[b] = t
    dve.wait(t)
    t = dve.do(lambda e: e.tensor_scalar(zb, zf, -1.0, None, ALU.mult))
    dve.wait(t)
    t = dve.do(lambda e: e.tensor_tensor(zb, zb, zf, ALU.max))
    act.wait(t)
    t = act.do(lambda e: e.activation(zb, zb, ACT.Exp, scale=-1.0))
    act.wait(t)
    t = act.do(lambda e: e.activation(zb, zb, ACT.Ln, bias=1.0))
    dve.wait(t)
    t = dve.do(lambda e: e.scalar_tensor_tensor(out=lf, in0=zf, scalar=0.0, in1=zb, op0=ALU.min, op1=ALU.subtract))
    dve.wait(t)
    for i in range(1, 8):
        t = dve.do(lambda e: e.tensor_tensor(Lp[:, i, :], Lp[:, i - 1, :], lf[:, (i - 1) * 8:i * 8], ALU.add))
        dve.wait(t)
    t_lp = t

    QT = reg(64, 2, 1024)
    KT = reg(72, 2, 1024)
    VV = reg(80, 8, P)
    QK = [reg(84 + 1.03125 * j, 4, 66) for j in range(2)]
    SQ = [reg(86.0625 + 1 * j, 256) for j in range(2)]
    OM = [reg(88.0625, P), m(P)]
    PB = [reg(89 + 4 * j, 1024) for j in range(2)]
    PT = [reg(97 + 4 * j, 8, P) for j in range(2)]
    OT = reg(105, 4, 1024)
    st4 = [m(4), m(4)]
    iv4 = [m(4), m(4)]
    nmax = [m(1), m(1)]
    rsum = [m(1), m(1)]
    rinv = [m(1), m(1)]
    pool.wait(xa_last)
    for j in range(2):
        pool.do(lambda e: e.memset(QK[j][:, 0:2, 64:65], 1.0))
        t_aug = pool.do(lambda e: e.memset(QK[j][:, 2:4, 65:66], 1.0))
    qk_free = [None, None]
    sq_rd = [None, None]
    att_done = [xa_last]
    OT_done = []
    pb_free, pt_free, om_free = [None, None], [None, None], [None, None]

    def cumulate():
        pe.wait(t_lp)
        b = bank()
        mm(ps[:, b, 0:64], ones, Lp.rearrange("p a b -> p (a b)"), True, False, False)
        t = mm(ps[:, b, 0:64], tri, lf, False, True, True)
        dve.wait(t)
        dve.do(lambda e: e.tensor_copy(cc.rearrange("p a b -> p (a b)"), ps[:, b, 0:64]))
        t_cc = dve.do(lambda e: e.tensor_scalar(ncc.rearrange("p a b -> p (a b)"), ps[:, b, 0:64], -1.0, None,
                                                ALU.mult))
        bfree[b] = t_cc
        pool.wait(t_cc)

    def project(g):
        slots = [ws.get(2 - q)[0] for q in range(3)]
        assert sorted(slots) == [0, 1, 2]
        w = lambda k: (wparts[:, :, k * P:(k + 1) * P], wparts[:, :, 1024 + k * P:1024 + (k + 1) * P])
        seg = dict(enumerate(slots))
        tt = []
        for i in range(NT):
            b = bank()
            for k in range(8):
                t = mm3(ps[:, b, 0:384], at(HT, slice(None), k, slice(i * P, (i + 1) * P)), w(k), k == 0, k == 7,
                        k == 7)
            if i == NT - 1:
                for s_ in range(3):
                    ws.done(s_, t)
            if g == 0 and i == 0:
                cumulate()
            j = i % 2
            if i >= 2:
                turn_qk(*tt[i - 2])
            pq, pk, pv_ = (ps[:, b, seg[q] * P:(seg[q] + 1) * P] for q in range(3))
            act.wait(t, sq_rd[j], xa_last)
            act.do(lambda e: e.activation(SQ[j][:, 0:P], pq, ACT.Square))
            t1 = act.do(lambda e: e.activation(SQ[j][:, P:2 * P], pk, ACT.Square))
            act.wait(*att_done)
            tv = act.do(lambda e: e.copy(VV[:, i, :], pv_))
            dve.wait(t1)
            t2 = dve.do(lambda e: e.tensor_reduce(st4[j], SQ[j].rearrange("p (h d) -> p h d", h=4), AX.X, ALU.add))
            sq_rd[j] = t2
            dve.wait(t2)
            t2 = dve.do(lambda e: e.tensor_scalar(st4[j], st4[j], 1.0 / 64, EPS, ALU.mult, ALU.add))
            pool.wait(t2)
            t3 = pool.do(lambda e: e.tensor_tensor(iv4[j], st4[j], nhalf[:, 0:4], ALU.pow))
            pool.wait(qk_free[j], t_aug)
            hs = lambda x: x[:, i, 2 * g:2 * g + 2].rearrange("p (h o) -> p h o", o=1)
            pool.do(lambda e: e.tensor_copy(QK[j][:, 0:2, 65:66], hs(cc)))
            t4 = pool.do(lambda e: e.tensor_copy(QK[j][:, 2:4, 64:65], hs(ncc)))
            dve.wait(t3, qk_free[j], tv)
            for q, src in ((0, pq), (1, pk)):
                t5 = dve.do(lambda e: e.tensor_tensor(
                    QK[j][:, 2 * q:2 * q + 2, 0:64], src.rearrange("p (h d) -> p h d", h=2),
                    iv4[j][:, 2 * q:2 * q + 2].rearrange("p (h o) -> p h o", o=1).to_broadcast([P, 2, 64]),
                    ALU.mult))
            bfree[b] = [t5, tv]
            tt.append((i, j, t4, t5, tv))
            conv_steps(2)
        turn_qk(*tt[6])
        return turn_qk(*tt[7])

    def turn_qk(i, j, t4, t5, tv):
        pe.wait(t4, t5)
        b = bank()
        for q in range(4):
            t = tr(ps[0:66, b, q * P:(q + 1) * P], QK[j][:, q, :], ident, q == 3)
        qk_free[j] = t
        sl = slice(i * P, (i + 1) * P)
        v = ps[0:66, b, :].rearrange("p (q n) -> p q n", q=4)
        act.wait(t, *att_done)
        act.do(lambda e: e.activation(QT[0:66, :, sl], v[:, 0:2, :], ACT.Copy, scale=gqk[0:66, 0:1]))
        ta = act.do(lambda e: e.activation(KT[0:66, :, sl], v[:, 2:4, :], ACT.Copy, scale=gqk[0:66, 1:2]))
        bfree[b] = ta
        return [ta, tv]

    def attention(g, ready):
        units = [(i, h) for n_ in range(4) for h in range(2) for i in (n_, NT - 1 - n_)]
        om = {i: n_ % 2 for n_, (i, h) in enumerate(units)}
        st = {}

        def qk(u):
            i, h = units[u]
            kw = (i + 1) * P
            b0 = 0 if u % 2 == 0 else 2
            pe.wait(bfree[b0], bfree[b0 + 1])
            for c0 in range(0, kw, 512):
                n = min(512, kw - c0)
                diag = c0 + n == kw
                o = ps[:, b0 + c0 // 512, 0:n]
                t = mm(o, QT[0:66, h, i * P:(i + 1) * P], KT[0:66, h, c0:c0 + n], True, not diag, False)
                if diag:
                    t = mm(o[:, n - P:n], ident, mask, False, True, True)
            j = u % 2
            sv = ps[:, b0:b0 + 2, :].rearrange("p a b -> p (a b)")[:, 0:kw]
            dve.wait(t)
            t1 = dve.do(lambda e: e.tensor_reduce(nmax[j], sv, AX.X, ALU.max, negate=True))
            act.wait(t1, pb_free[j])
            t2 = act.do(lambda e: e.activation(PB[j][:, 0:kw], sv, ACT.Exp, bias=nmax[j], accum_out=rsum[j]))
            bfree[b0] = bfree[b0 + 1] = t2
            st[u] = t2

        def turn_p(u):
            i, h = units[u]
            j = u % 2
            pe.wait(st[u])
            ts = []
            for c0 in range(0, i + 1, 4):
                n = min(4, i + 1 - c0)
                b = 4 + (c0 // 4)
                pe.wait(bfree[b])
                for c in range(n):
                    t = tr(ps[:, b, c * P:(c + 1) * P], PB[j][:, (c0 + c) * P:(c0 + c + 1) * P], ident, c == n - 1)
                q = act if c0 == 0 else dve
                q.wait(t, pt_free[j])
                o, i_ = PT[j][:, c0:c0 + n, :].rearrange("p a b -> p (a b)"), ps[:, b, 0:n * P]
                bfree[b] = (act.do(lambda e: e.copy(o, i_)) if c0 == 0 else
                            dve.do(lambda e: e.tensor_copy(o, i_)))
                ts.append(bfree[b])
            pb_free[j] = t
            dve.wait(st[u])
            st[("r", u)] = dve.do(lambda e: e.reciprocal(rinv[j], rsum[j]))
            st[u] = (st[u], ts)

        def pv(u):
            i, h = units[u]
            j = u % 2
            te, ts = st[u]
            pe.wait(*ts)
            pe.wait(bfree[6])
            for c in range(i + 1):
                t = mm(ps[:, 6, 0:64], PT[j][:, c, :], VV[:, c, h * 64:(h + 1) * 64], c == 0, c == i, c == i)
            pt_free[j] = t
            dve.wait(t, st[("r", u)], om_free[om[i]])
            bfree[6] = dve.do(lambda e: e.tensor_scalar(OM[om[i]][:, h * 64:(h + 1) * 64], ps[:, 6, 0:64], rinv[j],
                                                        None, ALU.mult))
            if h == 1:
                st[("o", i)] = bfree[6]

        def turn_o(i):
            pe.wait(st[("o", i)], bfree[7])
            t = tr(ps[:, 7, 0:P], OM[om[i]], ident, True)
            om_free[om[i]] = t
            act.wait(t, t_ffz)
            bfree[7] = act.do(lambda e: e.copy(OT[:, g, i * P:(i + 1) * P], ps[:, 7, 0:P]))
            OT_done.append(bfree[7])

        pe.wait(*ready)
        n = len(units)
        for u in range(n + 2):
            if u < n:
                qk(u)
            if u >= 3 and units[u - 3][1] == 1:
                turn_o(units[u - 3][0])
            if u >= 2:
                pv(u - 2)
            if 1 <= u <= n:
                turn_p(u - 1)
            if u % 2:
                conv_steps(1)
            if u in (8, 10, 12):
                ws.make((u - 8) // 2)
        turn_o(units[n - 1][0])
        att_done[:] = [pe_now()]

    for g in range(4):
        attention(g, project(g))
    att1_last = pe_now()

    GA = reg(64, 8, 1024)
    rs = reg(96, 1024)
    CN = (lambda ct: view(F32R, 100 if ct == 0 else 193 + 4 * (ct - 1) if ct < 3 else 165, [1024]),
          lambda ct: view(F32R, 137 + 4 * ct, [1024]))
    CN_done = []
    OTh, OTl = view(F32R, 121, [4, 1024]), view(F32R, 105, [4, 1024])
    t_cn = []
    mean, ln, OS_done = [], {}, []

    def ln_centre():
        conv_steps(200)
        t_conv = conv["t"]
        for hf in range(2):
            b = bank()
            pe.wait(*t_conv)
            for ct in range(4):
                t = mm(ps[:, b, :], ones, CO[:, ct, hf * 512:(hf + 1) * 512], ct == 0, ct == 3, ct == 3)
            dve.wait(t)
            for ct in range(4):
                v = CO[:, ct, hf * 512:(hf + 1) * 512]
                tc = dve.do(lambda e: e.scalar_tensor_tensor(out=v, in0=ps[:, b, :], scalar=-1.0 / 512, in1=v,
                                                             op0=ALU.mult, op1=ALU.add))
                q = CA[:, ct, hf * 512:(hf + 1) * 512]
                act.wait(tc)
                tq = act.do(lambda e: e.activation(q, v, ACT.Square))
            bfree[b] = tc
            mean.append(tq)

    def ln_scale():
        for hf in range(2):
            b = bank()
            pe.wait(mean[hf])
            for ct in range(4):
                t = mm(ps[:, b, :], ones, CA[:, ct, hf * 512:(hf + 1) * 512], ct == 0, ct == 3, ct == 3)
            r = rs[:, hf * 512:(hf + 1) * 512]
            dve.wait(t, att1_last)
            t1 = dve.do(lambda e: e.tensor_scalar(r, ps[:, b, :], 1.0 / 512, EPS, ALU.mult, ALU.add))
            bfree[b] = t1
            act.wait(t1)
            t1 = act.do(lambda e: e.activation(r, r, ACT.Sqrt))
            dve.wait(t1)
            t1 = dve.do(lambda e: e.reciprocal(r, r))
            dve.wait(t1)
            for ct in range(4):
                v = CO[:, ct, hf * 512:(hf + 1) * 512]
                tm = dve.do(lambda e: e.tensor_tensor(v, v, r, ALU.mult))
                t_cn.append((ct, hf, v, tm))
        ln["last"] = pe_now()

    def ln_apply():
        for c in range(4):
            OS_done.append(split(OT[:, c, :], (OTh[:, c, :], OTl[:, c, :]), [*OT_done, ln["last"]]))
        for ct, hf, v, tm in t_cn:
            act.wait(tm)
            t = act.do(lambda e: e.activation(v, v, ACT.Silu, bias=col("b_conv_ln", ct), scale=col("g_conv_ln", ct)))
            h_ = slice(hf * 512, (hf + 1) * 512)
            CN_done.append(split(v, (CN[0](ct)[:, h_], CN[1](ct)[:, h_]), [t, att1_last]))


    GA_done = []
    for mt in range(8):
        s, (w,) = ws.get()
        for hf in range(2):
            h_ = slice(hf * 512, (hf + 1) * 512)
            b = bank()
            for k in range(8):
                t = mm3(ps[:, b, :], at(w, slice(None), k), at(HT, slice(None), k, h_), k == 0, k == 7, k == 7)
            act.wait(t, att1_last)
            bfree[b] = act.do(lambda e: e.activation(GA[:, mt, h_], ps[:, b, :], ACT.Sigmoid))
            GA_done.append(bfree[b])
        ws.done(s, t)
        conv_steps(7)
        if mt == 3:
            ln_centre()
        if mt == 5:
            ln_scale()
        if mt == 6:
            ln_apply()

    sg = [reg(96 + 2 * j, 512) for j in range(2)]
    sg_free = [CN_done, CN_done]
    M_done = []
    for mt in range(8):
        s0, (wb_,) = ws.get()
        gbs = []
        for hf in range(2):
            h_ = slice(hf * 512, (hf + 1) * 512)
            b = bank()
            for k in range(8):
                t = mm3(ps[:, b, :], at(wb_, slice(None), k), at(HT, slice(None), k, h_), k == 0, k == 7, k == 7)
            act.wait(t, sg_free[hf])
            tb = act.do(lambda e: e.activation(sg[hf], ps[:, b, :], ACT.Sigmoid))
            bfree[b] = tb
            gbs.append(tb)
        ws.done(s0, t)
        s1, (wc_, wa_) = ws.get()
        for hf in range(2):
            h_ = slice(hf * 512, (hf + 1) * 512)
            b2, b3 = bank(), bank()
            pe.wait(*CN_done, *OS_done)
            for k in range(4):
                t2 = mm3(ps[:, b2, :], at(wc_, slice(None), k), (CN[0](k)[:, h_], CN[1](k)[:, h_]), k == 0, k == 3,
                         k == 3)
            for k in range(4):
                t3 = mm3(ps[:, b3, :], at(wa_, slice(None), k), (OTh[:, k, h_], OTl[:, k, h_]), k == 0, k == 3,
                         k == 3)
            ga = GA[:, mt, h_]
            dve.wait(t2, *GA_done)
            t4 = dve.do(lambda e: e.tensor_tensor(ga, ps[:, b2, :], ga, ALU.mult))
            bfree[b2] = t4
            dve.wait(gbs[hf], t3)
            t5 = dve.do(lambda e: e.tensor_tensor(sg[hf], ps[:, b3, :], sg[hf], ALU.mult))
            bfree[b3] = t5
            dve.wait(t4, t5)
            t6 = dve.do(lambda e: e.tensor_tensor(ga, ga, sg[hf], ALU.add))
            sg_free[hf] = t6
            M_done.append(t6)
        ws.done(s1, t3)
    merge_last = pe_now()

    X = reg(105, 8, 1024)
    pool.wait(merge_last)
    X_in = [land(f"xr{i}").dma(pool, X[:, i, :], x_in[i * P:(i + 1) * P, :]) for i in range(8)]
    MS = pair(0, 32, 8, 1024)
    ws.lend(193, merge_last)
    ws.make(1)
    MS_done = [split(GA[:, k, :], at(MS, slice(None), k), [M_done[2 * k + 1]], merge_last) for k in range(8)]

    def residual(q, i, b, waits, square):
        qs = slice(q * 256, (q + 1) * 256)
        dve.wait(*waits)
        bfree[b] = dve.do(lambda e: e.tensor_tensor(X[:, i, qs], ps[:, b, 0:256], X[:, i, qs], ALU.add))
        if square:
            act.wait(bfree[b], jk_t[i % 2])
            jk_t[i % 2] = act.do(lambda e: e.activation(jk[i % 2], X[:, i, qs], ACT.Square,
                                                        accum_out=ss4[:, i, q:q + 1]))
            return jk_t[i % 2]

    jk, jk_t = [reg(165, 256), reg(166, 256)], [None, None]
    X_t = {}
    for q in range(4):
        s0, (w0,) = ws.get()
        s1, (w1,) = ws.get()
        for i in range(NT):
            b = bank()
            for k in range(8):
                if q == 0 and i == 0:
                    pe.wait(MS_done[k])
                w = at(w0, slice(None), k) if k < 4 else at(w1, slice(None), k - 4)
                t = mm3(ps[:, b, 0:256], at(MS, slice(None), k, slice(i * P, (i + 1) * P)), w, k == 0, k == 7,
                        k == 7)
            if i == NT - 1:
                ws.done(s0, t)
                ws.done(s1, t)
            X_t[i] = residual(q, i, b, [t, X_in[i]], True)
            if i == NT - 1:
                ws.make(3)

    def norm_start(scratch, free):
        out_ = []
        for i0 in (0, 4):
            for i in range(i0, i0 + 4):
                dve.wait(X_t[i])
            t = dve.do(lambda e: e.tensor_reduce(ss[:, i0:i0 + 4], ss4[:, i0:i0 + 4, :], AX.X, ALU.add))
            t_inv = rms_inv(i0, i0 + 4, 1024.0, [t])
            dve.wait(free)
            out_.append(xhat(lambda i: X[:, i, :], scratch, i0, i0 + 4, t_inv))
        return out_

    H2 = pair(0, 32, 8, 1024)
    scr = lambda i: reg(64 + 4 * i, D)
    t_xh = norm_start(scr, None)
    H2_free = pe_now()
    H2_done = [turned(scr, H2, i0, i0 + 4, lambda f: col("g_ffn", f), None, None, t_xh[i0 // 4], H2_free)
               for i0 in (0, 4)]
    scr_last = pe_now()

    slots6 = [64, 72, 80, 88, 96, 137]
    ft = [[reg(145 + 2 * j, 512), None] for j in range(4)]
    nt_ = [0]
    arow = [reg(104, 256), reg(167, 256)]
    arow_free = [None, None]
    an = [0, None]
    mod_t = []

    def ada():
        n_ = an[0] // 2
        hf_ = an[0] % 2
        an[0] += 1
        j = n_ % 2
        s0, (w0,) = ws.get()
        if hf_ == 0:
            an[1] = bank()
        b = an[1]
        pe.wait(t_cv)
        for k in range(4 * hf_, 4 * hf_ + 4):
            w = at(w0, slice(None), k - 4 * hf_)
            mm(ps[0:4, b, 0:256], cv[:, k, 0:4], w[0], k == 0, False, False)
            t = mm(ps[0:2, b, 0:256], cv[:, k, 0:2], w[1], False, k == 7, k in (3, 7))
        ws.done(s0, t)
        if hf_ == 0:
            return
        dve.wait(t, arow_free[j])
        t = dve.do(lambda e: e.tensor_copy(arow[j][0:4, :], ps[0:4, b, 0:256]))
        bfree[b] = t
        pool.wait(t)
        arow_free[j] = land(f"mod{j}").dma(pool, mod_dram[:, n_ * 256:(n_ + 1) * 256], arow[j][0:4, :])
        mod_t[:] = (mod_t + [arow_free[j]])[-2:]

    mrow = [reg(137, P), reg(137.5, P), reg(138, P)]
    modT = m(48)
    mg, mgc, mg2 = m(8), m(8), m(8)
    shift = lambda c0, f: modT[:, c0 + f:c0 + f + 1]
    iC = [m(1), m(1)]
    xc = [reg(193 + 4 * j, D) for j in range(2)]
    cin = a["ctx_2"].rearrange("o s d -> (o s) d")
    XC = pair(137, 145, 8, CTX)
    late_ = {}

    def load_mod():
        pool.wait(*mod_t, pe_now())
        lm = land("mrow")
        for r, (hi, lo) in enumerate(((0, 2), (1, 3))):
            for part, row in ((mrow[0], hi), (mrow[1], lo)):
                for n_, (d0, c0) in enumerate(((0, 0), (16, 3))[:2 - r]):
                    src = mod_dram[row:row + 1, c0 * D:(c0 + 2) * D].rearrange("o (c p) -> (o c) p", p=P)
                    lm.dma(pool, part[32 * r + d0:32 * r + d0 + 16, :], src)
        for d0, c0 in ((0, 0), (16, 3), (32, 0)):
            lm_last = lm.dma(pool, mrow[2][d0:d0 + 16, :],
                       a["b_ada_2"][:, c0 * D:(c0 + 2) * D].rearrange("o (c p) -> (o c) p", p=P))
        late_["m"] = lm_last
        late_["x"] = [land(f"xc{j}").dma(pool, xc[j], cin[j * P:(j + 1) * P, :]) for j in range(2)]

    def mod_columns():
        t = late_["m"]
        dve.wait(t)
        t = dve.do(lambda e: e.tensor_tensor(mrow[0][0:48, :], mrow[0][0:48, :], mrow[1][0:48, :], ALU.add))
        dve.wait(t)
        t = dve.do(lambda e: e.tensor_tensor(mrow[0][0:48, :], mrow[0][0:48, :], mrow[2][0:48, :], ALU.add))
        pe.wait(t)
        b = bank()
        t = tr(ps[:, b, 0:48], mrow[0][0:48, :], ident[0:48, 0:48], True)
        dve.wait(t)
        t = dve.do(lambda e: e.tensor_copy(modT, ps[:, b, 0:48]))
        bfree[b] = t
        dve.wait(t)

        def gain(dst, name, c0):
            g0 = colsA[:, where[name]:where[name] + 8]
            return dve.do(lambda e: e.scalar_tensor_tensor(out=dst, in0=modT[:, c0:c0 + 8], scalar=1.0, in1=g0,
                                                           op0=ALU.add, op1=ALU.mult))

        gain(mg, "norm_pre_mix_2", 8)
        gain(mgc, "norm_pre_mix_2", 40)
        late_["mg"] = gain(mg2, "norm_pre_ffn_2", 24)
        t_scC = []
        t = None
        for j in range(2):
            act.wait(late_["x"][j], late_["mg"], t)
            t = act.do(lambda e: e.activation(reg(149, D), xc[j], ACT.Square, accum_out=iC[j]))
            dve.wait(t)
            t1 = dve.do(lambda e: e.tensor_scalar(iC[j], iC[j], 1.0 / D, EPS, ALU.mult, ALU.add))
            pool.wait(t1)
            t1 = pool.do(lambda e: e.tensor_tensor(iC[j], iC[j], nhalf[:, 0:1], ALU.pow))
            dve.wait(t1)
            t_scC.append(dve.do(lambda e: e.tensor_scalar(xc[j], xc[j], iC[j], None, ALU.mult)))
        late_["s"] = t_scC

    def turn_context():
        tmps = [[reg(104, 256), arow_free], [reg(168, 256), None]]
        late_["XC"] = turned(lambda i: xc[i], XC, 0, 2, lambda f: mgc[:, f:f + 1], lambda f: shift(32, f), tmps,
                             late_["s"], late_["s"], late_["mg"])

    for gi, fs in enumerate(groups):
        A = [pair(slots6[j], slots6[j] + 4, 1024) for j in range(len(fs))]
        a_free = pe_now()
        A_done = []
        if gi == len(groups) - 1:
            ws.retire(3)
        for fi, f in enumerate(fs):
            s0, (wg,) = ws.get()
            vs = []
            for hf in range(2):
                pe.wait(H2_done[hf])
                h_ = slice(hf * 512, (hf + 1) * 512)
                v = ft[nt_[0] % 4]
                nt_[0] += 1
                b = bank()
                for k in range(8):
                    t = mm3(ps[:, b, :], at(wg, slice(None), k), at(H2, slice(None), k, h_), k == 0, k == 7, k == 7)
                act.wait(t, v[1])
                t1 = act.do(lambda e: e.activation(v[0], ps[:, b, :], ACT.Silu))
                bfree[b] = t1
                vs.append((v, t1, h_))
            ws.done(s0, t)
            ada()
            s1, (wu,) = ws.get()
            for v, t1, h_ in vs:
                b = bank()
                for k in range(8):
                    t = mm3(ps[:, b, :], at(wu, slice(None), k), at(H2, slice(None), k, h_), k == 0, k == 7, k == 7)
                dve.wait(t1, t)
                t2 = dve.do(lambda e: e.tensor_tensor(v[0], ps[:, b, :], v[0], ALU.mult))
                bfree[b] = t2
                v[1] = split(v[0], (A[fi][0][:, h_], A[fi][1][:, h_]), [t2], a_free)
                A_done.append(v[1])
            ws.done(s1, t)
            ada()
            if f in (20, 21):
                ada()
                ada()
        last = gi == len(groups) - 1
        nf = len(fs)
        if last:
            load_mod()
        for q in range(4):
            s0, (w0,) = ws.get()
            s1, (w1,) = ws.get()
            pe.wait(*A_done)
            for i in range(NT):
                b = bank()
                for f in range(nf):
                    w = at(w0, slice(None), f) if f < 3 else at(w1, slice(None), f - 3)
                    t = mm3(ps[:, b, 0:256], (A[f][0][:, i * P:(i + 1) * P], A[f][1][:, i * P:(i + 1) * P]), w,
                            f == 0, f == nf - 1, f == nf - 1)
                if i == NT - 1:
                    ws.done(s0, t)
                    ws.done(s1, t)
                X_t[i] = residual(q, i, b, [t, X_t[i] if gi == 0 and q == 0 else None], last)
                if i == NT - 1:
                    ws.make(3)
            if last and q == 1:
                mod_columns()
            if last and q == 2:
                turn_context()
    ffn_last = pe_now()
    t_mg, XC_done = late_["mg"], late_["XC"]


    scr3 = lambda i: reg(64 + 4 * i, D)
    t_xh = norm_start(scr3, ffn_last)
    K2c = reg(193, 4, CTX)
    V2c = reg(197, 2, 512)
    kc_done = []
    for mt in range(4):
        s, (w,) = ws.get()
        pe.wait(*XC_done)
        b = bank()
        for k in range(8):
            t = mm3(ps[:, b, 0:CTX], at(w, slice(None), k), at(XC, slice(None), k), k == 0, k == 7, k == 7)
        ws.done(s, t)
        act.wait(t, *XC_done)
        bfree[b] = act.do(lambda e: e.copy(K2c[:, mt, :], ps[:, b, 0:CTX]))
        kc_done.append(bfree[b])
    for q in range(2):
        s0, (w0,) = ws.get()
        s1, (w1,) = ws.get()
        for i in range(2):
            b = bank()
            for k in range(8):
                w = at(w0, slice(None), k) if k < 4 else at(w1, slice(None), k - 4)
                t = mm3(ps[:, b, 0:256], at(XC, slice(None), k, slice(i * P, (i + 1) * P)), w, k == 0, k == 7, k == 7)
            act.wait(t)
            bfree[b] = act.do(lambda e: e.copy(V2c[:, i, q * 256:(q + 1) * 256], ps[:, b, 0:256]))
            kc_done.append(bfree[b])
        ws.done(s0, t)
        ws.done(s1, t)
    xc_last = pe_now()

    XN = pair(0, 32, 8, 1024)
    tmps = [[reg(96 + 2 * j, 512), xc_last] for j in range(4)]
    XN_done = [turned(scr3, XN, i0, i0 + 4, lambda f: mg[:, f:f + 1], lambda f: shift(0, f), tmps, t_xh[i0 // 4],
                      ffn_last, t_mg) for i0 in (0, 4)]
    scr3_last = pe_now()
    lx3 = land("x3out")
    pool.wait(*[X_t[i] for i in range(8)], t_xh)
    for i in range(8):
        t_x3 = lx3.dma(pool, x3_dram[i * P:(i + 1) * P, :], X[:, i, :])

    Q2 = reg(64, 4, 1024)
    K2 = reg(105, 4, 1024)
    V2 = reg(121, 8, 512)
    COS = reg(137, 1024)
    SIN = reg(141, 1024)
    QR = [reg(96 + 2 * j, 512) for j in range(4)]
    rot = m(P)
    pool.wait(xc_last)
    cl = land("cs")
    cl.dma(pool, COS, a["cos"])
    cl.dma(pool, rot, a["rot"])
    t_cs = cl.dma(pool, SIN, a["sin"])
    qr_free = [XN_done[1][-1]] * 4
    n = 0
    QK2_done = []
    pend = []

    def rope(j, t1, d, h_):
        pe.wait(t1, t_cs)
        b = bank()
        t = mm(ps[:, b, :], rot, QR[j], True, True, True)
        dve.wait(t, t_cs, t_x3)
        t2 = dve.do(lambda e: e.tensor_tensor(d, ps[:, b, :], SIN[:, h_], ALU.mult))
        bfree[b] = t2
        t3 = dve.do(lambda e: e.tensor_tensor(QR[j], QR[j], COS[:, h_], ALU.mult))
        dve.wait(t2, t3)
        t4 = dve.do(lambda e: e.tensor_tensor(d, d, QR[j], ALU.add))
        qr_free[j] = t4
        QK2_done.append(t4)

    for dst in (Q2, K2):
        for mt in range(4):
            s, (w,) = ws.get()
            for hf in range(2):
                h_ = slice(hf * 512, (hf + 1) * 512)
                j = n % 4
                n += 1
                pe.wait(XN_done[hf])
                b = bank()
                for k in range(8):
                    t = mm3(ps[:, b, :], at(w, slice(None), k), at(XN, slice(None), k, h_), k == 0, k == 7, k == 7)
                act.wait(t, qr_free[j])
                sc_ = 0.125 if dst is Q2 else 1.0
                t1 = act.do(lambda e: e.activation(QR[j], ps[:, b, :], ACT.Copy, scale=sc_))
                bfree[b] = t1
                if pend:
                    rope(*pend.pop())
                pend.append((j, t1, dst[:, mt, h_], h_))
            ws.done(s, t)
    V2_done = []
    for q in range(2):
        s0, (w0,) = ws.get()
        s1, (w1,) = ws.get()
        for i in range(8):
            b = bank()
            for k in range(8):
                w = at(w0, slice(None), k) if k < 4 else at(w1, slice(None), k - 4)
                t = mm3(ps[:, b, 0:256], at(XN, slice(None), k, slice(i * P, (i + 1) * P)), w, k == 0, k == 7, k == 7)
            if pend:
                rope(*pend.pop())
            act.wait(t, t_x3)
            bfree[b] = act.do(lambda e: e.copy(V2[:, i, q * 256:(q + 1) * 256], ps[:, b, 0:256]))
            V2_done.append(bfree[b])
        ws.done(s0, t)
        ws.done(s1, t)

    stacks = [dict(Q=[regR(o, 1024), regR(o + 4, 1024)], K=[regR(o + 8, 1280), regR(o + 13, 1280)],
                   L=regR(o + 18, 1280)) for o in (80, 137)]
    lo_half, hi_half = slice(0, 64), slice(64, 128)

    def build(h, free, maps=(0, 1)):
        sk = stacks[h % 2]
        out_ = []
        for mp in maps:
            own, other = ((lo_half, hi_half), (hi_half, lo_half))[mp]
            q_, qs, ks, kl = Q2[own, h, :], sk["Q"][mp], sk["K"][mp], sk["L"]
            act.wait(free, QK2_done, kc_done)
            t1 = act.do(lambda e: e.activation(qs[own, :], q_, ACT.Copy))
            dve.wait(t1)
            out_.append(dve.do(lambda e: e.tensor_tensor(qs[other, :], q_, qs[own, :].bitcast(F32), ALU.subtract)))
            for k_, c in ((K2[own, h, :], slice(0, 1024)), (K2c[own, h, :], slice(1024, 1280))):
                t1 = act.do(lambda e: e.activation(ks[own, c], k_, ACT.Copy))
                dve.wait(t1)
                out_.append(dve.do(lambda e: e.tensor_tensor(kl[own, c], k_, ks[own, c].bitcast(F32),
                                                             ALU.subtract)))
                out_.append(act.do(lambda e: e.activation(ks[other, c], k_, ACT.Copy)))
        return out_

    SK_done = {0: build(0, None)}

    CV = lambda ct: reg(137 + 4 * ct, 1024)
    u = reg(165, 1024)
    u_free = [QK2_done]
    CV_done = []
    for ct in range(4):
        o = CV(ct)
        ps_ = []
        t4s, t5s = [], []
        for n_ in range(3):
            s, (w,) = ws.get()
            for hf in range(2):
                pe.wait(XN_done[hf])
                h_ = slice(hf * 512, (hf + 1) * 512)
                b = bank()
                for k in range(8):
                    t = mm3(ps[:, b, :], at(w, slice(None), k), at(XN, slice(None), k, h_), k == 0, k == 7, k == 7)
                if n_ == 0:
                    act.wait(t, u_free[0])
                    bfree[b] = act.do(lambda e: e.copy(u[:, h_], ps[:, b, :]))
                    t4s.append(bfree[b])
                elif n_ == 1:
                    dve.wait(t, t4s[hf])
                    bfree[b] = dve.do(lambda e: e.tensor_tensor(u[:, h_], ps[:, b, :], u[:, h_], ALU.mult))
                    t5s.append(bfree[b])
                else:
                    ps_.append((b, t, h_))
            ws.done(s, t)
            if n_ == 1:
                wcol = lambda w_: col("conv_w", w_ * 4 + ct)
                dve.wait(*t5s, scr3_last)
                t = dve.do(lambda e: e.tensor_scalar(o, u, wcol(1), None, ALU.mult))
                dve.wait(t)
                t = dve.do(lambda e: e.scalar_tensor_tensor(out=o[:, 1:], in0=u[:, 0:S - 1], scalar=wcol(0),
                                                            in1=o[:, 1:], op0=ALU.mult, op1=ALU.add))
                dve.wait(t)
                tc = dve.do(lambda e: e.scalar_tensor_tensor(out=o[:, 0:S - 1], in0=u[:, 1:], scalar=wcol(2),
                                                             in1=o[:, 0:S - 1], op0=ALU.mult, op1=ALU.add))
                u_free[0] = tc
        for b, t, h_ in ps_:
            dve.wait(t, tc)
            bfree[b] = dve.do(lambda e: e.tensor_tensor(o[:, h_], ps[:, b, :], o[:, h_], ALU.mult))
            CV_done.append(bfree[b])

    xn_last = pe_now()
    assert ws.used == len(ws.specs)
    w_idle = ws.ready[len(ws.specs) - 1]

    MX = pair(0, 32, 8, 1024)
    PA = [[reg(160 + 10 * j, 1280), reg(165 + 10 * j, 1280)] for j in range(3)]
    PTa = [reg(64, 8, P), reg(105, 8, P)]
    PTb = [reg(103, 2, P), reg(104, 2, P)]
    OM2 = [reg(190 + 0.5 * j, P) for j in range(2)]
    SQ2 = reg(191, P)
    lams = reg(103, 256)
    lt = reg(104, 128)
    lamc = m(8)
    pairs = lambda n: [[m(1), m(1)] for _ in range(n)]
    m8, s8, r8 = pairs(3), pairs(3), pairs(3)
    sub_ss = [m(1), m(1)]
    subg = m(2)
    pool.wait(QK2_done)
    gsl = land("subg")
    gsl.dma(pool, subg[:, 0:1], a["subln_g_2"].rearrange("o d -> d o"))
    for i, nm in enumerate(("lambda_q1_2", "lambda_k1_2", "lambda_q2_2", "lambda_k2_2")):
        t_sg = gsl.dma(pool, lams[:, i * 64:(i + 1) * 64], a[nm].to_broadcast([P, 64]))
    dve.wait(t_sg)
    t_sg = dve.do(lambda e: e.tensor_scalar(subg[:, 1:2], subg[:, 0:1], 0.8, None, ALU.mult))
    t1 = dve.do(lambda e: e.tensor_tensor(lt[:, 0:64], lams[:, 0:64], lams[:, 64:128], ALU.mult))
    t2 = dve.do(lambda e: e.tensor_tensor(lt[:, 64:128], lams[:, 128:192], lams[:, 192:256], ALU.mult))
    dve.wait(t1, t2)
    t1 = dve.do(lambda e: e.tensor_reduce(lamc[:, 0:2], lt.rearrange("p (a b) -> p a b", a=2), AX.X, ALU.add))
    act.wait(t1)
    t1 = act.do(lambda e: e.activation(lamc[:, 2:4], lamc[:, 0:2], ACT.Exp))
    dve.wait(t1)
    t1 = dve.do(lambda e: e.tensor_tensor(lamc[:, 4:5], lamc[:, 3:4], lamc[:, 2:3], ALU.subtract))
    dve.wait(t1)
    t_lam = dve.do(lambda e: e.tensor_scalar(lamc[:, 5:6], lamc[:, 4:5], -0.2, None, ALU.add))
    nlam = lamc[:, 5:6]
    MXc_done = []
    Xt = lambda i: reg(80 + 4 * i, D) if i < 4 else reg(137 + 4 * (i - 4), D)
    G1, G2 = reg(96, D), reg(121, D)
    X3_in = []

    def x3_back(i0, i1, free):
        pool.wait(free)
        for i in range(i0, i1):
            X3_in.append(land(f"xr{i}").dma(pool, Xt(i), x3_dram[i * P:(i + 1) * P, :]))

    def mod_row(dst, chunk, norm, tmp, free, name):
        pool.wait(*free)
        lg = land(name)
        cs = slice(chunk * D, (chunk + 1) * D)
        lg.dma(pool, dst, mod_dram[0:1, cs].to_broadcast([P, D]))
        lg.dma(pool, tmp[0], mod_dram[2:3, cs].to_broadcast([P, D]))
        lg.dma(pool, tmp[1], a["b_ada_2"][:, cs].to_broadcast([P, D]))
        t = lg.dma(pool, tmp[2], a[norm].to_broadcast([P, D]))

        def combined():
            dve.wait(t)
            t1 = dve.do(lambda e: e.tensor_tensor(dst, dst, tmp[0], ALU.add))
            dve.wait(t1)
            t1 = dve.do(lambda e: e.tensor_tensor(dst, dst, tmp[1], ALU.add))
            dve.wait(t1)
            return dve.do(lambda e: e.tensor_tensor(dst, dst, tmp[2], ALU.mult))

        return combined

    units = [(h, i) for h in range(4) for i in range(NT)]
    st = {}
    p_free, pt2_free, om2_free = [None] * 3, [None] * 2, [None] * 2
    sq_free = [None]

    def scores(u, mp):
        h, i = units[u]
        j = u % 3
        sk = stacks[h % 2]
        b0 = 3 * mp
        pe.wait(bfree[b0], bfree[b0 + 1], bfree[b0 + 2], SK_done[h])
        r = slice(mp * 64, mp * 64 + 64)
        q_ = sk["Q"][mp][:, i * P:(i + 1) * P]
        for c in range(3):
            cs = slice(c * 512, min(c * 512 + 512, 1280))
            o = ps[:, b0 + c, 0:cs.stop - cs.start]
            mm(o, q_, sk["K"][mp][:, cs], True, False, False)
            t = mm(o, q_[r, :], sk["L"][r, cs], False, True, c == 2)
        sv = ps[:, b0:b0 + 3, :].rearrange("p a b -> p (a b)")[:, 0:1280]
        dve.wait(t)
        st[("x", u, mp)] = (sv, dve.do(lambda e: e.tensor_reduce(m8[u % 3][mp], sv, AX.X, ALU.max, negate=True)))

    def expo(u, mp):
        j, b0 = u % 3, 3 * mp
        sv, t1 = st[("x", u, mp)]
        act.wait(t1, p_free[j], w_idle)
        t2 = act.do(lambda e: e.activation(PA[j][mp], sv, ACT.Exp, bias=m8[j][mp], accum_out=s8[j][mp]))
        bfree[b0] = bfree[b0 + 1] = bfree[b0 + 2] = t2
        st[("e", u, mp)] = t2

    def combine(u):
        j = u % 3
        r_, s_ = r8[j], s8[j]
        dve.wait(st[("e", u, 0)], st[("e", u, 1)], t_lam)
        t1 = dve.do(lambda e: e.reciprocal(r_[1], s_[1]))
        st[("r", u)] = dve.do(lambda e: e.reciprocal(r_[0], s_[0]))
        dve.wait(t1)
        t1 = dve.do(lambda e: e.tensor_scalar(r_[1], r_[1], s_[0], nlam, ALU.mult, ALU.mult))
        dve.wait(t1)
        st[u] = dve.do(lambda e: e.scalar_tensor_tensor(out=PA[j][0], in0=PA[j][1], scalar=r_[1],
                                                        in1=PA[j][0], op0=ALU.mult, op1=ALU.add))

    tb67 = [0]

    def bank67():
        b = 6 + tb67[0] % 2
        tb67[0] += 1
        pe.wait(bfree[b])
        return b

    def turn_p2(u, groups_):
        j = u % 2
        pe.wait(st[u])
        for c0 in groups_:
            n = min(4, 10 - c0)
            b = bank67()
            for c in range(n):
                t = tr(ps[:, b, c * P:(c + 1) * P], PA[u % 3][0][:, (c0 + c) * P:(c0 + c + 1) * P], ident, c == n - 1)
            o = PTa[j][:, c0:c0 + n, :] if c0 < 8 else PTb[j]
            o, i_ = o.rearrange("p a b -> p (a b)"), ps[:, b, 0:n * P]
            act.wait(t, pt2_free[j], SK_done[0])
            bfree[b] = act.do(lambda e: e.copy(o, i_))
            st[("t", u, c0)] = bfree[b]
        p_free[u % 3] = t

    def pv2(u):
        h, i = units[u]
        j = u % 2
        b = bank67()
        for c in range(10):
            pe.wait(st[("t", u, c // 4 * 4)])
            v_ = V2[:, c, h * P:(h + 1) * P] if c < 8 else V2c[:, c - 8, h * P:(h + 1) * P]
            w_ = PTa[j][:, c, :] if c < 8 else PTb[j][:, c - 8, :]
            t = mm(ps[:, b, 0:P], w_, v_, c == 0, c == 9, c == 9)
        pt2_free[j] = t
        act.wait(t, st[("r", u)], om2_free[j])
        bfree[b] = act.do(lambda e: e.activation(OM2[j], ps[:, b, 0:P], ACT.Copy, scale=r8[u % 3][0]))
        act.wait(bfree[b], sq_free[0])
        t1 = act.do(lambda e: e.activation(SQ2, OM2[j], ACT.Square, accum_out=sub_ss[j]))
        sq_free[0] = t1
        pool.wait(t1)
        t1 = pool.do(lambda e: e.tensor_scalar(sub_ss[j], sub_ss[j], 1.0 / P, EPS, ALU.mult, ALU.add))
        pool.wait(t1)
        t1 = pool.do(lambda e: e.tensor_tensor(sub_ss[j], sub_ss[j], nhalf[:, 0:1], ALU.pow))
        pool.wait(t1)
        st[("m", u)] = pool.do(lambda e: e.tensor_scalar(OM2[j], OM2[j], sub_ss[j], None, ALU.mult))

    MXa_done = []

    def fin2(u):
        h, i = units[u]
        j = u % 2
        b = bank67()
        pe.wait(st[("m", u)])
        t = tr(ps[:, b, 0:P], OM2[j], ident, True)
        om2_free[j] = t
        bfree[b] = split_psum(ps[:, b, 0:P], at(MX, slice(None), h, slice(i * P, (i + 1) * P)), subg[:, 1:2],
                              [t, t_sg])
        MXa_done.append(bfree[b])

    wo2 = a["w_out_2"][0].rearrange("(c p) n -> p c n", p=P)
    wo = Stream([68, 72, 76, 109, 113], [121, 129, 153, 161, 169, 177, 185, 193], 1024, "o", None)
    wo.add(*[[(1, 1024, wo2[:, k:k + 1, :])] for k in range(8)])
    gtmp = [reg(72, D), reg(76, D), reg(113, D)]

    pe.wait(*QK2_done, *V2_done, *kc_done, *[x for x in bfree if x])
    nu = len(units)
    for u in range(nu + 3):
        if u < nu:
            scores(u, 0)
        if 2 <= u <= nu + 1:
            turn_p2(u - 2, (0, 4, 8))
        if 1 <= u <= nu:
            combine(u - 1)
        if u < nu:
            expo(u, 0)
            scores(u, 1)
        if u >= 3:
            fin2(u - 3)
        if u < nu:
            expo(u, 1)
        if 2 <= u <= nu + 1:
            pv2(u - 2)
        if u < 4:
            MXc_done.append(split(CV(u), at(MX, slice(None), 4 + u), [*CV_done], xn_last))
        if u in (4, NT + 1, 2 * NT + 1):
            h = u // NT + 1
            sk_free = [pe_now(), *MXc_done]
            SK_done[h] = build(h, sk_free, (0,))
        if u in (5, NT + 2, 2 * NT + 2):
            SK_done[h] = SK_done[h] + build(h, sk_free, (1,))
        if u == 3 * NT + 1:
            b0_free = pe_now()
            x3_back(0, 4, b0_free)
            g1_rest = mod_row(G1, 2, "norm_post_mix_2", gtmp, [b0_free, SK_done[3]], "g1")
        if u == 3 * NT + 5:
            t_G1 = g1_rest()
            wo.raw_free = [t_G1] * 5
            wo.load()
    att2_last = pe_now()
    x3_back(4, 8, att2_last)
    wr, anti = reg(104, 8, NE), reg(104.5, P)
    t_wr = land("wr").dma(pool, wr, a["w_router_2"][0].rearrange("(c p) n -> p c n", p=P))
    t = pool.do(lambda e: e.memset(anti, 0.0))
    pool.wait(t)
    t_anti = pool.do(lambda e: e.affine_select(out=anti, in_=anti, compare_op=ALU.not_equal, fill=1.0,
                                               base=1 - P, pattern=[[1, P]], channel_multiplier=1))

    wo.part_free = [[att2_last, *MXa_done[-1:]]] * 8
    wo.make(8)
    wo_ready = [wo.ready[k] for k in range(8)]
    wv = [tuple(x.rearrange("p (c n) -> p c n", c=1) for x in wo.slot(k)) for k in range(8)]
    tmp = [reg(64, D), reg(105, D)]
    junk = [reg(100, D), reg(117, D)]
    scr4 = lambda i: reg((68, 72, 76, 109, 113, 121, 125, 129)[i], D)
    mst = [m(2), m(2)]
    tmp_free = [att2_last, att2_last]
    X4_t, X4h_t = [], []
    lst = land("xhd")

    def x4_norm(i):
        t_inv = rms_inv(i, i + 1, 1024.0, [X4_t[i]])
        dve.wait(t_inv, wo_ready, wo2_last if i > 4 else None)
        t = dve.do(lambda e: e.tensor_scalar(scr4(i), Xt(i), inv[:, i:i + 1], None, ALU.mult))
        pool.wait(t)
        X4h_t.append(t)
        lst.dma(pool, xh_dram[i * P:(i + 1) * P, :], scr4(i))

    wo2_last = None
    for i in range(NT):
        j = i % 2
        b0 = 2 * (i % 4)
        pe.wait(bfree[b0], bfree[b0 + 1], *MXa_done, *MXc_done)
        for q in range(2):
            for k in range(8):
                pe.wait(wo_ready[k])
                t = mm3(ps[:, b0 + q, :], at(MX, slice(None), k, slice(i * P, (i + 1) * P)),
                        at(wv[k], slice(None), 0, slice(q * 512, (q + 1) * 512)), k == 0, k == 7, k == 7)
        v = ps[:, b0:b0 + 2, :].rearrange("p a b -> p (a b)")
        act.wait(t, att2_last, X4_t[i - 2] if i > 1 else None)
        t1 = act.do(lambda e: e.activation(junk[j], v, ACT.Square, accum_out=mst[j][:, 0:1]))
        dve.wait(t1)
        t1 = dve.do(lambda e: e.tensor_scalar(mst[j][:, 0:1], mst[j][:, 0:1], 1.0 / D, EPS, ALU.mult, ALU.add))
        pool.wait(t1)
        t1 = pool.do(lambda e: e.tensor_tensor(mst[j][:, 1:2], mst[j][:, 0:1], nhalf[:, 0:1], ALU.pow))
        dve.wait(t1, t_G1, tmp_free[j])
        t2 = dve.do(lambda e: e.scalar_tensor_tensor(out=tmp[j], in0=v, scalar=mst[j][:, 1:2], in1=G1,
                                                     op0=ALU.mult, op1=ALU.mult))
        bfree[b0] = bfree[b0 + 1] = t2
        dve.wait(t2, X3_in[i])
        t3 = dve.do(lambda e: e.tensor_tensor(Xt(i), Xt(i), tmp[j], ALU.add))
        tmp_free[j] = t3
        act.wait(t3, t1)
        X4_t.append(act.do(lambda e: e.activation(junk[j], Xt(i), ACT.Square, accum_out=ss[:, i:i + 1])))
        if i == NT - 1:
            wo2_last = pe_now()
        for k in (i - 2,) if i < NT - 1 else range(i - 2, NT):
            if k >= 0:
                x4_norm(k)

    XM = reg(0, 8, 1024)
    XM_done = []
    t_xhd = (lst.sem, lst.count)
    for i0 in (0, 4):
        pe.wait(X4h_t[i0:i0 + 4])
        for f in range(8):
            b = bank()
            for i in range(4):
                t = tr(ps[:, b, i * P:(i + 1) * P], scr4(i0 + i)[:, f * P:(f + 1) * P], ident, i == 3)
            d = XM[:, f, i0 * P:(i0 + 4) * P]
            if f % 2:
                act.wait(t, wo2_last)
                bfree[b] = act.do(lambda e: e.activation(d, ps[:, b, :], ACT.Identity, bias=shift(16, f),
                                                         scale=mg2[:, f:f + 1]))
            else:
                dve.wait(t, wo2_last)
                bfree[b] = dve.do(lambda e: e.tensor_scalar(d, ps[:, b, :], mg2[:, f:f + 1], shift(16, f), ALU.mult,
                                                            ALU.add))
            XM_done.append(bfree[b])
    scr4_last = pe_now()

    es = Stream([153, 161, 169, 177, 185, 193, 129], [32, 48, 0, 16], 2048, "e", None)
    es.raw_free = [wo2_last] * 6 + [[scr4_last, t_xhd]]
    for e_ in range(NE):
        for nm in ("w_gate_2", "w_up_2", "w_down_2"):
            w = a[nm][0, e_].rearrange("(c p) n -> p c n", p=P)
            for q in range(2):
                for k in (0, 4):
                    es.add([(4, 512, w[:, k:k + 4, q * 512:(q + 1) * 512])])
    es.load()

    lgT = reg(64, 1024)
    affT, w1_ = reg(105, 512), reg(107, 512)
    lg = reg(74, 4, 2 * NE)
    mx8 = reg(74.5, 8)
    ix8 = reg(75, P).bitcast(U32)
    top = reg(75.5, P)
    ixf = reg(76, P)
    AB = reg(76.5, 64)
    mge, dif = reg(77, NE), reg(77.25, NE)
    gT = m(NE)
    iT = m(NE).bitcast(U32)
    H2E = 2 * NE
    for hf in range(2):
        pe.wait(XM_done[8 * hf:8 * hf + 8], t_wr)
        b = bank()
        for k in range(8):
            t = mm(ps[0:NE, b, :], wr[:, k, :], XM[:, k, hf * 512:(hf + 1) * 512], k == 0, k == 7, k == 7)
        router_mm = t
        act.wait(t, X4_t)
        bfree[b] = act.do(lambda e: e.copy(lgT[0:NE, hf * 512:(hf + 1) * 512], ps[0:NE, b, :]))
        if hf == 0:
            b_l = bank()
        pe.wait(bfree[b])
        for i in range(4):
            c0 = i * H2E + hf * NE
            t = tr(ps[:, b_l, c0:c0 + NE], lgT[0:NE, (hf * 4 + i) * P:(hf * 4 + i + 1) * P], ident[0:NE, 0:NE], i == 3)
    v = ps[:, b_l, 0:P].rearrange("p (a b) -> p a b", a=8)
    lg8 = lg.rearrange("p a (h e) -> p (a h) e", h=2)
    bc = lambda x: x.rearrange("p (a o) -> p a o", o=1).to_broadcast([P, 8, NE])
    dve.wait(t, scr4_last, t_xhd)
    t = dve.do(lambda e: e.tensor_reduce(mx8, v, AX.X, ALU.max))
    dve.wait(t)
    t = dve.do(lambda e: e.tensor_tensor(lg8, v, bc(mx8), ALU.subtract))
    bfree[b_l] = t
    act.wait(t)
    t = act.do(lambda e: e.activation(lg8, lg8, ACT.Exp))
    dve.wait(t)
    t = dve.do(lambda e: e.tensor_reduce(mx8, lg8, AX.X, ALU.add))
    dve.wait(t)
    t = dve.do(lambda e: e.reciprocal(mx8, mx8))
    dve.wait(t)
    t = dve.do(lambda e: e.tensor_tensor(lg8, lg8, bc(mx8), ALU.mult))
    pe.wait(t)
    b = bank()
    for i in range(4):
        t = tr(ps[0:H2E, b, i * P:(i + 1) * P], lg[:, i, :], ident, i == 3)
    dve.wait(t, X4_t)
    t = dve.do(lambda e: e.tensor_copy(affT[0:H2E, :], ps[0:H2E, b, :]))
    bfree[b] = t
    es.part_free = [wo2_last, wo2_last, router_mm, router_mm]
    es.make(3, pool)
    g2_rest = mod_row(G2, 5, "norm_post_ffn_2", [reg(o, D) for o in (109, 113, 117)], [scr4_last, t_xhd], "g2")
    dve.wait(t)
    src, dst = affT, w1_
    for r in range(CAP // 8):
        rs_ = slice(r * 8, r * 8 + 8)
        t = dve.do(lambda e: e.max(top[0:H2E, rs_], src[0:H2E, :]))
        dve.wait(t)
        dve.do(lambda e: e.max_index(ix8[0:H2E, rs_], top[0:H2E, rs_], src[0:H2E, :]))
        t = dve.do(lambda e: e.match_replace(dst[0:H2E, :], top[0:H2E, rs_], src[0:H2E, :], -1.0))
        dve.wait(t)
        src, dst = dst, src
    t = dve.do(lambda e: e.tensor_copy(ixf[0:H2E, :], ix8[0:H2E, :]))
    pe.wait(t)
    b = bank()
    tr(ps[:, b, 0:H2E], top[0:H2E, :], ident[0:H2E, 0:H2E], False)
    t = tr(ps[:, b, H2E:2 * H2E], ixf[0:H2E, :], ident[0:H2E, 0:H2E], True)
    dve.wait(t)
    t = dve.do(lambda e: e.tensor_copy(AB, ps[:, b, 0:2 * H2E]))
    bfree[b] = t
    pe.wait(t, t_anti)
    b = bank()
    t = mm(ps[:, b, 0:2 * H2E], anti, AB, True, True, True)
    A_, Ai = AB[:, 0:NE], AB[:, H2E:H2E + NE]
    B_, Bi = ps[:, b, NE:H2E], ps[:, b, H2E + NE:2 * H2E]
    dve.wait(t)
    t = dve.do(lambda e: e.tensor_tensor(mge, A_, B_, ALU.is_ge))
    t_gT = dve.do(lambda e: e.tensor_tensor(gT, A_, B_, ALU.max))
    t1 = dve.do(lambda e: e.tensor_tensor(dif, Ai, Bi, ALU.subtract))
    dve.wait(t1)
    t1 = dve.do(lambda e: e.tensor_scalar(dif, dif, -512.0, None, ALU.add))
    dve.wait(t, t1)
    t = dve.do(lambda e: e.tensor_tensor(dif, dif, mge, ALU.mult))
    dve.wait(t)
    t = dve.do(lambda e: e.tensor_tensor(dif, dif, Bi, ALU.add))
    bfree[b] = t
    dve.wait(t)
    t_iT = dve.do(lambda e: e.tensor_scalar(iT, dif, 512.0, None, ALU.add))
    route_last = pe_now()

    XS = [reg(96 + 4 * j, D) for j in range(2)]
    XST = pair(64, 68, 8, P)
    HIT = pair(72, 76, 8, P)
    HID = [reg(105 + 4 * j, D) for j in range(2)]
    YS = [reg(113 + 4 * j, D) for j in range(2)]
    vt = [[reg(125 + 2 * j, 512), None] for j in range(2)]
    xs_t, xs_free, hid_t, down_t = {}, [None, None], {}, {}
    ys_t = [None] * 3
    sc_last = [None]
    scl_ = land("scat")

    def gather(e_):
        j = e_ % 2
        pool.wait(t_iT, t_xhd, xs_free[j], wo2_last)
        lg_ = land(f"xs{j}")
        lg_.count += 16
        pool.engine.indirect_dma_start(
            XS[j], None, xh_dram, bass.IndirectOffsetOnAxis(ap=iT[:, e_:e_ + 1], axis=0),
            bounds_check=S - 1).then_inc(lg_.sem, 16)
        xs_t[e_] = (lg_.sem, lg_.count)

    xst_t = {}

    def expert_x(e_, halves):
        j = e_ % 2
        pe.wait(xs_t[e_])
        tt_ = xst_t.setdefault(e_, [])
        for g_ in halves:
            b = bank()
            for f in range(4):
                t = tr(ps[:, b, f * P:(f + 1) * P], XS[j][:, (g_ * 4 + f) * P:(g_ * 4 + f + 1) * P], ident, f == 3)
            v = vt[g_]
            vv = v[0].rearrange("p (f n) -> p f n", f=4)
            act.wait(t, v[1], t_gT)
            for f in range(4):
                ff_ = g_ * 4 + f
                t2 = act.do(lambda e: e.activation(vv[:, f, :], ps[:, b, f * P:(f + 1) * P], ACT.Identity,
                                                   bias=shift(16, ff_), scale=mg2[:, ff_:ff_ + 1]))
            bfree[b] = t2
            v[1] = split(vv, at(XST, slice(None), slice(g_ * 4, g_ * 4 + 4)), [t2],
                         [hid_t.get(e_ - 1), route_last])
            tt_.append(v[1])
        xs_free[j] = t

    def hidden_turned(e_, g_, ready):
        j = e_ % 2
        pe.wait(ready)
        b = bank()
        for f in range(4):
            t = tr(ps[:, b, f * P:(f + 1) * P], HID[j][:, (g_ * 4 + f) * P:(g_ * 4 + f + 1) * P], ident, f == 3)
        bfree[b] = split_psum(ps[:, b, :], tuple(x.rearrange("p a b -> p (a b)") for x in
                                                 at(HIT, slice(None), slice(g_ * 4, g_ * 4 + 4))), None, [t],
                              [route_last, down_t.get(e_ - 1)])
        return bfree[b]

    gather(0)
    gather(1)
    expert_x(0, (0, 1))
    t_G2 = g2_rest()
    ys_t = [t_G2] * 2
    for e_ in range(NE):
        j = e_ % 2
        pe.wait(*xst_t[e_])
        bs = []
        for n_ in range(4):
            b = bank()
            for k0 in (0, 4):
                s, (w,) = es.get()
                for k in range(4):
                    t = mm3(ps[:, b, :], at(XST, slice(None), k0 + k), at(w, slice(None), k), k0 + k == 0,
                            k0 + k == 7, k == 3)
                es.done(s, t)
                if n_ == 3 and k0 == 0:
                    td = [hidden_turned(e_, 0, bs[2])]
            bs.append((b, t))
            if n_ < 2:
                h_ = HID[j][:, n_ * 512:(n_ + 1) * 512]
                act.wait(t, route_last, t_G2)
                t1 = act.do(lambda e: e.activation(h_, ps[:, b, :], ACT.Silu))
                bfree[b] = t1
                bs[n_] = t1
            else:
                h_ = HID[j][:, (n_ - 2) * 512:(n_ - 1) * 512]
                dve.wait(bs[n_ - 2], t)
                t2 = dve.do(lambda e: e.tensor_tensor(h_, ps[:, b, :], h_, ALU.mult))
                bfree[b] = t2
                bs[n_] = t2
        hid_t[e_] = t
        td.append(hidden_turned(e_, 1, bs[3]))
        jy = e_ % 2
        ty = []
        for q in range(2):
            b = bank()
            for k0 in (0, 4):
                s, (w,) = es.get()
                pe.wait(td[k0 // 4])
                for k in range(4):
                    t = mm3(ps[:, b, :], at(HIT, slice(None), k0 + k), at(w, slice(None), k), k0 + k == 0,
                            k0 + k == 7, k == 3)
                es.done(s, t)
                if q == 0 and e_ + 1 < NE:
                    expert_x(e_ + 1, (k0 // 4,))
            o = YS[jy][:, q * 512:(q + 1) * 512]
            act.wait(t, ys_t[jy], t_gT, route_last)
            bfree[b] = act.do(lambda e: e.activation(o, ps[:, b, :], ACT.Copy, scale=gT[:, e_:e_ + 1]))
            ty.append(bfree[b])
        down_t[e_] = t
        if e_ + 2 < NE:
            gather(e_ + 2)
        pool.wait(*ty, t_ffz, sc_last[0])
        scl_.count += 16
        pool.engine.indirect_dma_start(
            ff_dram, bass.IndirectOffsetOnAxis(ap=iT[:, e_:e_ + 1], axis=0), YS[jy], None,
            bounds_check=S - 1, compute_op=ALU.add).then_inc(scl_.sem, 16)
        sc_last[0] = ys_t[jy] = (scl_.sem, scl_.count)

    out2 = out.rearrange("o s d -> (o s) d")
    pe_last = pe_now()
    lo = land("out")
    f_ = [reg(4 * i, D) for i in range(NT)]
    sp.wait(sc_last[0], pe_last)
    tf = [land(f"f{i}").dma(sp, f_[i], ff_dram[i * P:(i + 1) * P, :]) for i in range(NT)]
    sq_t = []
    for i in range(NT):
        act.wait(tf[i], pe_last, sq_t[i - 2] if i > 1 else None)
        sq_t.append(act.do(lambda e: e.activation(reg(32 + 4 * (i % 2), D), f_[i], ACT.Square,
                                                  accum_out=ss[:, i:i + 1])))
    t_invs = [rms_inv(0, 1, 1024.0, [sq_t[0]])]
    for i in range(NT):
        if i + 1 < NT:
            t_invs.append(rms_inv(i + 1, i + 2, 1024.0, [sq_t[i + 1]]))
        dve.wait(t_invs[i], t_G2)
        t2 = dve.do(lambda e: e.scalar_tensor_tensor(out=f_[i], in0=f_[i], scalar=inv[:, i:i + 1], in1=G2,
                                                     op0=ALU.mult, op1=ALU.mult))
        adder = pool if i in (2, 5) else dve
        adder.wait(t2)
        t3 = adder.do(lambda e: e.tensor_tensor(f_[i], f_[i], Xt(i), ALU.add))
        sp.wait(t3)
        t_out = lo.dma(sp, out2[i * P:(i + 1) * P, :], f_[i])
    sp.wait(t_out)


_INS = ["x", "g_mix", "w_in", "b_forget", "w_dw", "b_dw", "g_conv_ln", "b_conv_ln", "w_conv_out", "g_q", "g_k",
        "w_attn_out", "w_out", "g_ffn", "w_ffn_in", "w_ffn_out", "c_2", "ctx_2", "c_ctx_2", "w_ada_2", "b_ada_2",
        "norm_pre_mix_2", "norm_post_mix_2", "norm_pre_ffn_2", "norm_post_ffn_2", "w_in_2", "conv_w_2",
        "lambda_q1_2", "lambda_k1_2", "lambda_q2_2", "lambda_k2_2", "subln_g_2", "w_out_2", "w_router_2",
        "w_gate_2", "w_up_2", "w_down_2"]


def _tables():
    f = np.float32
    row = np.repeat(np.arange(16, dtype=f), 64)
    colv = np.tile(np.arange(64, dtype=f), 16)
    iv = (f(10000.0) ** (-np.arange(0, 32, 2, dtype=f) / f(32))).astype(f)
    ar, ac = row[:, None] * iv[None, :], colv[:, None] * iv[None, :]
    ang = np.concatenate([ar, ar, ac, ac], axis=-1)
    cos, sin = np.cos(ang).astype(f), np.sin(ang).astype(f)
    rot = np.zeros((128, 128), f)
    for b in range(0, 128, 32):
        for i in range(16):
            rot[b + 16 + i, b + i] = -1.0
            rot[b + i, b + 16 + i] = 1.0
    two = lambda t: np.ascontiguousarray(np.concatenate([t.T, t.T], axis=0))
    return {"cos": two(cos), "sin": two(sin), "rot": rot}


def kernel(**inputs):
    import concourse.bacc as _bacc
    from concourse.bass_utils import run_bass_kernel_spmd as _run

    nc = _bacc.Bacc("TRN2", target_bir_lowering=False, num_devices=1)
    arrays, args = {}, {}
    every = {n: inputs[n] for n in _INS}
    every.update(_tables())
    for name, v in every.items():
        v = np.ascontiguousarray(v)
        arrays[f"in_{name}_dram"] = v
        args[name] = nc.dram_tensor(f"in_{name}_dram", v.shape, mybir.dt.from_np(v.dtype), kind="ExternalInput").ap()
    o = nc.dram_tensor("out_0_dram", (1, S, D), F32, kind="ExternalOutput").ap()
    program(nc, args, o)
    r = _run(nc, [arrays], core_ids=[0])
    return r.results[0]["out_0_dram"]
```
